# Optimizing a Trainium2 kernel written in Bass

```python
import math
import jax
import jax.numpy as jnp
from jax import lax
import numpy as np
import jax, jax.numpy as jnp

D_MODEL = 1024
BATCH = 1
SEQ = 256
DEPTH = 1

PLE_DIM = 256
GMLP_WIDTH = 1024
GMLP_GROUPS = 8
GMLP_CHUNK = 128
MOBA_HEADS = 8
MOBA_HEAD_DIM = 128
MOBA_WIDTH = MOBA_HEADS * MOBA_HEAD_DIM
MOBA_BLOCK = 256
MOBA_TOPK = 3
MOBA_QCHUNK = 32
REL_BUCKETS = 32
REL_MAX_DISTANCE = 1024
PEER_HEADS = 8
PEER_N_KEYS = 128
PEER_N_EXPERTS = PEER_N_KEYS * PEER_N_KEYS
PEER_TOPK = 16
PEER_KEY_DIM = 256
PEER_KEY_HALF = PEER_KEY_DIM // 2
PEER_TOK_CHUNK = 128
IN_WIDTHS = (GMLP_WIDTH, GMLP_WIDTH, MOBA_WIDTH, MOBA_WIDTH, MOBA_WIDTH, D_MODEL, D_MODEL)
IN_TOTAL = sum(IN_WIDTHS)
LN_EPS = 1e-5
NEG_INF = -1e30


def layer_norm(x, g, b):
    xf = x.astype(jnp.float32)
    mu = jnp.mean(xf, axis=-1, keepdims=True)
    var = jnp.mean(jnp.square(xf - mu), axis=-1, keepdims=True)
    y = (xf - mu) * lax.rsqrt(var + LN_EPS) * g.astype(jnp.float32) + b.astype(jnp.float32)
    return y.astype(x.dtype)

def t5_bucket(dist):
    n = jnp.maximum(dist, 0)
    max_exact = REL_BUCKETS // 2
    nf = jnp.maximum(n, max_exact).astype(jnp.float32)
    large = max_exact + (jnp.log(nf / max_exact) / math.log(REL_MAX_DISTANCE / max_exact)
                         * (REL_BUCKETS - max_exact)).astype(jnp.int32)
    large = jnp.minimum(large, REL_BUCKETS - 1)
    return jnp.where(n < max_exact, n, large)

def gmlp_spatial_gating(u, v, ln_g, ln_b, w_s, b_s):
    bsz, seq, width = v.shape
    v = layer_norm(v, ln_g, ln_b)
    vc = v.reshape(bsz, seq // GMLP_CHUNK, GMLP_CHUNK, GMLP_GROUPS, width // GMLP_GROUPS)
    w_causal = jnp.tril(w_s)
    s = jnp.einsum('gts,bnsgc->bntgc', w_causal, vc) + b_s.T[None, None, :, :, None]
    return u * s.reshape(bsz, seq, width)

def moba_attention(q, k, v, rel_bias):
    bsz, seq, nh, hd = q.shape
    nb = -(-seq // MOBA_BLOCK)
    s_pad = nb * MOBA_BLOCK
    pad = ((0, 0), (0, s_pad - seq), (0, 0), (0, 0))
    q, k, v = (jnp.pad(t, pad).transpose(0, 2, 1, 3) for t in (q, k, v))
    kb = k.reshape(bsz, nh, nb, MOBA_BLOCK, hd)
    vb = v.reshape(bsz, nh, nb, MOBA_BLOCK, hd)
    scale = hd ** -0.5

    k_mean = jnp.mean(kb.astype(jnp.float32), axis=3).astype(q.dtype)
    gate = jnp.einsum('bhtd,bhnd->bhtn', q, k_mean).astype(jnp.float32)
    q_blk = jnp.arange(s_pad) // MOBA_BLOCK
    past = jnp.arange(nb)[None, :] < q_blk[:, None]
    gate = jnp.where(past, gate, NEG_INF)
    n_sel = min(MOBA_TOPK, nb)
    _, sel = lax.top_k(gate, n_sel)
    sel_valid = jnp.arange(n_sel)[None, :] < q_blk[:, None]

    n_chunks = s_pad // MOBA_QCHUNK
    q_c = q.reshape(bsz, nh, n_chunks, MOBA_QCHUNK, hd).transpose(2, 0, 1, 3, 4)
    sel_c = sel.reshape(bsz, nh, n_chunks, MOBA_QCHUNK, n_sel).transpose(2, 0, 1, 3, 4)
    valid_c = sel_valid.reshape(n_chunks, MOBA_QCHUNK, n_sel)
    b_idx = jnp.arange(bsz)[:, None, None]
    h_idx = jnp.arange(nh)[None, :, None]
    bias_h = rel_bias.T.astype(jnp.float32)
    offs = jnp.arange(MOBA_BLOCK)

    def chunk_attend(args):
        c, qc, selc, validc = args
        t = c * MOBA_QCHUNK + jnp.arange(MOBA_QCHUNK)
        own = (c * MOBA_QCHUNK) // MOBA_BLOCK
        k_own = lax.dynamic_index_in_dim(kb, own, axis=2, keepdims=False)
        v_own = lax.dynamic_index_in_dim(vb, own, axis=2, keepdims=False)
        d_own = t[:, None] - (own * MOBA_BLOCK + offs)[None, :]
        l_own = (jnp.einsum('bhqd,bhkd->bhqk', qc, k_own).astype(jnp.float32) * scale
                 + bias_h[:, t5_bucket(d_own)])
        logits = [jnp.where(d_own >= 0, l_own, NEG_INF)]
        for r in range(n_sel):
            idx = selc[..., r]
            k_g = kb[b_idx, h_idx, idx]
            d_r = t[:, None] - (idx[..., None] * MOBA_BLOCK + offs)
            l_r = (jnp.einsum('bhqd,bhqkd->bhqk', qc, k_g).astype(jnp.float32) * scale
                   + bias_h[h_idx[..., None], t5_bucket(d_r)])
            logits.append(jnp.where(validc[None, None, :, r, None], l_r, NEG_INF))
        w = jax.nn.softmax(jnp.concatenate(logits, axis=-1), axis=-1).astype(qc.dtype)
        out = jnp.einsum('bhqk,bhkd->bhqd', w[..., :MOBA_BLOCK], v_own)
        for r in range(n_sel):
            v_g = vb[b_idx, h_idx, selc[..., r]]
            w_r = w[..., (r + 1) * MOBA_BLOCK:(r + 2) * MOBA_BLOCK]
            out = out + jnp.einsum('bhqk,bhqkd->bhqd', w_r, v_g)
        return out

    out = lax.map(chunk_attend, (jnp.arange(n_chunks), q_c, sel_c, valid_c))
    out = out.transpose(1, 0, 3, 2, 4).reshape(bsz, s_pad, nh * hd)
    return out[:, :seq]

def peer_ffn(h, w_q, sub_keys, u_tab, v_tab):
    bsz, seq, d = h.shape
    n_tok = bsz * seq
    xt = h.reshape(n_tok, d)
    q = (xt @ w_q).reshape(n_tok, PEER_HEADS, 2, PEER_KEY_HALF)
    s = jnp.einsum('thpk,pnk->thpn', q, sub_keys).astype(jnp.float32)
    top_s, top_i = lax.top_k(s, PEER_TOPK)
    n_cand = PEER_TOPK * PEER_TOPK
    cand_s = (top_s[:, :, 0, :, None] + top_s[:, :, 1, None, :]).reshape(n_tok, PEER_HEADS, n_cand)
    cand_i = (top_i[:, :, 0, :, None] * PEER_N_KEYS + top_i[:, :, 1, None, :]).reshape(n_tok, PEER_HEADS, n_cand)
    best_s, best_pos = lax.top_k(cand_s, PEER_TOPK)
    experts = jnp.take_along_axis(cand_i, best_pos, axis=-1)
    gates = jax.nn.softmax(best_s, axis=-1).astype(h.dtype)
    n_chunks = n_tok // PEER_TOK_CHUNK

    def chunk_ffn(args):
        xc, ec, gc = args
        hid = jax.nn.gelu(jnp.einsum('chkd,cd->chk', u_tab[ec], xc), approximate=False)
        return jnp.einsum('chk,chkd->cd', gc * hid, v_tab[ec])

    y = lax.map(chunk_ffn, (xt.reshape(n_chunks, PEER_TOK_CHUNK, d),
                            experts.reshape(n_chunks, PEER_TOK_CHUNK, PEER_HEADS, PEER_TOPK),
                            gates.reshape(n_chunks, PEER_TOK_CHUNK, PEER_HEADS, PEER_TOPK)))
    return y.reshape(bsz, seq, d)

def first_inputs(seed: int = 0) -> dict:
    key = jax.random.key(seed)
    ks = jax.random.split(key, 24)
    f32 = jnp.float32
    beta = (8.0 * DEPTH) ** -0.25

    def nrm(k, shape, s):
        return jax.random.normal(k, shape, f32) * s

    v_off = 2 * GMLP_WIDTH + 2 * MOBA_WIDTH
    col_scale = jnp.ones((IN_TOTAL,), f32).at[v_off:v_off + MOBA_WIDTH].set(beta)
    return {
        'x': nrm(ks[0], (BATCH, SEQ, D_MODEL), 1.0),
        'p': nrm(ks[1], (DEPTH, BATCH, SEQ, PLE_DIM), 1.0),
        'w_in': nrm(ks[2], (DEPTH, D_MODEL, IN_TOTAL), D_MODEL ** -0.5) * col_scale,
        'b_in': nrm(ks[3], (DEPTH, IN_TOTAL), 0.02),
        'gmlp_ln_g': 1.0 + nrm(ks[4], (DEPTH, GMLP_WIDTH), 0.02),
        'gmlp_ln_b': nrm(ks[5], (DEPTH, GMLP_WIDTH), 0.02),
        'gmlp_w_s': nrm(ks[6], (DEPTH, GMLP_GROUPS, GMLP_CHUNK, GMLP_CHUNK), GMLP_CHUNK ** -0.5),
        'gmlp_b_s': 1.0 + nrm(ks[7], (DEPTH, GMLP_GROUPS, GMLP_CHUNK), 0.02),
        'w_proj_a': nrm(ks[8], (DEPTH, GMLP_WIDTH, D_MODEL), beta * GMLP_WIDTH ** -0.5),
        'w_proj_b': nrm(ks[9], (DEPTH, MOBA_WIDTH, D_MODEL), beta * MOBA_WIDTH ** -0.5),
        'w_out': nrm(ks[10], (DEPTH, D_MODEL, D_MODEL), beta * D_MODEL ** -0.5),
        'ln1_g': 1.0 + nrm(ks[11], (DEPTH, D_MODEL), 0.02),
        'ln1_b': nrm(ks[12], (DEPTH, D_MODEL), 0.02),
        'rel_bias': nrm(ks[13], (REL_BUCKETS, MOBA_HEADS), 0.5),
        'peer_w_q': nrm(ks[14], (DEPTH, D_MODEL, PEER_HEADS * PEER_KEY_DIM), D_MODEL ** -0.5),
        'peer_sub_keys': nrm(ks[15], (DEPTH, 2, PEER_N_KEYS, PEER_KEY_HALF), PEER_KEY_HALF ** -0.5),
        'peer_u': nrm(ks[16], (DEPTH, PEER_N_EXPERTS, D_MODEL), D_MODEL ** -0.5),
        'peer_v': nrm(ks[17], (DEPTH, PEER_N_EXPERTS, D_MODEL), beta * PEER_HEADS ** -0.5),
        'ple_w_proj': nrm(ks[18], (DEPTH, PLE_DIM, D_MODEL), beta * PLE_DIM ** -0.5),
        'ple_w_gate': nrm(ks[19], (DEPTH, D_MODEL, D_MODEL), D_MODEL ** -0.5),
        'ple_b_gate': nrm(ks[20], (DEPTH, D_MODEL), 0.02),
        'ln2_g': 1.0 + nrm(ks[21], (DEPTH, D_MODEL), 0.02),
        'ln2_b': nrm(ks[22], (DEPTH, D_MODEL), 0.02),
    }

def first_block(x, p, w_in, b_in, gmlp_ln_g, gmlp_ln_b, gmlp_w_s, gmlp_b_s, w_proj_a, w_proj_b,
              w_out, ln1_g, ln1_b, rel_bias, peer_w_q, peer_sub_keys, peer_u, peer_v,
              ple_w_proj, ple_w_gate, ple_b_gate, ln2_g, ln2_b):
    alpha = (2.0 * DEPTH) ** 0.25
    bsz, seq, _ = x.shape
    splits = [sum(IN_WIDTHS[:j + 1]) for j in range(len(IN_WIDTHS) - 1)]
    for i in range(DEPTH):
        z = x @ w_in[i] + b_in[i]
        u_a, v_a, q_b, k_b, v_b, g_a, g_b = jnp.split(z, splits, axis=-1)
        a = gmlp_spatial_gating(jax.nn.gelu(u_a, approximate=False), jax.nn.gelu(v_a, approximate=False),
                                gmlp_ln_g[i], gmlp_ln_b[i], gmlp_w_s[i], gmlp_b_s[i])
        head_shape = (bsz, seq, MOBA_HEADS, MOBA_HEAD_DIM)
        o = moba_attention(q_b.reshape(head_shape), k_b.reshape(head_shape), v_b.reshape(head_shape), rel_bias)
        m = jax.nn.sigmoid(g_a) * (a @ w_proj_a[i]) + jax.nn.sigmoid(g_b) * (o @ w_proj_b[i])
        h = layer_norm(alpha * x + m @ w_out[i], ln1_g[i], ln1_b[i])
        f = peer_ffn(h, peer_w_q[i], peer_sub_keys[i], peer_u[i], peer_v[i])
        e = (p[i] @ ple_w_proj[i]) * jax.nn.sigmoid(h @ ple_w_gate[i] + ple_b_gate[i])
        x = layer_norm(alpha * h + f + e, ln2_g[i], ln2_b[i])
    return x


_first_inputs = first_inputs


def first_inputs(seed=0):
    import zlib

    import numpy as np

    out = dict(_first_inputs(seed))
    spreads = {}
    factors = {'b_in': 7.01,
     'gmlp_ln_g': 148.665,
     'gmlp_ln_b': 135.98,
     'gmlp_b_s': 103.088,
     'rel_bias': 24.914,
     'ple_b_gate': 28.999,
     'ln2_g': 20.795,
     'ln2_b': 21.373,
     'w_proj_b': 4.001}
    for name, (base, spread) in spreads.items():
        noise = np.random.default_rng([zlib.crc32(name.encode()), seed]).standard_normal(out[name].shape)
        drawn = base * np.exp(spread * noise) if base else spread * noise
        out[name] = jnp.asarray(drawn.astype(out[name].dtype))
    for name, factor in factors.items():
        out[name] = (out[name] * factor).astype(out[name].dtype)
    return out


_narrow_inputs = first_inputs


def first_inputs(seed=0):

    out = dict(_narrow_inputs(seed))
    wider = {'gmlp_ln_g': 3.94, 'gmlp_ln_b': 3.92, 'gmlp_b_s': 3.79, 'ln2_g': 3.1, 'ln2_b': 3.1}
    for name, times in wider.items():
        mean = out[name].mean()
        out[name] = (mean + times * (out[name] - mean)).astype(out[name].dtype)
    return out


DEPTH_2 = 2

N_MIXERS = 3
HEAD_DIM = 64
N_HEADS = D_MODEL // HEAD_DIM
D_FF = 4 * D_MODEL
ROPE_THETA = 10000.0
NORM_EPS = 1e-6
NEG_INF_2 = -1e30
NSA_KV_GROUPS = 4
NSA_CMP_LEN = 32
NSA_CMP_STRIDE = 16
NSA_CMP_HIDDEN = 4 * HEAD_DIM
NSA_SEL_LEN = 64
NSA_TOP_N = 16
NSA_WINDOW = 512
NSA_SEL_QBLOCK = 32
NSA_FORCE_BONUS = 1000.0
FOX_QBLOCK = 128
SWA_KV_HEADS = 2
SWA_WINDOW = 128
BAND_QBLOCK = 128
N_LAYERS_A = len(range(0, DEPTH_2, N_MIXERS))
N_LAYERS_B = len(range(1, DEPTH_2, N_MIXERS))
N_LAYERS_C = len(range(2, DEPTH_2, N_MIXERS))


def rms_norm(x, g):
    xf = x.astype(jnp.float32)
    y = xf * lax.rsqrt(jnp.mean(xf * xf, axis=-1, keepdims=True) + NORM_EPS)
    return (y * g.astype(jnp.float32)).astype(x.dtype)

def rope_tables(seq):
    inv = ROPE_THETA ** (-jnp.arange(0, HEAD_DIM, 2, dtype=jnp.float32) / HEAD_DIM)
    ang = jnp.arange(seq, dtype=jnp.float32)[:, None] * inv[None, :]
    return jnp.cos(ang), jnp.sin(ang)

def apply_rope(x, cos, sin):
    xf = x.astype(jnp.float32)
    x1, x2 = jnp.split(xf, 2, axis=-1)
    c = cos[None, :, None, :]
    s = sin[None, :, None, :]
    return jnp.concatenate([x1 * c - x2 * s, x2 * c + x1 * s], axis=-1).astype(x.dtype)

def banded_attention(q, k, v, window, sinks=None):
    B, T, H, dh = q.shape
    G = k.shape[2]
    rep = H // G
    blk = BAND_QBLOCK
    nb = T // blk
    span = blk + window
    scale = dh ** -0.5
    kp = jnp.pad(k, ((0, 0), (window, 0), (0, 0), (0, 0)))
    vp = jnp.pad(v, ((0, 0), (window, 0), (0, 0), (0, 0)))
    qc = q.reshape(B, nb, blk, G, rep, dh).transpose(1, 0, 2, 3, 4, 5)
    offs_q = jnp.arange(blk)
    offs_k = jnp.arange(span) - window

    def one(args):
        i, qi = args
        start = i * blk
        kc = lax.dynamic_slice_in_dim(kp, start, span, axis=1)
        vc = lax.dynamic_slice_in_dim(vp, start, span, axis=1)
        qpos = start + offs_q
        kpos = start + offs_k
        dist = qpos[:, None] - kpos[None, :]
        valid = (kpos[None, :] >= 0) & (dist >= 0) & (dist < window)
        s = jnp.einsum('bqgrd,bkgd->bgrqk', qi, kc).astype(jnp.float32) * scale
        s = jnp.where(valid, s, NEG_INF_2)
        if sinks is None:
            p = jax.nn.softmax(s, axis=-1)
        else:
            sink = jnp.broadcast_to(sinks.astype(jnp.float32).reshape(G, rep)[None, :, :, None, None],
                                    (B, G, rep, blk, 1))
            p = jax.nn.softmax(jnp.concatenate([s, sink], axis=-1), axis=-1)[..., :-1]
        return jnp.einsum('bgrqk,bkgd->bqgrd', p.astype(vc.dtype), vc)

    out = lax.map(one, (jnp.arange(nb), qc))
    return out.transpose(1, 0, 2, 3, 4, 5).reshape(B, T, H, dh)

def nsa_compress(tok, pos, w1, w2):
    B, T, G, dh = tok.shape
    nc = (T - NSA_CMP_LEN) // NSA_CMP_STRIDE + 1
    idx = np.arange(nc)[:, None] * NSA_CMP_STRIDE + np.arange(NSA_CMP_LEN)[None, :]
    win = tok[:, idx] + pos[:, None, :].astype(tok.dtype)
    win = win.transpose(0, 1, 3, 2, 4).reshape(B, nc, G, NSA_CMP_LEN * dh)
    return jax.nn.silu(win @ w1) @ w2

def nsa_selected_attention(qg, k, v, sel):
    B, T, G, rep, dh = qg.shape
    ns = T // NSA_SEL_LEN
    n = sel.shape[-1]
    qb = NSA_SEL_QBLOCK
    nq = T // qb
    scale = dh ** -0.5
    kb = k.reshape(B, ns, NSA_SEL_LEN, G, dh).transpose(0, 3, 1, 2, 4)
    vb = v.reshape(B, ns, NSA_SEL_LEN, G, dh).transpose(0, 3, 1, 2, 4)
    qc = qg.reshape(B, nq, qb, G, rep, dh).transpose(1, 0, 2, 3, 4, 5)
    sc = sel.reshape(B, G, nq, qb, n).transpose(2, 0, 1, 3, 4)
    gather = jax.vmap(jax.vmap(lambda tab, ix: tab[ix]))
    offs = jnp.arange(NSA_SEL_LEN)

    def one(args):
        i, qi, si = args
        gk = gather(kb, si).reshape(B, G, qb, n * NSA_SEL_LEN, dh)
        gv = gather(vb, si).reshape(B, G, qb, n * NSA_SEL_LEN, dh)
        kpos = (si[..., None] * NSA_SEL_LEN + offs).reshape(B, G, qb, n * NSA_SEL_LEN)
        qpos = i * qb + jnp.arange(qb)
        valid = kpos <= qpos[None, None, :, None]
        s = jnp.einsum('bqgrd,bgqkd->bgrqk', qi, gk).astype(jnp.float32) * scale
        s = jnp.where(valid[:, :, None], s, NEG_INF_2)
        p = jax.nn.softmax(s, axis=-1)
        return jnp.einsum('bgrqk,bgqkd->bqgrd', p.astype(gv.dtype), gv)

    out = lax.map(one, (jnp.arange(nq), qc, sc))
    return out.transpose(1, 0, 2, 3, 4, 5).reshape(B, T, G * rep, dh)

def nsa_mixer(h, w_in, cmp_pos, cmp_w1, cmp_w2, w_out, cos, sin):
    B, T, _ = h.shape
    H, G, dh = N_HEADS, NSA_KV_GROUPS, HEAD_DIM
    rep = H // G
    kvw = G * dh
    scale = dh ** -0.5
    proj = h @ w_in
    sizes = [H * dh, kvw, kvw, kvw, kvw, kvw, kvw, 3 * H]
    cuts = np.cumsum(sizes)[:-1].tolist()
    q, kc_t, vc_t, ks, vs, kw, vw, gate = jnp.split(proj, cuts, axis=-1)
    q = apply_rope(q.reshape(B, T, H, dh), cos, sin)
    kc_t = apply_rope(kc_t.reshape(B, T, G, dh), cos, sin)
    ks = apply_rope(ks.reshape(B, T, G, dh), cos, sin)
    kw = apply_rope(kw.reshape(B, T, G, dh), cos, sin)
    vc_t = vc_t.reshape(B, T, G, dh)
    vs = vs.reshape(B, T, G, dh)
    vw = vw.reshape(B, T, G, dh)
    qg = q.reshape(B, T, G, rep, dh)
    tpos = jnp.arange(T)

    kcmp = nsa_compress(kc_t, cmp_pos[0], cmp_w1[0], cmp_w2[0])
    vcmp = nsa_compress(vc_t, cmp_pos[1], cmp_w1[1], cmp_w2[1])
    nc = kcmp.shape[1]
    s = jnp.einsum('btgrd,bcgd->bgrtc', qg, kcmp).astype(jnp.float32) * scale
    cend = jnp.arange(nc) * NSA_CMP_STRIDE + NSA_CMP_LEN - 1
    cvalid = cend[None, :] <= tpos[:, None]
    p_cmp = jax.nn.softmax(jnp.where(cvalid, s, NEG_INF_2), axis=-1)
    p_cmp = jnp.where((tpos >= NSA_CMP_LEN - 1)[:, None], p_cmp, 0.0)
    o_cmp = jnp.einsum('bgrtc,bcgd->btgrd', p_cmp.astype(vcmp.dtype), vcmp).reshape(B, T, H, dh)

    ns = T // NSA_SEL_LEN
    c_lo = np.arange(nc)[:, None] * NSA_CMP_STRIDE
    s_lo = np.arange(ns)[None, :] * NSA_SEL_LEN
    ov = np.clip(np.minimum(c_lo + NSA_CMP_LEN, s_lo + NSA_SEL_LEN) - np.maximum(c_lo, s_lo), 0, None)
    overlap = jnp.asarray(ov.astype(np.float32) / NSA_CMP_LEN)
    imp = jnp.einsum('bgrtc,cn->bgtn', p_cmp, overlap)
    tblk = tpos // NSA_SEL_LEN
    j = jnp.arange(ns)
    forced = (j[None, :] == 0) | (j[None, :] == tblk[:, None]) | (j[None, :] == tblk[:, None] - 1)
    bvalid = j[None, :] <= tblk[:, None]
    score = jnp.where(bvalid, imp + jnp.where(forced, NSA_FORCE_BONUS, 0.0), -1.0)
    n_top = min(NSA_TOP_N, ns)
    _, sel = lax.top_k(score, n_top)

    o_slc = nsa_selected_attention(qg, ks, vs, sel)
    o_win = banded_attention(q, kw, vw, NSA_WINDOW)

    g = jax.nn.sigmoid(gate.astype(jnp.float32)).reshape(B, T, H, 3)
    o = g[..., 0:1] * o_cmp + g[..., 1:2] * o_slc + g[..., 2:3] * o_win
    return o.astype(h.dtype).reshape(B, T, H * dh) @ w_out

def fox_attention(q, k, v, logf):
    B, T, H, dh = q.shape
    blk = FOX_QBLOCK
    nb = T // blk
    scale = dh ** -0.5
    c = jnp.cumsum(logf, axis=1).transpose(0, 2, 1)
    outs = []
    for i in range(nb):
        lo, hi = i * blk, (i + 1) * blk
        s = jnp.einsum('bqhd,bkhd->bhqk', q[:, lo:hi], k[:, :hi]).astype(jnp.float32) * scale
        s = s + c[:, :, lo:hi, None] - c[:, :, None, :hi]
        causal = jnp.arange(lo, hi)[:, None] >= jnp.arange(hi)[None, :]
        p = jax.nn.softmax(jnp.where(causal, s, NEG_INF_2), axis=-1)
        outs.append(jnp.einsum('bhqk,bkhd->bqhd', p.astype(v.dtype), v[:, :hi]))
    return jnp.concatenate(outs, axis=1)

def fox_mixer(h, w_in, b_f, w_out):
    B, T, _ = h.shape
    H, dh = N_HEADS, HEAD_DIM
    proj = h @ w_in
    q, k, v, fl = jnp.split(proj, [H * dh, 2 * H * dh, 3 * H * dh], axis=-1)
    logf = jax.nn.log_sigmoid(fl.astype(jnp.float32) + b_f.astype(jnp.float32))
    o = fox_attention(q.reshape(B, T, H, dh), k.reshape(B, T, H, dh), v.reshape(B, T, H, dh), logf)
    return o.reshape(B, T, H * dh) @ w_out

def swa_mixer(h, w_in, b_in, sinks, w_out, b_out, cos, sin):
    B, T, _ = h.shape
    H, G, dh = N_HEADS, SWA_KV_HEADS, HEAD_DIM
    proj = h @ w_in + b_in
    q, k, v = jnp.split(proj, [H * dh, H * dh + G * dh], axis=-1)
    q = apply_rope(q.reshape(B, T, H, dh), cos, sin)
    k = apply_rope(k.reshape(B, T, G, dh), cos, sin)
    o = banded_attention(q, k, v.reshape(B, T, G, dh), SWA_WINDOW, sinks)
    return o.reshape(B, T, H * dh) @ w_out + b_out

def squared_relu_mlp(h, w_up, w_down):
    return jnp.square(jax.nn.relu(h @ w_up)) @ w_down

def second_inputs(seed: int = 0) -> dict:
    key = jax.random.key(seed)
    ks = jax.random.split(key, 20)
    D, H, dh = D_MODEL, N_HEADS, HEAD_DIM
    f32 = jnp.float32
    nsa_in_w = H * dh + 6 * NSA_KV_GROUPS * dh + 3 * H
    fox_in_w = 3 * H * dh + H
    swa_in_w = H * dh + 2 * SWA_KV_HEADS * dh
    cmp_in = NSA_CMP_LEN * dh
    nrm = lambda k, shape, fan: jax.random.normal(k, shape, f32) * (fan ** -0.5)
    return {
        'x': jax.random.normal(ks[0], (BATCH, SEQ, D), f32),
        'norm_g': 1.0 + 0.02 * jax.random.normal(ks[1], (DEPTH_2, 4, D), f32),
        'mlp_w_up': nrm(ks[2], (DEPTH_2, D, D_FF), D),
        'mlp_w_down': nrm(ks[3], (DEPTH_2, D_FF, D), D_FF),
        'nsa_w_in': nrm(ks[4], (N_LAYERS_A, D, nsa_in_w), D),
        'nsa_cmp_pos': 0.2 * jax.random.normal(ks[5], (N_LAYERS_A, 2, NSA_CMP_LEN, dh), f32),
        'nsa_cmp_w1': nrm(ks[6], (N_LAYERS_A, 2, cmp_in, NSA_CMP_HIDDEN), cmp_in),
        'nsa_cmp_w2': nrm(ks[7], (N_LAYERS_A, 2, NSA_CMP_HIDDEN, dh), NSA_CMP_HIDDEN),
        'nsa_w_out': nrm(ks[8], (N_LAYERS_A, H * dh, D), H * dh),
        'fox_w_in': nrm(ks[9], (N_LAYERS_B, D, fox_in_w), D),
        'fox_b_f': jax.random.uniform(ks[10], (N_LAYERS_B, H), f32, 1.0, 5.0),
        'fox_w_out': nrm(ks[11], (N_LAYERS_B, H * dh, D), H * dh),
        'swa_w_in': nrm(ks[12], (N_LAYERS_C, D, swa_in_w), D),
        'swa_b_in': 0.02 * jax.random.normal(ks[13], (N_LAYERS_C, swa_in_w), f32),
        'swa_sinks': jax.random.normal(ks[14], (N_LAYERS_C, H), f32),
        'swa_w_out': nrm(ks[15], (N_LAYERS_C, H * dh, D), H * dh),
        'swa_b_out': 0.02 * jax.random.normal(ks[16], (N_LAYERS_C, D), f32),
    }

def second_block(x, norm_g, mlp_w_up, mlp_w_down, nsa_w_in, nsa_cmp_pos, nsa_cmp_w1, nsa_cmp_w2, nsa_w_out,
              fox_w_in, fox_b_f, fox_w_out, swa_w_in, swa_b_in, swa_sinks, swa_w_out, swa_b_out):
    T = x.shape[1]
    cos, sin = rope_tables(T)
    for i in range(DEPTH_2):
        kind = i % N_MIXERS
        slot = i // N_MIXERS
        h = rms_norm(x, norm_g[i, 0])
        if kind == 0:
            m = nsa_mixer(h, nsa_w_in[slot], nsa_cmp_pos[slot], nsa_cmp_w1[slot], nsa_cmp_w2[slot],
                          nsa_w_out[slot], cos, sin)
        elif kind == 1:
            m = fox_mixer(h, fox_w_in[slot], fox_b_f[slot], fox_w_out[slot])
        else:
            m = swa_mixer(h, swa_w_in[slot], swa_b_in[slot], swa_sinks[slot], swa_w_out[slot],
                          swa_b_out[slot], cos, sin)
        x = x + rms_norm(m, norm_g[i, 1])
        h = rms_norm(x, norm_g[i, 2])
        x = x + rms_norm(squared_relu_mlp(h, mlp_w_up[i], mlp_w_down[i]), norm_g[i, 3])
    return x


DEPTH_3 = 2

N_MIXERS_3 = 2
N_MLSTM = (DEPTH_3 + 1) // 2
N_HGRN = DEPTH_3 // 2
CHUNK = 64
M_HEADS = 8
M_DV = D_MODEL // M_HEADS
M_DQK = M_DV // 2
M_QK = M_HEADS * M_DQK
M_V = M_HEADS * M_DV
M_PROJ = 2 * M_QK + 2 * M_V + 2 * M_HEADS
CONV_K = 4
IGATE_CAP = 15.0
HG_EXPAND = 128
HG_HEADS = D_MODEL // HG_EXPAND
HG_DK = HG_EXPAND
HG_DV = D_MODEL // HG_HEADS
HG_PROJ = 2 * HG_HEADS * HG_DK + 2 * D_MODEL
D_FF_3 = 2816
N_EXPERTS = 8
TOP_K = 2
D_FF_EXPERT = D_FF_3 // 2
EPS = 1e-6
NEG = -1e30
F_FLOOR = 1e-30


def rmsnorm(x, w):
    x32 = x.astype(jnp.float32)
    y = x32 * lax.rsqrt(jnp.mean(x32 * x32, axis=-1, keepdims=True) + EPS)
    return (y * w.astype(jnp.float32)).astype(x.dtype)

def head_rmsnorm(h, w):
    nh, dh = h.shape[1], h.shape[3]
    y = h * lax.rsqrt(jnp.mean(h * h, axis=-1, keepdims=True) + EPS)
    return y * w.astype(jnp.float32).reshape(1, nh, 1, dh)

def split_heads(a, nh):
    b, s, _ = a.shape
    return a.reshape(b, s, nh, -1).transpose(0, 2, 1, 3)

def merge_heads(a):
    b, h, s, d = a.shape
    return a.transpose(0, 2, 1, 3).reshape(b, s, h * d)

def to_chunks(a):
    b, h, s = a.shape[:3]
    return jnp.moveaxis(a.reshape((b, h, s // CHUNK, CHUNK) + a.shape[3:]), 2, 0)

def from_chunks(a):
    a = jnp.moveaxis(a, 0, 2)
    b, h, nc, l = a.shape[:4]
    return a.reshape((b, h, nc * l) + a.shape[4:])

def causal_conv(x, w, b):
    ch = x.shape[-1]
    y = lax.conv_general_dilated(x, w[:, None, :].astype(x.dtype), window_strides=(1,),
                                 padding=[(w.shape[0] - 1, 0)],
                                 dimension_numbers=('NWC', 'WIO', 'NWC'),
                                 feature_group_count=ch)
    return y + b.astype(x.dtype)

def mlstm_chunkwise(q, k, v, li, f_pre):
    bsz, nh, _, dk = q.shape
    dv = v.shape[-1]
    lf = jax.nn.log_sigmoid(f_pre)
    mask = jnp.tril(jnp.ones((CHUNK, CHUNK), dtype=bool))

    def step(carry, xs):
        c_st, n_st, m_st = carry
        qc, kc, vc, lic, lfc = xs
        b = jnp.cumsum(lfc, axis=-1)
        d = jnp.where(mask, b[..., :, None] - b[..., None, :] + lic[..., None, :], NEG)
        inter = b + m_st[..., None]
        m_t = jnp.maximum(inter, jnp.max(d, axis=-1))
        w_inter = jnp.exp(inter - m_t)
        s = jnp.einsum('bhtd,bhsd->bhts', qc, kc) * jnp.exp(d - m_t[..., None])
        num = (w_inter[..., None] * jnp.einsum('bhtd,bhdv->bhtv', qc, c_st)
               + jnp.einsum('bhts,bhsv->bhtv', s, vc))
        den = w_inter * jnp.einsum('bhtd,bhd->bht', qc, n_st) + jnp.sum(s, axis=-1)
        h = num / jnp.maximum(jnp.abs(den), jnp.exp(-m_t))[..., None]
        b_last = b[..., -1]
        dl = b_last[..., None] - b + lic
        m_new = jnp.maximum(b_last + m_st, jnp.max(dl, axis=-1))
        wk = jnp.exp(dl - m_new[..., None])
        decay = jnp.exp(b_last + m_st - m_new)
        c_new = decay[..., None, None] * c_st + jnp.einsum('bhs,bhsd,bhsv->bhdv', wk, kc, vc)
        n_new = decay[..., None] * n_st + jnp.einsum('bhs,bhsd->bhd', wk, kc)
        return (c_new, n_new, m_new), h

    init = (jnp.zeros((bsz, nh, dk, dv), jnp.float32),
            jnp.zeros((bsz, nh, dk), jnp.float32),
            jnp.zeros((bsz, nh), jnp.float32))
    _, hs = lax.scan(step, init, (to_chunks(q), to_chunks(k), to_chunks(v), to_chunks(li), to_chunks(lf)))
    return from_chunks(hs)

def hgrn2_chunkwise(q, k, log_f, v):
    bsz, nh, _, dk = q.shape
    dv = v.shape[-1]
    mask = jnp.tril(jnp.ones((CHUNK, CHUNK), dtype=bool))

    def step(s_st, xs):
        qc, kc, gc, vc = xs
        bc = jnp.cumsum(gc, axis=2)
        diff = bc[:, :, :, None, :] - bc[:, :, None, :, :]
        decay = jnp.exp(jnp.where(mask[:, :, None], diff, NEG))
        a = jnp.einsum('bhtd,bhsd,bhtsd->bhts', qc, kc, decay)
        o = (jnp.einsum('bhtd,bhdv->bhtv', qc * jnp.exp(bc), s_st)
             + jnp.einsum('bhts,bhsv->bhtv', a, vc))
        b_last = bc[:, :, -1]
        s_new = (jnp.exp(b_last)[..., None] * s_st
                 + jnp.einsum('bhsd,bhsv->bhdv', kc * jnp.exp(b_last[:, :, None] - bc), vc))
        return s_new, o

    init = jnp.zeros((bsz, nh, dk, dv), jnp.float32)
    _, os_ = lax.scan(step, init, (to_chunks(q), to_chunks(k), to_chunks(log_f), to_chunks(v)))
    return from_chunks(os_)

def mlstm_mixer(h, w_in, i_bias, f_bias, conv_w, conv_b, norm_w, w_out):
    proj = h @ w_in
    qk = jax.nn.silu(causal_conv(proj[..., :2 * M_QK], conv_w, conv_b))
    q = split_heads(qk[..., :M_QK], M_HEADS).astype(jnp.float32)
    k = split_heads(qk[..., M_QK:], M_HEADS).astype(jnp.float32) * (M_DQK ** -0.5)
    v = split_heads(proj[..., 2 * M_QK:2 * M_QK + M_V], M_HEADS).astype(jnp.float32)
    o = proj[..., 2 * M_QK + M_V:2 * M_QK + 2 * M_V]
    gates = proj[..., 2 * M_QK + 2 * M_V:].astype(jnp.float32)
    i_pre = gates[..., :M_HEADS] + i_bias.astype(jnp.float32)
    i_pre = IGATE_CAP * jnp.tanh(i_pre / IGATE_CAP)
    f_pre = gates[..., M_HEADS:] + f_bias.astype(jnp.float32)
    hh = mlstm_chunkwise(q, k, v, jnp.swapaxes(i_pre, 1, 2), jnp.swapaxes(f_pre, 1, 2))
    hh = merge_heads(head_rmsnorm(hh, norm_w)).astype(h.dtype) * jax.nn.sigmoid(o)
    return hh @ w_out

def hgrn2_mixer(h, w_in, lb, norm_w, w_out):
    proj = h @ w_in
    fd = HG_HEADS * HG_DK
    q = jax.nn.silu(proj[..., :fd]).astype(jnp.float32)
    f = proj[..., fd:2 * fd].astype(jnp.float32)
    i = proj[..., 2 * fd:2 * fd + D_MODEL].astype(jnp.float32)
    g = proj[..., 2 * fd + D_MODEL:]
    lb = lb.astype(jnp.float32)
    f_t = lb + (1.0 - lb) * jax.nn.sigmoid(f)
    log_f = jnp.log(jnp.maximum(f_t, F_FLOOR))
    k = (1.0 - lb) * jax.nn.sigmoid(-f)
    o = hgrn2_chunkwise(split_heads(q, HG_HEADS), split_heads(k, HG_HEADS),
                        split_heads(log_f, HG_HEADS), split_heads(i, HG_HEADS))
    o = merge_heads(head_rmsnorm(o, norm_w)).astype(h.dtype) * jax.nn.silu(g)
    return o @ w_out

def swiglu(t, wg, wu, wd):
    return (jax.nn.silu(t @ wg) * (t @ wu)) @ wd

def moe_swiglu(h, router_w, wg, wu, wd):
    bsz, s, d = h.shape
    t = h.reshape(bsz * s, d)
    logits = (t @ router_w).astype(jnp.float32)
    top_logits, top_idx = lax.top_k(logits, TOP_K)
    top_w = jax.nn.softmax(top_logits, axis=-1)
    gates = jnp.einsum('tk,tke->te', top_w, jax.nn.one_hot(top_idx, N_EXPERTS, dtype=jnp.float32)).astype(h.dtype)
    y = jnp.zeros_like(t)
    for e in range(N_EXPERTS):
        y = y + gates[:, e:e + 1] * swiglu(t, wg[e], wu[e], wd[e])
    return y.reshape(bsz, s, d)

def third_inputs(seed: int = 0) -> dict:
    key = jax.random.key(seed)
    ks = iter(jax.random.split(key, 32))

    def nrm(shape, scale):
        return jax.random.normal(next(ks), shape, jnp.float32) * scale

    d = D_MODEL
    return {
        'x': nrm((BATCH, SEQ, d), 1.0),
        'c': nrm((BATCH, d), 1.0),
        'ada_w': nrm((DEPTH_3, d, 6 * d), 0.5 * d ** -0.5),
        'ada_b': nrm((DEPTH_3, 6 * d), 0.02),
        'norm1_w': 1.0 + nrm((DEPTH_3, d), 0.02),
        'norm2_w': 1.0 + nrm((DEPTH_3, d), 0.02),
        'final_norm_w': 1.0 + nrm((d,), 0.02),
        'm_w_in': nrm((N_MLSTM, d, M_PROJ), d ** -0.5),
        'm_i_bias': nrm((N_MLSTM, M_HEADS), 0.1),
        'm_f_bias': jnp.linspace(3.0, 6.0, M_HEADS, dtype=jnp.float32)[None, :] + nrm((N_MLSTM, M_HEADS), 0.1),
        'm_conv_w': nrm((N_MLSTM, CONV_K, 2 * M_QK), CONV_K ** -0.5),
        'm_conv_b': nrm((N_MLSTM, 2 * M_QK), 0.01),
        'm_norm_w': 1.0 + nrm((N_MLSTM, M_V), 0.02),
        'm_w_out': nrm((N_MLSTM, M_V, d), M_V ** -0.5),
        'h_w_in': nrm((N_HGRN, d, HG_PROJ), d ** -0.5),
        'h_lb_logits': nrm((N_HGRN, HG_HEADS * HG_DK), 0.5),
        'h_norm_w': 1.0 + nrm((N_HGRN, d), 0.02),
        'h_w_out': nrm((N_HGRN, d, d), d ** -0.5),
        'ffn_w_gate': nrm((N_MLSTM, d, D_FF_3), d ** -0.5),
        'ffn_w_up': nrm((N_MLSTM, d, D_FF_3), d ** -0.5),
        'ffn_w_down': nrm((N_MLSTM, D_FF_3, d), D_FF_3 ** -0.5),
        'moe_router': nrm((N_HGRN, d, N_EXPERTS), d ** -0.5),
        'moe_w_gate': nrm((N_HGRN, N_EXPERTS, d, D_FF_EXPERT), d ** -0.5),
        'moe_w_up': nrm((N_HGRN, N_EXPERTS, d, D_FF_EXPERT), d ** -0.5),
        'moe_w_down': nrm((N_HGRN, N_EXPERTS, D_FF_EXPERT, d), D_FF_EXPERT ** -0.5),
    }

def third_block(x, c, ada_w, ada_b, norm1_w, norm2_w, final_norm_w,
              m_w_in, m_i_bias, m_f_bias, m_conv_w, m_conv_b, m_norm_w, m_w_out,
              h_w_in, h_lb_logits, h_norm_w, h_w_out,
              ffn_w_gate, ffn_w_up, ffn_w_down,
              moe_router, moe_w_gate, moe_w_up, moe_w_down):
    cond = jax.nn.silu(c)
    gam = jax.nn.softmax(h_lb_logits.astype(jnp.float32), axis=0)
    lower_bounds = jnp.cumsum(gam, axis=0) - gam[:1]
    for layer in range(DEPTH_3):
        j = layer // N_MIXERS_3
        mod = (cond @ ada_w[layer] + ada_b[layer])[:, None, :]
        shift1, scale1, gate1, shift2, scale2, gate2 = jnp.split(mod, 6, axis=-1)
        hn = rmsnorm(x, norm1_w[layer]) * (1 + scale1) + shift1
        if layer % N_MIXERS_3 == 0:
            y = mlstm_mixer(hn, m_w_in[j], m_i_bias[j], m_f_bias[j], m_conv_w[j], m_conv_b[j],
                            m_norm_w[j], m_w_out[j])
        else:
            y = hgrn2_mixer(hn, h_w_in[j], lower_bounds[j], h_norm_w[j], h_w_out[j])
        x = x + gate1 * y
        hn = rmsnorm(x, norm2_w[layer]) * (1 + scale2) + shift2
        if layer % 2 == 0:
            y = swiglu(hn, ffn_w_gate[j], ffn_w_up[j], ffn_w_down[j])
        else:
            y = moe_swiglu(hn, moe_router[j], moe_w_gate[j], moe_w_up[j], moe_w_down[j])
        x = x + gate2 * y
    return rmsnorm(x, final_norm_w)


def setup_inputs(seed=0):
    out = dict(first_inputs(seed))
    for name, value in second_inputs(seed + 1).items():
        if name != "x":
            out[name + "_2"] = value
    for name, value in third_inputs(seed + 2).items():
        if name != "x":
            out[name + "_3"] = value
    return out


def reference(
    x, p, w_in, b_in, gmlp_ln_g, gmlp_ln_b, gmlp_w_s, gmlp_b_s, w_proj_a, w_proj_b, w_out,
    ln1_g, ln1_b, rel_bias, peer_w_q, peer_sub_keys, peer_u, peer_v, ple_w_proj, ple_w_gate,
    ple_b_gate, ln2_g, ln2_b, norm_g_2, mlp_w_up_2, mlp_w_down_2, nsa_w_in_2, nsa_cmp_pos_2,
    nsa_cmp_w1_2, nsa_cmp_w2_2, nsa_w_out_2, fox_w_in_2, fox_b_f_2, fox_w_out_2, swa_w_in_2,
    swa_b_in_2, swa_sinks_2, swa_w_out_2, swa_b_out_2, c_3, ada_w_3, ada_b_3, norm1_w_3,
    norm2_w_3, final_norm_w_3, m_w_in_3, m_i_bias_3, m_f_bias_3, m_conv_w_3, m_conv_b_3,
    m_norm_w_3, m_w_out_3, h_w_in_3, h_lb_logits_3, h_norm_w_3, h_w_out_3, ffn_w_gate_3,
    ffn_w_up_3, ffn_w_down_3, moe_router_3, moe_w_gate_3, moe_w_up_3, moe_w_down_3,
):
    x = first_block(
        x, p, w_in, b_in, gmlp_ln_g, gmlp_ln_b, gmlp_w_s, gmlp_b_s, w_proj_a, w_proj_b, w_out,
        ln1_g, ln1_b, rel_bias, peer_w_q, peer_sub_keys, peer_u, peer_v, ple_w_proj, ple_w_gate,
        ple_b_gate, ln2_g, ln2_b,
    )
    x = second_block(
        x, norm_g_2, mlp_w_up_2, mlp_w_down_2, nsa_w_in_2, nsa_cmp_pos_2, nsa_cmp_w1_2,
        nsa_cmp_w2_2, nsa_w_out_2, fox_w_in_2, fox_b_f_2, fox_w_out_2, swa_w_in_2, swa_b_in_2,
        swa_sinks_2, swa_w_out_2, swa_b_out_2,
    )
    return third_block(
        x, c_3, ada_w_3, ada_b_3, norm1_w_3, norm2_w_3, final_norm_w_3, m_w_in_3, m_i_bias_3,
        m_f_bias_3, m_conv_w_3, m_conv_b_3, m_norm_w_3, m_w_out_3, h_w_in_3, h_lb_logits_3,
        h_norm_w_3, h_w_out_3, ffn_w_gate_3, ffn_w_up_3, ffn_w_down_3, moe_router_3,
        moe_w_gate_3, moe_w_up_3, moe_w_down_3,
    )


_drawn_inputs = setup_inputs


def setup_inputs(seed=0):
    import zlib

    import numpy as np

    out = dict(_drawn_inputs(seed))
    spreads = {}
    factors = {'norm_g_2': 8.0,
     'nsa_cmp_pos_2': 6.475,
     'fox_b_f_2': 3.433,
     'c_3': 3.462,
     'ada_w_3': 3.309,
     'ada_b_3': 8.0,
     'norm1_w_3': 8.0,
     'norm2_w_3': 8.0,
     'final_norm_w_3': 7.536,
     'm_w_in_3': 7.485,
     'm_i_bias_3': 24.396,
     'm_f_bias_3': 8.0,
     'm_conv_w_3': 8.0,
     'm_conv_b_3': 64.0,
     'm_norm_w_3': 8.0,
     'm_w_out_3': 7.55,
     'h_w_in_3': 6.355,
     'h_norm_w_3': 64.0,
     'h_w_out_3': 6.298,
     'ffn_w_gate_3': 6.019,
     'ffn_w_up_3': 5.619,
     'ffn_w_down_3': 5.657,
     'moe_router_3': 8.0,
     'moe_w_gate_3': 8.0,
     'moe_w_up_3': 7.524,
     'moe_w_down_3': 7.494}
    for name, (base, spread) in spreads.items():
        noise = np.random.default_rng([zlib.crc32(name.encode()), seed]).standard_normal(out[name].shape)
        drawn = base * np.exp(spread * noise) if base else spread * noise
        out[name] = jnp.asarray(drawn.astype(out[name].dtype))
    for name, factor in factors.items():
        out[name] = (out[name] * factor).astype(out[name].dtype)
    return out
```

```python
import math
from contextlib import ExitStack, contextmanager

import concourse.bass as bass
import numpy as np
from concourse import mybir

F32 = mybir.dt.float32
F32R = mybir.dt.float32r
U32 = mybir.dt.uint32
ALU = mybir.AluOpType
ACT = mybir.ActivationFunctionType
AX = mybir.AxisListType

P = 128
TOKENS = 256
TT = TOKENS // P
D = 1024
DK = D // P
CHUNK = 4096
RING = 4
WIDE = 512
NEG = -1e30
ALPHA = 2.0 ** 0.25
LN_EPS = 1e-5
RMS_EPS = 1e-6
TRI = 3 * P
HEADS_A, HEADS_B, HEADS_C = 8, 16, 8
KEYS, TOPK, PEER_HEADS = 128, 16, 8
GROUPS, REP, HD = 4, 4, 64
N_CMP, CMP_LEN, CMP_STRIDE = 15, 32, 16
FFN_TILES, EXPERTS, EXPERT_TILES = 22, 8, 11
MLP_TILES = 32
LOG_FLOOR = math.log(1e-30)
IGATE_CAP = 15.0



def _k_major(w):
    k, n = w.shape
    return w.reshape(k // P, P, n).transpose(1, 0, 2).reshape(P, -1)


def _columns(v):
    return v.reshape(-1, P).T


def _rows(v):
    return np.broadcast_to(v.reshape(1, -1), (P, v.size))


def _pad_rows(a):
    out = np.zeros((P,) + a.shape[1:], a.dtype)
    out[:a.shape[0]] = a
    return out


def _bucket_of_distance():
    dist = np.arange(TOKENS)
    far = np.maximum(dist, 16).astype(np.float32)
    large = 16 + (np.log(far / np.float32(16)) / np.float32(math.log(64)) * np.float32(16)).astype(np.int32)
    return np.where(dist < 16, dist, np.minimum(large, 31))


def _rope_tables():
    inv = np.float32(10000.0) ** (-np.arange(0, HD, 2, dtype=np.float32) / np.float32(HD))
    angle = (np.arange(TOKENS, dtype=np.float32)[:, None] * inv[None, :]).astype(np.float32)
    table = lambda f: np.tile(f(angle).astype(np.float32).T, (4, 1))
    return table(np.cos), table(np.sin)


def _chunk_layout(a):
    out = []

    def product(w, step=WIDE):
        for n in range(0, w.shape[1], step):
            out.append(_k_major(w[:, n:n + step]))

    w = a["w_in"][0]
    for lo in (1024, 0, 4096, 2048, 3072, 5120, 6144):
        product(w[:, lo:lo + D])
    product(a["w_proj_a"][0])
    product(a["w_proj_b"][0])
    product(a["w_out"][0])
    product(a["ple_w_gate"][0])
    out.append(_k_major(a["ple_w_proj"][0]))
    product(a["peer_w_q"][0])
    u = a["peer_u"][0].reshape(KEYS, KEYS, DK, P).transpose(1, 3, 2, 0).reshape(KEYS, P, D)
    v = a["peer_v"][0].reshape(KEYS, KEYS, D).transpose(1, 0, 2)
    for j in range(0, KEYS, 2):
        out.append(np.concatenate([u[j], v[j], u[j + 1], v[j + 1]], 1))

    def mlp(up, down):
        for f in range(0, MLP_TILES, 2):
            out.append(np.concatenate([x for g in (f, f + 1) for x in
                                       (_k_major(up[:, g * P:g * P + P]), down[g * P:g * P + P])], 1))

    def glu(gate, up, down):
        for f in range(0, gate.shape[1], P):
            out.append(np.concatenate([_k_major(gate[:, f:f + P]), _k_major(up[:, f:f + P]), down[f:f + P]], 1))

    w = a["nsa_w_in_2"][0]
    order = [g * REP + r for pair in range(2) for r in range(REP) for g in (2 * pair, 2 * pair + 1)]
    q = w[:, :D].reshape(D, 16, HD)[:, order].reshape(D, D)
    kc, vc, ks, vs, kw, vw = (w[:, D + 256 * n:D + 256 * n + 256] for n in range(6))
    product(q)
    product(np.concatenate([kc, ks], 1))
    product(np.concatenate([kw, vc], 1))
    product(np.concatenate([vs, vw], 1))
    product(w[:, D + 6 * 256:])
    out.append(_k_major(a["nsa_cmp_w1_2"][0, 0]))
    out.append(_k_major(a["nsa_cmp_w1_2"][0, 1]))
    product(a["nsa_w_out_2"][0])
    mlp(a["mlp_w_up_2"][0], a["mlp_w_down_2"][0])
    product(a["fox_w_in_2"][0])
    product(a["fox_w_out_2"][0])
    mlp(a["mlp_w_up_2"][1], a["mlp_w_down_2"][1])
    product(a["ada_w_3"][0])
    product(a["ada_w_3"][1])
    product(a["m_w_in_3"][0])
    product(a["m_w_out_3"][0])
    glu(a["ffn_w_gate_3"][0], a["ffn_w_up_3"][0], a["ffn_w_down_3"][0])
    product(a["h_w_in_3"][0])
    product(a["h_w_out_3"][0])
    product(a["moe_router_3"][0])
    for f in range(EXPERT_TILES):
        for e in range(EXPERTS):
            tile = slice(f * P, f * P + P)
            glu(a["moe_w_gate_3"][0, e][:, tile], a["moe_w_up_3"][0, e][:, tile], a["moe_w_down_3"][0, e][tile])
    return out


def _param_layout(a):
    rel = a["rel_bias"].T[:, _bucket_of_distance()]
    t, s = np.arange(TOKENS)[:, None], np.arange(TOKENS)[None, :]
    toeplitz = rel[:, np.maximum(t - s, 0)]
    bias = np.concatenate([toeplitz[:, :P, :P], toeplitz[:, P:, :]], 2).transpose(1, 0, 2).reshape(P, -1)
    b_in = a["b_in"][0]
    w_s = a["gmlp_w_s"][0].transpose(2, 0, 1).reshape(P, -1)
    cos, sin = _rope_tables()
    pos = a["nsa_cmp_pos_2"][0].reshape(2, 16, P)
    w2 = a["nsa_cmp_w2_2"][0].reshape(2, 2, P, HD)
    w2k = np.concatenate([w2[0], w2[0]], 2).transpose(1, 0, 2).reshape(P, -1)
    w2v = w2[1].transpose(1, 0, 2).reshape(P, -1)
    ada = a["ada_b_3"].reshape(2, 6, D)
    return {
        "cols": {
            "b_u": _columns(b_in[0:1024]), "b_q": _columns(b_in[2048:3072]), "b_k": _columns(b_in[3072:4096]),
            "b_ga": _columns(b_in[5120:6144]), "b_gb": _columns(b_in[6144:7168]),
            "norm_g": np.concatenate([_columns(a["norm_g_2"][i, j]) for i in range(2) for j in (0, 2)], 1),
            "norm_w": np.concatenate([_columns(a[n][i]) for i in range(2) for n in ("norm1_w_3", "norm2_w_3")], 1),
            "conv_w": a["m_conv_w_3"][0].reshape(4, 8, P).transpose(2, 1, 0).reshape(P, -1),
            "conv_b": _columns(a["m_conv_b_3"][0]),
            "pos_k": pos[0].T, "pos_v": pos[1].T,
            "b_f": _pad_rows(a["fox_b_f_2"][0][:, None]),
            "i_bias": _pad_rows(a["m_i_bias_3"][0][:, None]), "f_bias": _pad_rows(a["m_f_bias_3"][0][:, None]),
            "cond": _columns(a["c_3"][0]),
        },
        "mix": {
            "b_va": _rows(b_in[1024:2048]), "b_vb": _rows(b_in[4096:5120]), "ln_g": _rows(a["gmlp_ln_g"][0]),
            "ln_b": _rows(a["gmlp_ln_b"][0]), "b_s": _rows(a["gmlp_b_s"][0]), "w_s": w_s,
            "ln1_g": _rows(a["ln1_g"][0]), "ln1_b": _rows(a["ln1_b"][0]), "rel": bias,
        },
        "peer": {
            "b_gate": _rows(a["ple_b_gate"][0]),
            "pT": _k_major(a["p"][0, 0].T), "keys": a["peer_sub_keys"][0].transpose(2, 0, 1).reshape(P, -1),
        },
        "ln2": {"g": _rows(a["ln2_g"][0]), "b": _rows(a["ln2_b"][0])},
        "nsa": {
            "cos": cos, "sin": sin, "w2k": w2k, "w2v": w2v,
            "post1": _rows(a["norm_g_2"][0, 1]), "post2": _rows(a["norm_g_2"][0, 3]),
        },
        "fox": {"post1": _rows(a["norm_g_2"][1, 1]), "post2": _rows(a["norm_g_2"][1, 3])},
        "ada": {
            "gates": np.concatenate([_rows(ada[i, j]) for i in range(2) for j in (2, 5)], 1),
            "shifts": np.concatenate([_columns(ada[i, j]) for i in range(2) for j in (0, 1, 3, 4)], 1),
        },
        "mlstm": {"norm_w": _rows(a["m_norm_w_3"][0])},
        "hgrn": {"norm_w": _rows(a["h_norm_w_3"][0])},
        "last": {"norm_w": _rows(a["final_norm_w_3"])},
    }



def spread(ap, axis, n):
    shape = list(ap.shape)
    return ap.unsqueeze(axis).broadcast_to(shape[:axis] + [n] + shape[axis:])


class Chain:

    def __init__(self, eng, sem):
        self.eng, self.sem, self.n = eng, sem, 0

    def __call__(self, ins):
        self.n += 1
        ins.then_inc(self.sem, 1)
        self.eng.wait_ge(self.sem, self.n)


class Stream:

    def __init__(self, dram, widths, ring, loaded, used):
        self.dram, self.widths, self.ring, self.loaded, self.used = dram, widths, ring, loaded, used
        self.asked = 0
        self.taken = 0
        self.pending = False

    def release(self, ins):
        if self.pending:
            ins.then_inc(self.used, 1)
            self.pending = False

    def slot(self, c):
        return self.ring[:, c % RING, :]

    def feed(self, sp, n):
        end = min(self.taken + n + RING - 1, len(self.widths))
        while self.asked < end:
            c = self.asked
            same = 0
            while c + same < end and self.widths[c + same] == self.widths[c]:
                same += 1
            turns = same // RING
            w = self.widths[c]
            if c >= RING and turns >= 2:
                with sp.Fori(0, turns) as i:
                    for s in range(RING):
                        sp.wait_ge(self.used, i * RING + (c + s - RING + 1))
                        src = self.dram[bass.ds(i * RING + (c + s), 1), :, 0:w].rearrange("a p n -> (a p) n")
                        sp.dma_start(self.slot(c + s)[:, 0:w], src).then_inc(self.loaded[(c + s) % RING], 16)
                self.asked += turns * RING
            else:
                if c >= RING:
                    sp.wait_ge(self.used, c - RING + 1)
                sp.dma_start(self.slot(c)[:, 0:w], self.dram[c, :, 0:w]).then_inc(self.loaded[c % RING], 16)
                self.asked += 1

    def wait(self, eng, c, turn=None):
        value = 16 * (c // RING + 1)
        eng.wait_ge(self.loaded[c % RING], value if turn is None else turn * 16 + value)

    def take(self, pe):
        c = self.taken
        self.taken += 1
        self.wait(pe, c)
        return c


def build(nc, d, widths, offsets):
    ctx = ExitStack()
    with ctx:
        names = {}

        def buffer(name, shape, dt=F32):
            names[name] = names.get(name, 0) + 1
            return nc.sbuf_tensor(name if names[name] == 1 else f"{name}_{names[name]}", shape, dt)

        def sbuf(name, shape, dt=F32, mem=ctx):
            return mem.enter_context(buffer(name, shape, dt))

        stage = [0]
        former = []

        @contextmanager
        def signals(*names):
            stage[0] += 1
            sems = [nc.alloc_semaphore(f"{n}_{stage[0]}") for n in names]
            if former:
                nc.clear_and_free_semaphores(former)
            former[:] = sems
            yield sems

        ring = sbuf("ring", [P, RING, CHUNK])
        x = sbuf("x", [P, TT, D])
        hT = sbuf("hT", [P, DK, TOKENS])
        n_cols = max(o + n for o, n in offsets["cols"].values())
        cols = sbuf("cols", [P, n_cols])
        ident = sbuf("ident", [P, P])
        ones = sbuf("ones", [P, TOKENS])
        mask = sbuf("mask", [P, TRI])
        eps_ln = sbuf("eps_ln", [P, 1])
        minus_half = sbuf("minus_half", [P, 16])
        ps = ctx.enter_context(nc.psum_tensor("ps", [P, 8, WIDE], F32))

        loaded = [ctx.enter_context(nc.semaphore(f"chunk_loaded_{i}")) for i in range(RING)]
        used = ctx.enter_context(nc.semaphore("chunk_used"))
        stream = Stream(d["stream"], widths, ring, loaded, used)

        def col(name, n=0, rows=P):
            o = offsets["cols"][name][0] + n
            return cols[0:rows, o:o + 1]

        def params(section, mem):
            n = max(o + w for o, w in offsets[section].values())
            buf = sbuf("params_" + section, [P, n], mem=mem)
            return buf, {k: buf[:, o:o + w] for k, (o, w) in offsets[section].items()}


        def product_t(pe, rhs, blocks, at, ready, freed, banks=4):
            c = stream.take(pe)
            w = stream.slot(c)
            n = stream.widths[c] // DK
            for b, (o, m) in enumerate(blocks):
                if at + b >= banks:
                    pe.wait_ge(freed, at + b - banks + 1)
                for k in range(DK):
                    last = pe.matmul(ps[0:m, (at + b) % banks, 0:TOKENS], w[:, k * n + o:k * n + o + m], rhs[:, k, :],
                                     start=(k == 0), stop=(k == DK - 1))
                    if b == 0 and k == 0:
                        stream.release(last)
                last.then_inc(ready, 1)
            stream.pending = True
            return at + len(blocks)

        def product_n(pe, lhsT, at, ready, freed, tiles=TT, k_tiles=DK):
            c = stream.take(pe)
            w = stream.slot(c)
            n = stream.widths[c] // k_tiles
            if at >= 2:
                pe.wait_ge(freed, at - 1)
            for t in range(tiles):
                for k in range(k_tiles):
                    last = pe.matmul(ps[:, 4 + 2 * (at % 2) + t, 0:n], lhsT[:, k, t * P:t * P + P], w[:, k * n:k * n + n],
                                     start=(k == 0), stop=(k == k_tiles - 1))
                    if t == 0 and k == 0:
                        stream.release(last)
            last.then_inc(ready, 1)
            stream.pending = True
            return at + 1

        def bank_n(at, n=WIDE):
            return ps[:, 4 + 2 * (at % 2):6 + 2 * (at % 2), 0:n]

        ALL_T = [(n * P, P) for n in range(4)]

        def transposes(pe, src, ready, freed, blocks=DK, banks=4):
            for b in range(blocks):
                if b >= banks:
                    pe.wait_ge(freed, b - banks + 1)
                for t in range(TT):
                    last = pe.transpose(ps[:, b % banks, t * P:t * P + P], src[:, t, b * P:b * P + P], ident[:])
                last.then_inc(ready, 1)

        stats = sbuf("stats", [P, TT, 2, 6])
        moments = sbuf("moments", [P, TT, 2])
        squares = sbuf("squares", [P, TT])
        spare = sbuf("spare", [P, TT])
        rstd = sbuf("rstd", [P, TT])

        def y_banks(t):
            return ps[:, 4 + t:8:2, :]

        def halves(ap):
            return ap.rearrange("p (c n) -> p c n", c=2)

        def power(pool, var_ready, rstd_ready):
            pool.wait_ge(var_ready, 1)
            pool.tensor_tensor(rstd[:], spare[:], minus_half[:, 0:TT], ALU.pow).then_inc(rstd_ready, 1)

        def layer_norm(dve, step, y, g, b, out, var_ready, rstd_ready):
            for t in range(TT):
                for c in range(2):
                    last = dve.bn_stats(stats[:, t, c, :], y[:, t, c * WIDE:c * WIDE + WIDE])
            step(last)
            for t in range(TT):
                last = dve.bn_aggr(moments[:, t, :], stats[:, t, :, :].rearrange("p a b -> p (a b)"))
            step(last)
            dve.tensor_scalar(spare[:], moments[:, :, 1], LN_EPS, None, ALU.add).then_inc(var_ready, 1)
            dve.wait_ge(rstd_ready, 1)
            for t in range(TT):
                last = dve.tensor_scalar(y[:, t, :], y[:, t, :], moments[:, t, 0:1], rstd[:, t:t + 1],
                                         ALU.subtract, ALU.mult)
            step(last)
            step(dve.tensor_tensor(y[:, :, :], y[:, :, :], spread(g, 1, TT), ALU.mult))
            return dve.tensor_tensor(out[:, :, :], y[:, :, :], spread(b, 1, TT), ALU.add)

        def pre_norm(gain, bias=None):
            with signals("squared", "var_ready", "rstd_ready", "scaled", "turned", "turned_read") as (
                    squared, var_ready, rstd_ready, scaled, turned, turned_read), \
                    buffer("xhat", [P, TT, D], F32) as xhat, \
                    nc.Block() as block:
                @block.scalar
                def _(act):
                    for t in range(TT):
                        last = act.activation(xhat[:, t, :], x[:, t, :], ACT.Square, accum_out=squares[:, t:t + 1])
                    last.then_inc(squared, 1)
                    for b in range(DK):
                        act.wait_ge(turned, b + 1)
                        act.activation(hT[:, b, :], ps[:, b % 4, 0:TOKENS], ACT.Identity, scale=gain(b),
                                       bias=0.0 if bias is None else bias(b)).then_inc(turned_read, 1)

                @block.vector
                def _(dve):
                    dve.wait_ge(squared, 1)
                    dve.tensor_scalar(spare[:], squares[:], 1.0 / D, RMS_EPS, ALU.mult, ALU.add).then_inc(var_ready, 1)
                    dve.wait_ge(rstd_ready, 1)
                    for t in range(TT):
                        last = dve.tensor_scalar(xhat[:, t, :], x[:, t, :], rstd[:, t:t + 1], None, ALU.mult)
                    last.then_inc(scaled, 1)

                @block.gpsimd
                def _(pool):
                    power(pool, var_ready, rstd_ready)

                @block.tensor
                def _(pe):
                    pe.wait_ge(scaled, 1)
                    transposes(pe, xhat, turned, turned_read)



        with signals("x_loaded", "pool_step") as (x_loaded, pool_step), nc.Block() as block:
            @block.sync
            def _(sp):
                sp.dma_start(x[:], d["x"]).then_inc(x_loaded, 16)
                sp.dma_start(hT[:], d["xT"]).then_inc(x_loaded, 16)
                sp.dma_start(cols[:], d["cols"]).then_inc(x_loaded, 16)
                stream.feed(sp, 0)
                sp.wait_ge(x_loaded, 48)

            @block.gpsimd
            def _(pool):
                step = Chain(pool, pool_step)
                pool.memset(ones[:], 1.0)
                pool.memset(minus_half[:], -0.5)
                pool.memset(mask[:], 0.0)
                step(pool.memset(ident[:], 0.0))
                pool.affine_select(out=ident[:], in_=ident[:], compare_op=ALU.not_equal, fill=1.0, base=0,
                                   pattern=[[-1, P]], channel_multiplier=1)
                for o in (0, 2 * P):
                    pool.affine_select(out=mask[:, o:o + P], in_=mask[:, o:o + P], compare_op=ALU.is_ge, fill=NEG,
                                       base=0, pattern=[[-1, P]], channel_multiplier=1)


        def mixers(mem):
            buf, p = params("mix", mem)
            uT, qT, kT, gaT, gbT = (sbuf(n, [P, DK, TOKENS], mem=mem) for n in ("uT", "qT", "kT", "gaT", "gbT"))
            v_a = sbuf("v_a", [P, TT, D], mem=mem)
            v_b = sbuf("v_b", [P, TT, D], mem=mem)

            with signals("params_loaded", "t_ready", "t_read", "n_ready", "n_read", "va_gelu", "var_ready", "rstd_ready",
                         "dve_step") as (params_loaded, t_ready, t_read, n_ready, n_read, va_gelu, var_ready,
                                         rstd_ready, dve_step), nc.Block() as block:
                @block.sync
                def _(sp):
                    sp.dma_start(buf[:], d["mix"]).then_inc(params_loaded, 16)
                    stream.feed(sp, 14)

                @block.tensor
                def _(pe):
                    at_t = at_n = 0
                    for part in "aabb":
                        if part == "a":
                            at_n = product_n(pe, hT, at_n, n_ready, n_read)
                        else:
                            at_t = product_t(pe, hT, ALL_T, at_t, t_ready, t_read)
                    for _ in range(2):
                        at_n = product_n(pe, hT, at_n, n_ready, n_read)
                    for _ in range(8):
                        at_t = product_t(pe, hT, ALL_T, at_t, t_ready, t_read)

                @block.scalar
                def _(act):
                    act.wait_ge(n_read, 2)
                    act.activation(v_a[:], v_a[:], ACT.Gelu).then_inc(va_gelu, 1)
                    at = 0
                    for out, bias, func in ((uT, "b_u", ACT.Gelu), (qT, "b_q", ACT.Identity), (kT, "b_k", ACT.Identity),
                                            (gaT, "b_ga", ACT.Sigmoid), (gbT, "b_gb", ACT.Sigmoid)):
                        for b in range(DK):
                            act.wait_ge(t_ready, at + 1)
                            act.activation(out[:, b, :], ps[:, at % 4, 0:TOKENS], func,
                                           bias=col(bias, b)).then_inc(t_read, 1)
                            at += 1

                @block.vector
                def _(dve):
                    step = Chain(dve, dve_step)
                    dve.wait_ge(params_loaded, 16)
                    for at, (out, bias, c) in enumerate(((v_a, "b_va", 0), (v_a, "b_va", 1), (v_b, "b_vb", 0), (v_b, "b_vb", 1))):
                        dve.wait_ge(n_ready, at + 1)
                        o = c * WIDE
                        dve.tensor_tensor(out[:, :, o:o + WIDE], bank_n(at), spread(p[bias][:, o:o + WIDE], 1, TT),
                                          ALU.add).then_inc(n_read, 1)
                    dve.wait_ge(va_gelu, 1)
                    layer_norm(dve, step, v_a, p["ln_g"], p["ln_b"], v_a, var_ready, rstd_ready)

                @block.gpsimd
                def _(pool):
                    power(pool, var_ready, rstd_ready)
                    pool.wait_ge(params_loaded, 16)
                    w = p["w_s"].rearrange("p (g t) -> p g t", g=8)
                    pool.affine_select(out=w, in_=w, compare_op=ALU.is_ge, fill=0.0, base=0, pattern=[[0, 8], [1, P]],
                                       channel_multiplier=-1)

            w_s = p["w_s"].rearrange("p (g t) -> p g t", g=8)
            b_s = p["b_s"].rearrange("p (g t) -> p g t", g=8)

            with signals("mixed", "mixed_read", "gated") as (mixed, mixed_read, gated), \
                    buffer("gate", [P, 2, TOKENS], F32) as gate, nc.Block() as block:
                @block.tensor
                def _(pe):
                    for g in range(8):
                        if g >= 4:
                            pe.wait_ge(mixed_read, g - 3)
                        for t in range(TT):
                            last = pe.matmul(ps[:, g % 4, t * P:t * P + P], v_a[:, t, g * P:g * P + P], w_s[:, g, :],
                                             start=True, stop=True)
                        last.then_inc(mixed, 1)

                @block.vector
                def _(dve):
                    for g in range(8):
                        dve.wait_ge(mixed, g + 1)
                        if g >= 2:
                            dve.wait_ge(gated, g - 1)
                        dve.tensor_tensor(gate[:, g % 2, :].rearrange("p (t n) -> p t n", t=TT),
                                          ps[:, g % 4, 0:TOKENS].rearrange("p (t n) -> p t n", t=TT),
                                          spread(b_s[:, g, :], 1, TT), ALU.add).then_inc(mixed_read, 1)

                @block.gpsimd
                def _(pool):
                    for g in range(8):
                        pool.wait_ge(mixed_read, g + 1)
                        pool.tensor_tensor(uT[:, g, :], uT[:, g, :], gate[:, g % 2, :], ALU.mult).then_inc(gated, 1)

            rel = p["rel"].rearrange("p (h n) -> p h n", h=HEADS_A)
            scale = float(P) ** -0.5

            def scores(pe, h):
                pe.matmul(ps[:, h % 2, 0:P], qT[:, h, 0:P], kT[:, h, 0:P], start=True, stop=True)
                return pe.matmul(ps[:, h % 2, P:TRI], qT[:, h, P:TOKENS], kT[:, h, :], start=True, stop=True)

            def logits(dve, step, h, out):
                step(dve.scalar_tensor_tensor(out, ps[:, h % 2, 0:TRI], scale, rel[:, h, :], ALU.mult, ALU.add))
                return dve.tensor_tensor(out, out, mask[:], ALU.add)

            attention(HEADS_A, scores, logits, lambda h, s: v_b[:, s, h * P:h * P + P],
                      lambda h, t: ps[:, 4 + 2 * (h // 4) + t, (h % 4) * P:(h % 4) * P + P])
            o = v_a
            oT, mT = qT, kT
            turn_heads(o, oT)

            with signals("t_ready", "t_read", "summed") as (t_ready, t_read, summed), \
                    buffer("part_b", [P, 2, TOKENS], F32) as part_b, nc.Block() as block:
                @block.sync
                def _(sp):
                    stream.feed(sp, 4)

                @block.tensor
                def _(pe):
                    at = 0
                    for rhs in (uT, uT, oT, oT):
                        at = product_t(pe, rhs, ALL_T, at, t_ready, t_read)

                @block.vector
                def _(dve):
                    for at in range(2 * DK):
                        b = at % DK
                        dve.wait_ge(t_ready, at + 1)
                        if at < DK:
                            dve.tensor_tensor(mT[:, b, :], ps[:, at % 4, 0:TOKENS], gaT[:, b, :], ALU.mult).then_inc(t_read, 1)
                        else:
                            if b >= 2:
                                dve.wait_ge(summed, b - 1)
                            dve.tensor_tensor(part_b[:, b % 2, :], ps[:, at % 4, 0:TOKENS], gbT[:, b, :],
                                              ALU.mult).then_inc(t_read, 1)

                @block.gpsimd
                def _(pool):
                    for b in range(DK):
                        pool.wait_ge(t_read, DK + b + 1)
                        pool.tensor_tensor(mT[:, b, :], mT[:, b, :], part_b[:, b % 2, :], ALU.add).then_inc(summed, 1)

            with signals("n_ready", "n_read", "var_ready", "rstd_ready", "dve_step", "normed", "turned", "turned_read") as (
                    n_ready, n_read, var_ready, rstd_ready, dve_step, normed, turned, turned_read), nc.Block() as block:
                @block.sync
                def _(sp):
                    stream.feed(sp, 2)

                @block.tensor
                def _(pe):
                    for at in range(2):
                        product_n(pe, mT, at, n_ready, n_read)
                    pe.wait_ge(normed, 1)
                    transposes(pe, x, turned, turned_read)

                @block.vector
                def _(dve):
                    step = Chain(dve, dve_step)
                    for at in range(2):
                        dve.wait_ge(n_ready, at + 1)
                        o = x[:, :, at * WIDE:at * WIDE + WIDE]
                        step(dve.scalar_tensor_tensor(o, o, ALPHA, bank_n(at), ALU.mult, ALU.add))
                    layer_norm(dve, step, x, p["ln1_g"], p["ln1_b"], x, var_ready, rstd_ready).then_inc(normed, 1)

                @block.gpsimd
                def _(pool):
                    power(pool, var_ready, rstd_ready)

                @block.scalar
                def _(act):
                    copy_turned(act, hT, turned, turned_read)

        def copy_turned(act, out, turned, turned_read):
            for b in range(DK):
                act.wait_ge(turned, b + 1)
                act.activation(out[:, b, :], ps[:, b % 4, 0:TOKENS], ACT.Copy).then_inc(turned_read, 1)

        def turn_heads(o, oT):
            with signals("copied", "turned", "turned_read") as (copied, turned, turned_read), nc.Block() as block:
                @block.vector
                def _(dve):
                    for t in range(TT):
                        dve.tensor_copy(halves(o[:, t, :]), y_banks(t)).then_inc(copied, 1)

                @block.tensor
                def _(pe):
                    pe.wait_ge(copied, TT)
                    transposes(pe, o, turned, turned_read)

                @block.scalar
                def _(act):
                    copy_turned(act, oT, turned, turned_read)

        def attention(n, scores, logits, values, out, gate=None, starts=True):
            with signals("scored", "biased", "exped", "probs_ready", "probs_turned", "turned_copied", "weighted", "dve_step") as (
                    scored, biased, exped, probs_ready, probs_turned, turned_copied, weighted, dve_step), ExitStack() as mem:
                prob = sbuf("prob", [P, 2, TRI], mem=mem)
                prob_t = sbuf("prob_t", [P, 2, TRI], mem=mem)
                top = sbuf("top", [P, 2, TT], mem=mem)
                total = sbuf("total", [P, 2, TT], mem=mem)
                part = (slice(0, P), slice(P, TRI))
                block = mem.enter_context(nc.Block())

                @block.tensor
                def _(pe):
                    for i in range(n + 2):
                        if i < n:
                            if i >= 2:
                                pe.wait_ge(biased, i - 1)
                            scores(pe, i).then_inc(scored, 1)
                        j = i - 1
                        if 0 <= j < n:
                            pe.wait_ge(probs_ready, j + 1)
                            if j >= 2:
                                pe.wait_ge(turned_copied, j - 1)
                            for b in range(3):
                                last = pe.transpose(ps[:, 2 + j % 2, b * P:b * P + P], prob[:, j % 2, b * P:b * P + P], ident[:])
                            last.then_inc(probs_turned, 1)
                        j = i - 2
                        if j >= 0:
                            pe.wait_ge(turned_copied, j + 1)
                            t = prob_t[:, j % 2, :]
                            pe.matmul(out(j, 0), t[:, 0:P], values(j, 0), start=starts, stop=True, skip_group_check=True)
                            pe.matmul(out(j, 1), t[:, P:2 * P], values(j, 0), start=starts, stop=False, skip_group_check=True)
                            pe.matmul(out(j, 1), t[:, 2 * P:TRI], values(j, 1), start=False, stop=True,
                                      skip_group_check=True).then_inc(weighted, 1)

                @block.vector
                def _(dve):
                    step = Chain(dve, dve_step)
                    for i in range(n + 1):
                        if i < n:
                            dve.wait_ge(scored, i + 1)
                            if i >= 2:
                                dve.wait_ge(probs_turned, i - 1)
                            step(logits(dve, step, i, prob[:, i % 2, :]))
                            for t in range(TT):
                                last = dve.tensor_reduce(top[:, i % 2, t:t + 1], prob[:, i % 2, part[t]], AX.X, ALU.max,
                                                         negate=True)
                            last.then_inc(biased, 1)
                        j = i - 1
                        if j >= 0:
                            dve.wait_ge(exped, j + 1)
                            step(dve.reciprocal(total[:, j % 2, :], total[:, j % 2, :]))
                            if gate is not None:
                                step(dve.tensor_tensor(total[:, j % 2, :], total[:, j % 2, :], gate(j), ALU.mult))
                            for t in range(TT):
                                o = prob[:, j % 2, part[t]]
                                last = dve.tensor_scalar(o, o, total[:, j % 2, t:t + 1], None, ALU.mult)
                            last.then_inc(probs_ready, 1)

                @block.scalar
                def _(act):
                    for i in range(n + 2):
                        if i < n:
                            act.wait_ge(biased, i + 1)
                            for t in range(TT):
                                o = prob[:, i % 2, part[t]]
                                last = act.activation(o, o, ACT.Exp, bias=top[:, i % 2, t:t + 1],
                                                      accum_out=total[:, i % 2, t:t + 1])
                            last.then_inc(exped, 1)
                        j = i - 1
                        if 0 <= j < n:
                            act.wait_ge(probs_turned, j + 1)
                            if j >= 2:
                                act.wait_ge(weighted, j - 1)
                            act.activation(prob_t[:, j % 2, :], ps[:, 2 + j % 2, 0:TRI], ACT.Copy).then_inc(turned_copied, 1)


        def feed_forward(kind, tiles, act_func, gates=1, starts=True, stops=True, scale_by=None, x_parts=None, work=None):
            per_chunk = 2 if gates == 1 else 1
            n_up = gates * D
            size = n_up + D
            turn = RING * per_chunk
            first = stream.taken
            n_chunks = tiles // per_chunk
            head = 2
            with signals("up_ready", "acted", "scaled_ready", "full_ready", "high_ready", "hidden_ready", "down_done",
                         "up_hi_ready", "up_split", "down_hi_ready", "down_split", "x_hi_ready", "x_split") as (
                    up_ready, acted, scaled_ready, full_ready, high_ready, hidden_ready, down_done,
                    up_hi_ready, up_split, down_hi_ready, down_split, x_hi_ready, x_split), \
                    buffer("hidden_hi", [P, 2, TOKENS], F32R) as hidden_hi, \
                    buffer("hidden_lo", [P, 2, TOKENS], F32R) as hidden_lo, \
                    buffer("up_hi", [P, 2, n_up], F32R) as up_hi, buffer("up_lo", [P, 2, n_up], F32R) as up_lo, \
                    buffer("down_hi", [P, 2, D], F32R) as down_hi, buffer("down_lo", [P, 2, D], F32R) as down_lo, \
                    ExitStack() as mem:
                if x_parts is None:
                    x_hi, x_lo = (sbuf(n, [P, DK, TOKENS], F32R, mem=mem) for n in ("x_hi", "x_lo"))
                else:
                    x_hi, x_lo = x_parts
                if work is None:
                    work = sbuf("work", [P, 2, 2, TOKENS], mem=mem)
                act_out, full = work[:, 0], work[:, 1]
                block = mem.enter_context(nc.Block())

                def later(value, i):
                    return value if i is None else i * turn + value

                def raw(j):
                    o = j % per_chunk * size
                    return stream.slot(first + j // per_chunk)[:, o:o + size]

                def run(eng, step, n, times=1):
                    span = turn * times
                    turns = max((n - head) // span, 0)
                    for j in range(min(head, n)):
                        step(j)
                    if turns:
                        with eng.Fori(0, turns) as i:
                            for j in range(head, head + span):
                                step(j, i * times if times > 1 else i)
                    for j in range(head + turns * span, n):
                        step(j)

                @block.sync
                def _(sp):
                    stream.feed(sp, n_chunks)

                @block.tensor
                def _(pe):
                    def up(j, i=None):
                        hi, lo = up_hi[:, j % 2, :], up_lo[:, j % 2, :]
                        pe.wait_ge(up_split, later(j + 1, i))
                        if i is not None or j >= 2:
                            pe.wait_ge(hidden_ready, later(j - 1, i))
                        for g in range(gates):
                            out = ps[:, j % 2, g * TOKENS:g * TOKENS + TOKENS]
                            for k in range(DK):
                                o = g * D + k * P
                                last = pe.matmul(out, hi[:, o:o + P], x_hi[:, k, :], start=(k == 0), stop=False)
                                if g == 0 and k == 0 and i is None and j == 0:
                                    stream.release(last)
                                pe.matmul(out, hi[:, o:o + P], x_lo[:, k, :], start=False, stop=False)
                                last = pe.matmul(out, lo[:, o:o + P], x_hi[:, k, :], start=False, stop=(k == DK - 1))
                        last.then_inc(up_ready, 1)

                    def down(j, i=None):
                        hi, lo = down_hi[:, j % 2, :], down_lo[:, j % 2, :]
                        pe.wait_ge(down_split, later(j + 1, i))
                        pe.wait_ge(hidden_ready, later(j + 1, i))
                        for t in range(TT):
                            tokens = slice(t * P, t * P + P)
                            for c in range(2):
                                o = c * WIDE
                                out = ps[:, 4 + 2 * c + t, :]
                                last = pe.matmul(out, hidden_hi[:, j % 2, tokens], hi[:, o:o + WIDE],
                                                 start=(starts and i is None and j == 0), stop=False, skip_group_check=True)
                                if t == 0 and c == 0 and j % per_chunk == per_chunk - 1:
                                    last.then_inc(used, 1)
                                pe.matmul(out, hidden_hi[:, j % 2, tokens], lo[:, o:o + WIDE], start=False, stop=False,
                                          skip_group_check=True)
                            for c in range(2):
                                o = c * WIDE
                                last = pe.matmul(ps[:, 4 + 2 * c + t, :], hidden_lo[:, j % 2, tokens], hi[:, o:o + WIDE], start=False,
                                                 stop=(stops and i is None and j == tiles - 1), skip_group_check=True)
                        last.then_inc(down_done, 1)

                    def step(j, i=None):
                        up(j + 1, i)
                        down(j, i)

                    if x_parts is None:
                        pe.wait_ge(x_split, 1)
                    up(0)
                    run(pe, step, tiles - 1)
                    down(tiles - 1)
                    stream.taken += n_chunks
                    stream.pending = False

                @block.scalar
                def _(act):
                    def split_up(j, i=None):
                        if j % per_chunk == 0:
                            stream.wait(act, first + j // per_chunk, i)
                        act.activation(up_hi[:, j % 2, :], raw(j)[:, 0:n_up], ACT.Copy).then_inc(up_hi_ready, 1)

                    def split_down(j, i=None):
                        if i is not None or j >= 2:
                            act.wait_ge(down_done, later(j - 1, i))
                        act.activation(down_hi[:, j % 2, :], raw(j)[:, n_up:size], ACT.Copy).then_inc(down_hi_ready, 1)

                    def step(j, i=None):
                        act.wait_ge(up_ready, later(j + 1, i))
                        if i is not None or j >= 2:
                            act.wait_ge(hidden_ready, later(j - 1, i))
                        act.activation(act_out[:, j % 2, :], ps[:, j % 2, 0:TOKENS], act_func).then_inc(acted, 1)
                        if i is not None or j + 2 < tiles:
                            split_up(j + 2, i)
                        if i is not None or j + 1 < tiles:
                            split_down(j + 1, i)

                    split_up(0)
                    split_up(1)
                    split_down(0)
                    run(act, step, tiles - 2)
                    for j in range(tiles - 2, tiles):
                        step(j)

                @block.vector
                def _(dve):
                    def split_up(j, i=None):
                        dve.wait_ge(up_hi_ready, later(j + 1, i))
                        dve.tensor_tensor(up_lo[:, j % 2, :], raw(j)[:, 0:n_up], up_hi[:, j % 2, :], ALU.subtract).then_inc(up_split, 1)

                    def split_down(j, i=None):
                        dve.wait_ge(down_hi_ready, later(j + 1, i))
                        dve.tensor_tensor(down_lo[:, j % 2, :], raw(j)[:, n_up:size], down_hi[:, j % 2, :],
                                          ALU.subtract).then_inc(down_split, 1)

                    def step(j, i=None):
                        b = j % 2
                        dve.wait_ge(acted, later(j + 1, i))
                        if i is not None or j >= 2:
                            dve.wait_ge(down_done, later(j - 1, i))
                        if kind == "relu2":
                            ins = dve.tensor_tensor(full[:, b, :], act_out[:, b, :], act_out[:, b, :], ALU.mult)
                        elif kind == "peer":
                            gate = scale_by[:, j, :] if i is None else \
                                scale_by[:, bass.ds(i * turn + j, 1), :].rearrange("p a n -> p (a n)")
                            ins = dve.tensor_tensor(full[:, b, :], act_out[:, b, :], gate, ALU.mult)
                        elif kind == "swiglu":
                            ins = dve.tensor_tensor(full[:, b, :], act_out[:, b, :], ps[:, b, TOKENS:2 * TOKENS], ALU.mult)
                        else:
                            dve.tensor_tensor(act_out[:, b, :], act_out[:, b, :], scale_by[:, j % EXPERTS, :],
                                              ALU.mult).then_inc(scaled_ready, 1)
                            dve.wait_ge(scaled_ready, later(j + 1, i))
                            ins = dve.tensor_tensor(full[:, b, :], act_out[:, b, :], ps[:, b, TOKENS:2 * TOKENS], ALU.mult)
                        ins.then_inc(full_ready, 1)
                        dve.wait_ge(full_ready, later(j + 1, i))
                        dve.tensor_copy(hidden_hi[:, b, :], full[:, b, :]).then_inc(high_ready, 1)
                        dve.wait_ge(high_ready, later(j + 1, i))
                        dve.tensor_tensor(hidden_lo[:, b, :], full[:, b, :], hidden_hi[:, b, :], ALU.subtract).then_inc(hidden_ready, 1)
                        if i is not None or j + 2 < tiles:
                            split_up(j + 2, i)
                        if i is not None or j + 1 < tiles:
                            split_down(j + 1, i)

                    if x_parts is None:
                        dve.tensor_copy(x_hi[:], hT[:]).then_inc(x_hi_ready, 1)
                        dve.wait_ge(x_hi_ready, 1)
                        dve.tensor_tensor(x_lo[:], hT[:], x_hi[:], ALU.subtract).then_inc(x_split, 1)
                    split_up(0)
                    split_up(1)
                    split_down(0)
                    run(dve, step, tiles - 2, times=EXPERTS // turn if kind == "moe" else 1)
                    for j in range(tiles - 2, tiles):
                        step(j)


        def peer(mem):
            expert = sbuf("expert", [P, 3, TOKENS], mem=mem)
            key_no = sbuf("key_no", [P, KEYS], mem=mem)
            groups = PEER_HEADS * 2
            lists = PEER_HEADS * TOPK
            with ExitStack() as route:
                buf, p = params("peer", route)
                rest = sbuf("rest", [P, TT, D], mem=route)
                qT = sbuf("qT", [P, groups, TOKENS], mem=route)
                score = sbuf("score", [P, TT, groups, KEYS], mem=route)
                pT = p["pT"].rearrange("p (k n) -> p k n", k=2)

                with signals("params_loaded", "n_ready", "n_read", "t_ready", "t_read", "gate_biased", "gate_ready",
                             "dve_step", "turned_q") as (params_loaded, n_ready, n_read, t_ready, t_read, gate_biased,
                                                         gate_ready, dve_step, turned_q), nc.Block() as block:
                    @block.sync
                    def _(sp):
                        sp.dma_start(buf[:], d["peer"]).then_inc(params_loaded, 16)
                        stream.feed(sp, 7)

                    @block.tensor
                    def _(pe):
                        at = 0
                        for _ in range(2):
                            at = product_n(pe, hT, at, n_ready, n_read)
                        pe.wait_ge(params_loaded, 16)
                        c = stream.take(pe)
                        w = stream.slot(c)
                        for h in range(2):
                            pe.wait_ge(n_read, h + 1)
                            for t in range(TT):
                                for k in range(2):
                                    last = pe.matmul(ps[:, 4 + 2 * h + t, :], pT[:, k, t * P:t * P + P],
                                                     w[:, k * D + h * WIDE:k * D + h * WIDE + WIDE], start=(k == 0), stop=(k == 1))
                                    if h + t + k == 0:
                                        stream.release(last)
                            last.then_inc(n_ready, 1)
                        stream.pending = True
                        at_t = 0
                        for _ in range(4):
                            at_t = product_t(pe, hT, ALL_T, at_t, t_ready, t_read)

                    @block.scalar
                    def _(act):
                        act.wait_ge(gate_biased, 1)
                        act.activation(rest[:], rest[:], ACT.Sigmoid).then_inc(gate_ready, 1)
                        for b in range(groups):
                            act.wait_ge(t_ready, b + 1)
                            act.activation(qT[:, b, :], ps[:, b % 4, 0:TOKENS], ACT.Copy).then_inc(t_read, 1)

                    @block.vector
                    def _(dve):
                        step = Chain(dve, dve_step)
                        dve.wait_ge(params_loaded, 16)
                        for h in range(2):
                            o = slice(h * WIDE, h * WIDE + WIDE)
                            dve.wait_ge(n_ready, h + 1)
                            last = dve.tensor_tensor(rest[:, :, o], bank_n(h), spread(p["b_gate"][:, o], 1, TT), ALU.add)
                            last.then_inc(n_read, 1)
                        dve.wait_ge(n_read, 2)
                        dve.memset(spare[:], 0.0).then_inc(gate_biased, 1)
                        dve.wait_ge(gate_ready, 1)
                        for h in range(2):
                            o = slice(h * WIDE, h * WIDE + WIDE)
                            dve.wait_ge(n_ready, 3 + h)
                            step(dve.tensor_tensor(rest[:, :, o], rest[:, :, o], bank_n(h), ALU.mult))
                        step(dve.scalar_tensor_tensor(x[:, :, :], x[:, :, :], ALPHA, rest[:, :, :], ALU.mult, ALU.add))

                keys = p["keys"].rearrange("p (h n) -> p h n", h=2)
                with signals("scored", "score_read") as (scored, score_read), nc.Block() as block:
                    @block.tensor
                    def _(pe):
                        for n in range(TT * groups // 4):
                            t, g = n // 4, n % 4 * 4
                            if n >= 4:
                                pe.wait_ge(score_read, n - 3)
                            for b in range(4):
                                last = pe.matmul(ps[:, n % 4, b * KEYS:b * KEYS + KEYS], qT[:, g + b, t * P:t * P + P],
                                                 keys[:, (g + b) % 2, :], start=True, stop=True)
                            last.then_inc(scored, 1)

                    @block.scalar
                    def _(act):
                        for n in range(TT * groups // 4):
                            act.wait_ge(scored, n + 1)
                            act.activation(score[:, n // 4, n % 4 * 4:n % 4 * 4 + 4, :],
                                           ps[:, n % 4, :].rearrange("p (b n) -> p b n", b=4), ACT.Copy).then_inc(score_read, 1)

                    @block.gpsimd
                    def _(pool):
                        pool.iota(key_no[:], pattern=[[1, KEYS]], base=0, channel_multiplier=0,
                                  allow_small_or_imprecise_dtypes=True)

                found = sbuf("found", [P, TT, 3, lists], mem=route)
                left = sbuf("left", [P, groups, KEYS], mem=route)
                best = sbuf("best", [P, groups, TOPK], mem=route)
                best_no = sbuf("best_no", [P, groups, TOPK], U32, mem=route)
                best_key = sbuf("best_key", [P, groups, TOPK], mem=route)
                sums = sbuf("sums", [P, PEER_HEADS, TOPK, TOPK], mem=route)
                top = sbuf("top", [P, PEER_HEADS, TOPK], mem=route)
                top_no = sbuf("top_no", [P, PEER_HEADS, TOPK], U32, mem=route)
                top_part = sbuf("top_part", [P, 2, PEER_HEADS, TOPK], U32, mem=route)
                top_pos = sbuf("top_pos", [P, 2, PEER_HEADS, TOPK], mem=route)
                gate_sum = sbuf("gate_sum", [P, PEER_HEADS], mem=route)

                with signals("dve_step", "top_ready", "exped", "found_ready", "turned") as (
                        dve_step, top_ready, exped, found_ready, turned), nc.Block() as block:
                    @block.vector
                    def _(dve):
                        step = Chain(dve, dve_step)

                        def best_16(values, n, out, out_no, rest_of):
                            for g in range(n):
                                last = dve.max(out[:, g, 0:8], values(g))
                            step(last)
                            for g in range(n):
                                dve.max_index(out_no[:, g, 0:8], out[:, g, 0:8], values(g))
                                last = dve.match_replace(rest_of(g), out[:, g, 0:8], values(g), -3.0e38)
                            step(last)
                            for g in range(n):
                                last = dve.max(out[:, g, 8:16], rest_of(g))
                            step(last)
                            for g in range(n):
                                last = dve.max_index(out_no[:, g, 8:16], out[:, g, 8:16], rest_of(g))
                            step(last)

                        for t in range(TT):
                            best_16(lambda g: score[:, t, g, :], groups, best, best_no, lambda g: left[:, g, :])
                            step(dve.tensor_copy(best_key[:], best_no[:]))
                            halves_s = best[:].rearrange("p (h a) k -> p h a k", a=2)
                            halves_k = best_key[:].rearrange("p (h a) k -> p h a k", a=2)
                            step(dve.tensor_tensor(sums[:], spread(halves_s[:, :, 0, :], 3, TOPK),
                                                   spread(halves_s[:, :, 1, :], 2, TOPK), ALU.add))
                            flat = sums[:].rearrange("p h a b -> p h (a b)")
                            rest_sums = left[:].rearrange("p (h a) n -> p h (a n)", a=2)
                            best_16(lambda h: flat[:, h, :], PEER_HEADS, top, top_no, lambda h: rest_sums[:, h, :])
                            g = found[:, t, 2, :].rearrange("p (h k) -> p h k", k=TOPK)
                            dve.tensor_tensor(g, top[:], top[:, :, 0:1].broadcast_to([P, PEER_HEADS, TOPK]),
                                              ALU.subtract).then_inc(top_ready, 1)
                            dve.tensor_scalar(top_part[:, 0], top_no[:], 4, None, ALU.logical_shift_right)
                            step(dve.tensor_scalar(top_part[:, 1], top_no[:], 15, None, ALU.bitwise_and))
                            step(dve.tensor_copy(top_pos[:], top_part[:]))
                            for a in range(2):
                                step(dve.tensor_tensor(sums[:], spread(top_pos[:, a], 3, TOPK),
                                                       spread(spread(key_no[:, 0:TOPK], 1, TOPK), 1, PEER_HEADS), ALU.is_equal))
                                step(dve.tensor_tensor(sums[:], sums[:], spread(halves_k[:, :, a, :], 2, TOPK), ALU.mult))
                                step(dve.tensor_reduce(found[:, t, a, :].rearrange("p (h k) -> p h k", k=TOPK), sums[:], AX.X, ALU.add))
                            dve.wait_ge(exped, t + 1)
                            step(dve.tensor_reduce(gate_sum[:], g, AX.X, ALU.add))
                            step(dve.reciprocal(gate_sum[:], gate_sum[:]))
                            dve.tensor_tensor(g, g, spread(gate_sum[:], 2, TOPK), ALU.mult).then_inc(found_ready, 1)

                    @block.scalar
                    def _(act):
                        for t in range(TT):
                            act.wait_ge(top_ready, t + 1)
                            act.activation(found[:, t, 2, :], found[:, t, 2, :], ACT.Exp).then_inc(exped, 1)
                        act.wait_ge(turned, 1)
                        for a in range(3):
                            act.activation(expert[:, a, :], ps[:, a, 0:TOKENS], ACT.Copy)

                    @block.tensor
                    def _(pe):
                        for t in range(TT):
                            pe.wait_ge(found_ready, t + 1)
                            for a in range(3):
                                last = pe.transpose(ps[:, a, t * P:t * P + P], found[:, t, a, :], ident[:])
                        last.then_inc(turned, 1)

            half = KEYS // 2
            with ExitStack() as dense:
                gates = sbuf("gates", [P, half, TOKENS], mem=dense)
                x_parts = [sbuf(n, [P, DK, TOKENS], F32R, mem=dense) for n in ("x_hi", "x_lo")]
                work = hT[:, 0:4, :].rearrange("p (a b) n -> p a b n", a=2)
                for part in range(2):
                    spread_gates(expert, key_no, gates, part * half, x_parts if part == 0 else None)
                    feed_forward("peer", half, ACT.Gelu, scale_by=gates, starts=(part == 0), stops=(part == 1),
                                 x_parts=x_parts, work=work)

            buf_2, p = params("ln2", mem)
            with signals("params_loaded", "var_ready", "rstd_ready", "dve_step") as (
                    params_loaded, var_ready, rstd_ready, dve_step), nc.Block() as block:
                @block.sync
                def _(sp):
                    sp.dma_start(buf_2[:], d["ln2"]).then_inc(params_loaded, 16)

                @block.vector
                def _(dve):
                    step = Chain(dve, dve_step)
                    for t in range(TT):
                        last = dve.tensor_tensor(halves(x[:, t, :]), halves(x[:, t, :]), y_banks(t), ALU.add)
                    step(last)
                    dve.wait_ge(params_loaded, 16)
                    layer_norm(dve, step, x, p["g"], p["b"], x, var_ready, rstd_ready)

                @block.gpsimd
                def _(pool):
                    power(pool, var_ready, rstd_ready)

        def spread_gates(expert, key_no, gates, first, x_parts=None):
            n = gates.shape[1]
            few = 4
            with signals("hot_ready", "placed", "placed_read", "x_hi_ready") as (hot_ready, placed, placed_read, x_hi_ready), \
                    buffer("row_hot", [P, 2, few, KEYS], F32) as row_hot, \
                    buffer("col_hot", [P, 2, few, n], F32) as col_hot, nc.Block() as block:
                steps = TOKENS // few

                def tokens(a, s, i):
                    if i is None:
                        return expert[:, a, s * few:s * few + few]
                    return expert[:, a, bass.ds(i * 4 * few + s * few, few)]

                def count(s, i):
                    return s if i is None else i * 4 + s

                @block.vector
                def _(dve):
                    def hot(s, i=None):
                        if i is not None or s >= 2:
                            dve.wait_ge(placed, count(s - 1, i))
                        dve.tensor_tensor(row_hot[:, s % 2], spread(key_no[:, :], 1, few), spread(tokens(0, s, i), 2, KEYS),
                                          ALU.is_equal)
                        second, gate = tokens(1, s, i), tokens(2, s, i)
                        for m in range(few):
                            last = dve.tensor_scalar(col_hot[:, s % 2, m, :], key_no[:, first:first + n], second[:, m:m + 1],
                                                     gate[:, m:m + 1], ALU.is_equal, ALU.mult)
                        last.then_inc(hot_ready, 1)

                    for s in range(4):
                        hot(s)
                    if x_parts is not None:
                        dve.tensor_copy(x_parts[0][:], hT[:]).then_inc(x_hi_ready, 1)
                        dve.wait_ge(x_hi_ready, 1)
                        dve.tensor_tensor(x_parts[1][:], hT[:], x_parts[0][:], ALU.subtract)
                    with dve.Fori(1, steps // 4) as i:
                        for s in range(4):
                            hot(s, i)

                @block.tensor
                def _(pe):
                    def place(s, i=None):
                        pe.wait_ge(hot_ready, count(s + 1, i))
                        if i is not None:
                            pe.wait_ge(placed_read, count(s - 3, i))
                        for m in range(few):
                            last = pe.matmul(ps[:, s % 4, m * n:m * n + n], row_hot[:, s % 2, m, :], col_hot[:, s % 2, m, :],
                                             start=True, stop=True)
                        last.then_inc(placed, 1)

                    for s in range(4):
                        place(s)
                    with pe.Fori(1, steps // 4) as i:
                        for s in range(4):
                            place(s, i)

                @block.scalar
                def _(act):
                    def read(s, i=None):
                        act.wait_ge(placed, count(s + 1, i))
                        to = gates[:, :, s * few:s * few + few] if i is None else gates[:, :, bass.ds(i * 4 * few + s * few, few)]
                        act.activation(to.rearrange("p j m -> p m j"), ps[:, s % 4, 0:few * n].rearrange("p (m j) -> p m j", m=few),
                                       ACT.Copy).then_inc(placed_read, 1)

                    for s in range(4):
                        read(s)
                    with act.Fori(1, steps // 4) as i:
                        for s in range(4):
                            read(s, i)


        def post_norm(g, params_loaded=None, mixer=None):
            with signals("n_ready", "n_read", "squared", "var_ready", "rstd_ready", "dve_step") as (
                    n_ready, n_read, squared, var_ready, rstd_ready, dve_step), \
                    buffer("scaled_y", [P, D]) as scaled_y, buffer("junk", [P, TT, D]) as junk, nc.Block() as block:
                if mixer is not None:
                    @block.sync
                    def _(sp):
                        stream.feed(sp, 2)

                    @block.tensor
                    def _(pe):
                        for at in range(2):
                            product_n(pe, mixer, at, n_ready, n_read)

                @block.scalar
                def _(act):
                    if mixer is not None:
                        act.wait_ge(n_ready, 2)
                    for t in range(TT):
                        last = act.activation(halves(junk[:, t, :]), y_banks(t), ACT.Square, accum_out=squares[:, t:t + 1])
                    last.then_inc(squared, 1)

                @block.vector
                def _(dve):
                    step = Chain(dve, dve_step)
                    dve.wait_ge(squared, 1)
                    dve.tensor_scalar(spare[:], squares[:], 1.0 / D, RMS_EPS, ALU.mult, ALU.add).then_inc(var_ready, 1)
                    dve.wait_ge(rstd_ready, 1)
                    for t in range(TT):
                        step(dve.scalar_tensor_tensor(halves(scaled_y[:]), y_banks(t), rstd[:, t:t + 1], halves(g), ALU.mult, ALU.mult))
                        step(dve.tensor_tensor(x[:, t, :], x[:, t, :], scaled_y[:], ALU.add))

                @block.gpsimd
                def _(pool):
                    power(pool, var_ready, rstd_ready)

        def nsa(mem):
            buf, p = params("nsa", mem)
            pre_norm(lambda b: col("norm_g", b))

            with ExitStack() as mix:
                n_rope = 14
                qk = sbuf("qk", [P, n_rope, TOKENS], mem=mix)
                v_cmp_t = sbuf("v_cmp_t", [P, 2, TOKENS], mem=mix)
                v_tok = sbuf("v_tok", [P, TT, 2, GROUPS, HD], mem=mix)
                branch = sbuf("branch", [P, TT, 16, 3], mem=mix)

                rot = sbuf("rot", [P, P], mem=mix)
                shift = sbuf("shift", [P, TOKENS], mem=mix)
                cmp_mask = sbuf("cmp_mask", [P, TT, N_CMP], mem=mix)
                cmp_seen = sbuf("cmp_seen", [P, TT], mem=mix)
                own_head = sbuf("own_head", [P, 8], mem=mix)

                with signals("params_loaded", "t_ready", "t_read", "n_ready", "n_read", "gates_copied", "pool_step") as (
                        params_loaded, t_ready, t_read, n_ready, n_read, gates_copied, pool_step), nc.Block() as block:
                    @block.sync
                    def _(sp):
                        sp.dma_start(buf[:], d["nsa"]).then_inc(params_loaded, 16)
                        stream.feed(sp, 6)
                        sp.wait_ge(params_loaded, 16)

                    @block.tensor
                    def _(pe):
                        at = 0
                        for _ in range(4):
                            at = product_t(pe, hT, ALL_T, at, t_ready, t_read)
                        for n in range(2):
                            product_n(pe, hT, n, n_ready, n_read)

                    @block.scalar
                    def _(act):
                        for at in range(16):
                            out = qk[:, at, :] if at < n_rope else v_cmp_t[:, at - n_rope, :]
                            act.wait_ge(t_ready, at + 1)
                            act.activation(out, ps[:, at % 4, 0:TOKENS], ACT.Copy).then_inc(t_read, 1)
                        act.wait_ge(gates_copied, 1)
                        act.activation(branch[:], branch[:], ACT.Sigmoid)

                    @block.vector
                    def _(dve):
                        dve.wait_ge(n_ready, 1)
                        dve.tensor_copy(v_tok[:].rearrange("p t a g n -> p t (a g n)"), bank_n(0)).then_inc(n_read, 1)
                        dve.wait_ge(n_ready, 2)
                        dve.tensor_copy(branch[:].rearrange("p t h a -> p t (h a)"), bank_n(1, 48)).then_inc(gates_copied, 1)

                    @block.gpsimd
                    def _(pool):
                        step = Chain(pool, pool_step)
                        pool.memset(rot[:], 0.0)
                        pool.memset(shift[:], 0.0)
                        pool.memset(cmp_mask[:], 0.0)
                        pool.memset(cmp_seen[:], 1.0)
                        step(pool.memset(own_head[:], 1.0))
                        r = rot[:].rearrange("p (h a n) -> p h a n", h=2, a=2)
                        for a, sign in ((0, -1.0), (1, 1.0)):
                            pool.affine_select(out=r[:, :, a, :], in_=r[:, :, a, :], compare_op=ALU.not_equal, fill=sign,
                                               base=-32 * (1 - a), pattern=[[-HD, 2], [-1, 32]], channel_multiplier=1)
                        pool.affine_select(out=shift[:], in_=shift[:], compare_op=ALU.not_equal, fill=1.0, base=HD,
                                           pattern=[[-1, TOKENS]], channel_multiplier=1)
                        pool.affine_select(out=cmp_mask[:], in_=cmp_mask[:], compare_op=ALU.is_ge, fill=NEG, base=1 - CMP_LEN,
                                           pattern=[[P, TT], [-CMP_STRIDE, N_CMP]], channel_multiplier=1)
                        pool.affine_select(out=cmp_seen[:], in_=cmp_seen[:], compare_op=ALU.is_ge, fill=0.0, base=1 - CMP_LEN,
                                           pattern=[[P, TT]], channel_multiplier=1)
                        step(pool.affine_select(out=own_head[:], in_=own_head[:], compare_op=ALU.is_ge, fill=0.0, base=0,
                                                pattern=[[-N_CMP, 8]], channel_multiplier=1))
                        pool.affine_select(out=own_head[:], in_=own_head[:], compare_op=ALU.is_ge, fill=0.0, base=N_CMP - 1,
                                           pattern=[[N_CMP, 8]], channel_multiplier=-1)

                with signals("rotated", "with_sin", "with_cos", "rotated_read") as (rotated, with_sin, with_cos, rotated_read), \
                        buffer("part_sin", [P, 2, 2, TOKENS]) as part_sin, nc.Block() as block:
                    pairs = n_rope // 2

                    @block.tensor
                    def _(pe):
                        for n in range(pairs):
                            if n >= 4:
                                pe.wait_ge(with_sin, n - 3)
                            for b in range(2):
                                last = pe.matmul(ps[:, n % 4, b * TOKENS:b * TOKENS + TOKENS], rot[:], qk[:, 2 * n + b, :],
                                                 start=True, stop=True)
                            last.then_inc(rotated, 1)

                    @block.vector
                    def _(dve):
                        for n in range(pairs):
                            dve.wait_ge(rotated, n + 1)
                            if n >= 2:
                                dve.wait_ge(with_cos, 2 * (n - 1))
                            dve.tensor_tensor(part_sin[:, n % 2], ps[:, n % 4, :].rearrange("p (b n) -> p b n", b=2),
                                              spread(p["sin"], 1, 2), ALU.mult).then_inc(with_sin, 1)

                    @block.gpsimd
                    def _(pool):
                        for n in range(pairs):
                            o = qk[:, 2 * n:2 * n + 2, :]
                            pool.wait_ge(with_sin, n + 1)
                            pool.tensor_tensor(o, o, spread(p["cos"], 1, 2), ALU.mult).then_inc(with_cos, 1)
                            pool.wait_ge(with_cos, 2 * n + 1)
                            pool.tensor_tensor(o, o, part_sin[:, n % 2], ALU.add).then_inc(with_cos, 1)

                cmp = mix.enter_context(ExitStack())
                kv_pairs = sbuf("kv_pairs", [P, 2, GROUPS, P], mem=cmp)
                pos_part = sbuf("pos_part", [P, 2, 2], mem=cmp)
                hid = sbuf("hid", [P, 2, 2, GROUPS, N_CMP], mem=cmp)
                hid_heads = sbuf("hid_heads", [P, 2, 16, N_CMP], mem=cmp)
                k_cmp = sbuf("k_cmp", [P, GROUPS, N_CMP], mem=cmp)
                v_cmp = sbuf("v_cmp", [P, 2, 8, HD], mem=cmp)
                rows = 8 * N_CMP
                w2k = p["w2k"].rearrange("p (a n) -> p a n", a=2)
                w2v = p["w2v"].rearrange("p (a n) -> p a n", a=2)

                with signals("paired", "pairs_copied", "hid_ready", "pos_copied", "hid_done", "hid_spread", "k_ready", "v_ready") as (
                        paired, pairs_copied, hid_ready, pos_copied, hid_done, hid_spread, k_ready, v_ready), nc.Block() as block:
                    @block.sync
                    def _(sp):
                        stream.feed(sp, 2)

                    @block.tensor
                    def _(pe):
                        for a in range(2):
                            for g in range(GROUPS):
                                half = g % 2
                                lanes = slice(half * HD, half * HD + HD)
                                src = qk[lanes, 8 + g // 2, :] if a == 0 else v_cmp_t[lanes, g // 2, :]
                                for parity in range(2):
                                    s = HD * (half + 1 - parity)
                                    last = pe.matmul(ps[:, a + 6 * half, g // 2 * P:g // 2 * P + P], shift[lanes, s:s + P],
                                                     src.rearrange("p (j a) -> p a j", a=2)[:, parity, :],
                                                     start=(parity == 0), stop=(parity == 1))
                            last.then_inc(paired, 1)
                        for a in range(2):
                            c = stream.take(pe)
                            w = stream.slot(c)
                            pe.wait_ge(pairs_copied, a + 1)
                            for n in range(2):
                                bank = 2 + 2 * a + n
                                for k in range(16):
                                    last = pe.matmul(ps[:, bank, 0:GROUPS * N_CMP], w[:, k * 256 + n * P:k * 256 + n * P + P],
                                                     kv_pairs[:, a, :, k:k + 8 * N_CMP - 7:8], start=(k == 0), stop=(k == 15))
                                    if n + k == 0:
                                        stream.release(last)
                                for k in range(16):
                                    last = pe.matmul(ps[:, bank, 64:65], w[:, k * 256 + n * P:k * 256 + n * P + P],
                                                     col("pos_k" if a == 0 else "pos_v", k), start=(k == 0), stop=(k == 15))
                                last.then_inc(hid_ready, 1)
                            stream.pending = True
                        pe.wait_ge(hid_done, 2)
                        for n in range(2):
                            last = pe.matmul(ps[:, 6, 0:GROUPS * N_CMP], w2k[:, n, :], hid[:, 0, n].rearrange("p g c -> p (g c)"),
                                             start=(n == 0), stop=(n == 1))
                        last.then_inc(k_ready, 1)
                        pe.wait_ge(hid_spread, 1)
                        for b in range(2):
                            for n in range(2):
                                last = pe.matmul(ps[0:rows, 7, b * HD:b * HD + HD],
                                                 hid_heads[:, n, 8 * b:8 * b + 8, :].rearrange("p h c -> p (h c)"), w2v[:, n, :],
                                                 start=(n == 0), stop=(n == 1))
                        last.then_inc(v_ready, 1)

                    @block.scalar
                    def _(act):
                        for a in range(2):
                            act.wait_ge(paired, a + 1)
                            for half in range(2):
                                last = act.activation(kv_pairs[:, a].rearrange("p (g b) j -> p b g j", b=2)[:, half],
                                                      ps[:, a + 6 * half, 0:2 * P].rearrange("p (g j) -> p g j", g=2), ACT.Copy)
                            last.then_inc(pairs_copied, 1)
                        for a in range(2):
                            for n in range(2):
                                bank = 2 + 2 * a + n
                                act.wait_ge(hid_ready, 2 * a + n + 1)
                                act.activation(pos_part[:, a, n:n + 1], ps[:, bank, 64:65], ACT.Copy).then_inc(pos_copied, 1)
                                act.wait_ge(pos_copied, 2 * a + n + 1)
                                act.activation(hid[:, a, n], ps[:, bank, 0:GROUPS * N_CMP].rearrange("p (g c) -> p g c", g=GROUPS),
                                               ACT.Silu, bias=pos_part[:, a, n:n + 1]).then_inc(hid_done, 1)
                        act.wait_ge(k_ready, 1)
                        act.activation(k_cmp[:], ps[:, 6, 0:GROUPS * N_CMP].rearrange("p (g c) -> p g c", g=GROUPS), ACT.Copy)

                    @block.vector
                    def _(dve):
                        dve.wait_ge(hid_done, 4)
                        for n in range(2):
                            last = dve.tensor_copy(hid_heads[:, n].rearrange("p (g r) c -> p g r c", g=GROUPS),
                                                   spread(hid[:, 1, n], 2, REP))
                        last.then_inc(hid_spread, 1)
                        dve.wait_ge(v_ready, 1)
                        for b in range(2):
                            dve.tensor_tensor(v_cmp[0:rows, b], spread(ps[0:rows, 7, b * HD:b * HD + HD], 1, 8),
                                              spread(own_head[0:rows, :], 2, HD), ALU.mult)

                def q_of(h, t0, t1):
                    g, r = h // REP, h % REP
                    half = g % 2 * HD
                    return qk[half:half + HD, (g // 2) * REP + r, t0:t1]

                with signals("scored", "biased", "exped", "probs_ready", "turned", "turned_copied", "dve_step") as (
                        scored, biased, exped, probs_ready, turned, turned_copied, dve_step), \
                        buffer("prob_cmp", [P, TT, 16, N_CMP]) as prob, buffer("prob_cmp_t", [P, TT, 2, P]) as prob_t, \
                        buffer("cmp_top", [P, TT, 16]) as cmp_top, nc.Block() as block:
                    @block.tensor
                    def _(pe):
                        for t in range(TT):
                            for h in range(16):
                                g = h // REP
                                half = g % 2
                                at = (g // 2 * REP + h % REP) * N_CMP
                                last = pe.matmul(ps[:, t + 2 * half, at:at + N_CMP], q_of(h, t * P, t * P + P),
                                                 k_cmp[half * HD:half * HD + HD, g, :], start=True, stop=True)
                            last.then_inc(scored, 1)
                        for t in range(TT):
                            pe.wait_ge(probs_ready, t + 1)
                            for b in range(2):
                                last = pe.transpose(ps[0:rows, 2 + t, b * P:b * P + P],
                                                    prob[:, t, 8 * b:8 * b + 8, :].rearrange("p h c -> p (h c)"), ident[:])
                            last.then_inc(turned, 1)
                        for t in range(TT):
                            pe.wait_ge(turned_copied, t + 1)
                            for b in range(2):
                                pe.matmul(ps[:, 4 + 2 * b + t, :], prob_t[0:rows, t, b, :],
                                          v_cmp[0:rows, b].rearrange("p h n -> p (h n)"), start=True, stop=False,
                                          skip_group_check=True)

                    @block.vector
                    def _(dve):
                        step = Chain(dve, dve_step)
                        for t in range(TT):
                            o = prob[:, t]
                            dve.wait_ge(scored, t + 1)
                            for g in range(GROUPS):
                                at = g // 2 * REP * N_CMP
                                last = dve.scalar_tensor_tensor(
                                    o[:, g * REP:g * REP + REP, :],
                                    ps[:, t + 2 * (g % 2), at:at + REP * N_CMP].rearrange("p (h c) -> p h c", h=REP), HD ** -0.5,
                                    spread(cmp_mask[:, t, :], 1, REP), ALU.mult, ALU.add)
                            step(last)
                            step(dve.tensor_reduce(cmp_top[:, t, :], o, AX.X, ALU.max))
                            dve.tensor_tensor(o, o, spread(cmp_top[:, t, :], 2, N_CMP), ALU.subtract).then_inc(biased, 1)
                        for t in range(TT):
                            o = prob[:, t]
                            dve.wait_ge(exped, t + 1)
                            step(dve.tensor_reduce(cmp_top[:, t, :], o, AX.X, ALU.add))
                            step(dve.reciprocal(cmp_top[:, t, :], cmp_top[:, t, :]))
                            step(dve.scalar_tensor_tensor(cmp_top[:, t, :], cmp_top[:, t, :], cmp_seen[:, t:t + 1], branch[:, t, :, 0],
                                                          ALU.mult, ALU.mult))
                            dve.tensor_tensor(o, o, spread(cmp_top[:, t, :], 2, N_CMP), ALU.mult).then_inc(probs_ready, 1)

                    @block.scalar
                    def _(act):
                        for t in range(TT):
                            act.wait_ge(biased, t + 1)
                            act.activation(prob[:, t], prob[:, t], ACT.Exp).then_inc(exped, 1)
                        for t in range(TT):
                            act.wait_ge(turned, t + 1)
                            act.activation(prob_t[0:rows, t], ps[0:rows, 2 + t, 0:2 * P].rearrange("p (b n) -> p b n", b=2),
                                           ACT.Copy).then_inc(turned_copied, 1)

                def scores(pe, i):
                    h, a = i // 2, i % 2
                    half = h // REP % 2 * HD
                    k = qk[half:half + HD, 10 + 2 * a + h // REP // 2, :]
                    pe.matmul(ps[:, i % 2, 0:P], q_of(h, 0, P), k[:, 0:P], start=True, stop=True)
                    return pe.matmul(ps[:, i % 2, P:TRI], q_of(h, P, TOKENS), k, start=True, stop=True)

                def logits(dve, step, i, out):
                    return dve.scalar_tensor_tensor(out, ps[:, i % 2, 0:TRI], HD ** -0.5, mask[:], ALU.mult, ALU.add)

                attention(32, scores, logits, lambda i, s: v_tok[:, s, i % 2, i // 2 // REP, :],
                          lambda i, t: ps[:, 4 + 2 * (i // 16) + t, i // 2 % 8 * HD:i // 2 % 8 * HD + HD],
                          gate=lambda i: branch[:, :, i // 2, 1 + i % 2], starts=False)
                o = sbuf("o", [P, TT, D], mem=mix)
                oT = sbuf("oT", [P, DK, TOKENS], mem=mix)
                turn_heads(o, oT)
                post_norm(p["post1"], mixer=oT)

            pre_norm(lambda b: col("norm_g", DK + b))
            feed_forward("relu2", MLP_TILES, ACT.Relu)
            post_norm(p["post2"])

        def fox(mem):
            buf, p = params("fox", mem)
            pre_norm(lambda b: col("norm_g", 2 * DK + b))
            with ExitStack() as mix:
                qT = sbuf("qT", [P, DK, TOKENS], mem=mix)
                kT = sbuf("kT", [P, DK, TOKENS], mem=mix)
                v = sbuf("v", [P, TT, D], mem=mix)
                forget = sbuf("forget", [HEADS_B, 3, TOKENS], mem=mix)
                decay = sbuf("decay", [P, TT, HEADS_B], mem=mix)
                pick = sbuf("pick", [HEADS_B, HEADS_B, P], mem=mix)

                with signals("params_loaded", "t_ready", "t_read", "n_ready", "n_read", "act_step", "dve_step", "summed",
                             "turned", "pool_step") as (params_loaded, t_ready, t_read, n_ready, n_read, act_step, dve_step,
                                                        summed, turned, pool_step), nc.Block() as block:
                    @block.sync
                    def _(sp):
                        sp.dma_start(buf[:], d["fox"]).then_inc(params_loaded, 16)
                        stream.feed(sp, 7)
                        sp.wait_ge(params_loaded, 16)

                    @block.tensor
                    def _(pe):
                        at = 0
                        for _ in range(4):
                            at = product_t(pe, hT, ALL_T, at, t_ready, t_read)
                        for n in range(2):
                            product_n(pe, hT, n, n_ready, n_read)
                        product_t(pe, hT, [(0, HEADS_B)], at, t_ready, t_read)
                        pe.wait_ge(summed, 1)
                        for t in range(TT):
                            last = pe.transpose(ps[:, 1, t * HEADS_B:t * HEADS_B + HEADS_B], forget[:, 2, t * P:t * P + P],
                                                ident[0:HEADS_B, 0:HEADS_B])
                        last.then_inc(turned, 1)

                    @block.scalar
                    def _(act):
                        for at in range(16):
                            out = qT[:, at, :] if at < DK else kT[:, at - DK, :]
                            act.wait_ge(t_ready, at + 1)
                            act.activation(out, ps[:, at % 4, 0:TOKENS], ACT.Copy,
                                           scale=HD ** -0.5 if at < DK else 1.0).then_inc(t_read, 1)
                        act.wait_ge(act_step, 1)
                        act.activation(forget[:, 1], forget[:, 1], ACT.Exp, scale=-1.0).then_inc(act_step, 1)
                        act.wait_ge(act_step, 2)
                        act.activation(forget[:, 1], forget[:, 1], ACT.Ln, bias=1.0).then_inc(act_step, 1)
                        act.wait_ge(turned, 1)
                        act.activation(decay[:], ps[:, 1, 0:TT * HEADS_B].rearrange("p (t h) -> p t h", t=TT), ACT.Copy)

                    @block.vector
                    def _(dve):
                        step = Chain(dve, dve_step)
                        for n in range(2):
                            dve.wait_ge(n_ready, n + 1)
                            dve.tensor_copy(v[:, :, n * WIDE:n * WIDE + WIDE], bank_n(n)).then_inc(n_read, 1)
                        dve.wait_ge(t_ready, 17)
                        step(dve.tensor_scalar(forget[:, 0], ps[0:HEADS_B, 0, 0:TOKENS], col("b_f", rows=HEADS_B), None, ALU.add))
                        dve.scalar_tensor_tensor(forget[:, 1], forget[:, 0], -1.0, forget[:, 0], ALU.mult, ALU.max).then_inc(act_step, 1)
                        dve.wait_ge(act_step, 3)
                        step(dve.scalar_tensor_tensor(forget[:, 0], forget[:, 0], 0.0, forget[:, 1], ALU.min, ALU.subtract))
                        dve.tensor_tensor_scan(forget[:, 2], ones[0:HEADS_B, :], forget[:, 0], 0.0, ALU.mult, ALU.add).then_inc(summed, 1)

                    @block.gpsimd
                    def _(pool):
                        step = Chain(pool, pool_step)
                        step(pool.memset(pick[:], 0.0))
                        pool.affine_select(out=pick[:], in_=pick[:], compare_op=ALU.not_equal, fill=-1.0, base=0,
                                           pattern=[[-1, HEADS_B], [0, P]], channel_multiplier=1)

                key_decay = sbuf("key_decay", [P, HEADS_B, TOKENS], mem=mix)
                with signals("repeated", "repeated_read") as (repeated, repeated_read), nc.Block() as block:
                    @block.tensor
                    def _(pe):
                        for n in range(HEADS_B // 2):
                            if n >= 4:
                                pe.wait_ge(repeated_read, n - 3)
                            for b in range(2):
                                last = pe.matmul(ps[:, n % 4, b * TOKENS:b * TOKENS + TOKENS], pick[:, 2 * n + b, :], forget[:, 2, :],
                                                 start=True, stop=True)
                            last.then_inc(repeated, 1)

                    @block.scalar
                    def _(act):
                        for n in range(HEADS_B // 2):
                            act.wait_ge(repeated, n + 1)
                            act.activation(key_decay[:, 2 * n:2 * n + 2, :], ps[:, n % 4, :].rearrange("p (b n) -> p b n", b=2),
                                           ACT.Copy).then_inc(repeated_read, 1)

                def scores(pe, h):
                    half = slice(h % 2 * HD, h % 2 * HD + HD)
                    pe.matmul(ps[:, h % 2, 0:P], qT[half, h // 2, 0:P], kT[half, h // 2, 0:P], start=True, stop=True)
                    return pe.matmul(ps[:, h % 2, P:TRI], qT[half, h // 2, P:TOKENS], kT[half, h // 2, :], start=True, stop=True)

                def logits(dve, step, h, out):
                    for t, o, n in ((0, 0, P), (1, P, TOKENS)):
                        last = dve.scalar_tensor_tensor(out[:, o:o + n], ps[:, h % 2, o:o + n], decay[:, t, h:h + 1],
                                                        key_decay[:, h, 0:n], ALU.add, ALU.add)
                    step(last)
                    return dve.tensor_tensor(out, out, mask[:], ALU.add)

                attention(HEADS_B, scores, logits, lambda h, s: v[:, s, h * HD:h * HD + HD],
                          lambda h, t: ps[:, 4 + 2 * (h // 8) + t, h % 8 * HD:h % 8 * HD + HD])
                oT = kT
                turn_heads(v, oT)
                post_norm(p["post1"], mixer=oT)

            pre_norm(lambda b: col("norm_g", 3 * DK + b))
            feed_forward("relu2", MLP_TILES, ACT.Relu)
            post_norm(p["post2"])


        def add_gated(gate, mixer=None):
            with signals("n_ready", "n_read", "dve_step") as (n_ready, n_read, dve_step), \
                    buffer("gated_y", [P, TT, D]) as gated_y, nc.Block() as block:
                if mixer is not None:
                    @block.sync
                    def _(sp):
                        stream.feed(sp, 2)

                    @block.tensor
                    def _(pe):
                        for at in range(2):
                            product_n(pe, mixer, at, n_ready, n_read)

                @block.vector
                def _(dve):
                    step = Chain(dve, dve_step)
                    if mixer is not None:
                        dve.wait_ge(n_ready, 2)
                    for t in range(TT):
                        last = dve.tensor_tensor(halves(gated_y[:, t, :]), y_banks(t), halves(gate), ALU.mult)
                    step(last)
                    dve.tensor_tensor(x[:], x[:], gated_y[:], ALU.add)

        def modulation(p, gain):
            with signals("cond_ready", "cond_spread", "n_ready", "n_read", "turned", "dve_step") as (
                    cond_ready, cond_spread, n_ready, n_read, turned, dve_step), \
                    buffer("cond", [P, DK]) as cond, buffer("cond_all", [P, DK, P]) as cond_all, \
                    buffer("mod_row", [1, 8, D]) as mod_row, nc.Block() as block:
                chunks = 24

                @block.sync
                def _(sp):
                    stream.feed(sp, chunks)

                @block.scalar
                def _(act):
                    act.activation(cond[:], cols[:, offsets["cols"]["cond"][0]:][:, 0:DK], ACT.Silu).then_inc(cond_ready, 1)

                @block.tensor
                def _(pe):
                    pe.wait_ge(cond_spread, 1)
                    for at in range(chunks):
                        product_n(pe, cond_all, at, n_ready, n_read, tiles=1)
                    pe.wait_ge(n_read, chunks)
                    for n in range(8 * DK):
                        last = pe.matmul(ps[:, 0, n:n + 1], mod_row[0:1, n // DK, n % DK * P:n % DK * P + P], ones[0:1, 0:1],
                                         start=True, stop=True)
                    last.then_inc(turned, 1)

                @block.vector
                def _(dve):
                    step = Chain(dve, dve_step)
                    dve.wait_ge(cond_ready, 1)
                    dve.tensor_copy(cond_all[:], spread(cond[:], 2, P)).then_inc(cond_spread, 1)
                    for at in range(chunks):
                        layer, piece, half = at // 12, at % 12 // 2, at % 2
                        o = slice(half * WIDE, half * WIDE + WIDE)
                        bank = 4 + 2 * (at % 2)
                        dve.wait_ge(n_ready, at + 1)
                        if piece in (2, 5):
                            g = p["gates"][:, (2 * layer + piece // 3) * D:][:, o]
                            dve.tensor_tensor(g, g, ps[:, bank, :], ALU.add).then_inc(n_read, 1)
                        else:
                            dve.tensor_copy(mod_row[0:1, 4 * layer + piece - piece // 3, o], ps[0:1, bank, :]).then_inc(n_read, 1)
                    dve.wait_ge(turned, 1)
                    step(dve.tensor_tensor(p["shifts"], p["shifts"], ps[:, 0, 0:8 * DK], ALU.add))
                    o, n = offsets["cols"]["norm_w"]
                    pairs = p["shifts"].rearrange("p (n a k) -> p n a k", a=2, k=DK)
                    dve.scalar_tensor_tensor(gain[:], pairs[:, :, 1, :], 1.0, cols[:, o:o + n].rearrange("p (n k) -> p n k", k=DK),
                                             ALU.add, ALU.mult)

        def head_norm(o, gate, norm_w, oT):
            with signals("copied", "squared", "var_ready", "rstd_ready", "weighed", "normed", "turned", "turned_read", "dve_step") as (
                    copied, squared, var_ready, rstd_ready, weighed, normed, turned, turned_read, dve_step), \
                    buffer("square", [P, TT, D]) as square, buffer("head_var", [P, TT, HEADS_C]) as head_var, nc.Block() as block:
                @block.scalar
                def _(act):
                    for t in range(TT):
                        act.activation(halves(square[:, t, :]), y_banks(t), ACT.Square).then_inc(squared, 1)
                    copy_turned(act, oT, turned, turned_read)

                @block.vector
                def _(dve):
                    step = Chain(dve, dve_step)
                    heads = lambda a: a.rearrange("p t (h n) -> p t h n", h=HEADS_C)
                    for t in range(TT):
                        dve.wait_ge(squared, t + 1)
                        last = dve.tensor_reduce(head_var[:, t, :], square[:, t, :].rearrange("p (h n) -> p h n", h=HEADS_C), AX.X, ALU.add)
                    step(last)
                    dve.tensor_scalar(head_var[:], head_var[:], 1.0 / P, RMS_EPS, ALU.mult, ALU.add).then_inc(var_ready, 1)
                    dve.wait_ge(weighed, 1)
                    for t in range(TT):
                        last = dve.tensor_tensor(halves(o[:, t, :]), y_banks(t), halves(gate[:, t, :]), ALU.mult)
                    step(last)
                    dve.wait_ge(rstd_ready, 1)
                    dve.tensor_tensor(heads(o[:]), heads(o[:]), spread(head_var[:], 3, P), ALU.mult).then_inc(normed, 1)

                @block.gpsimd
                def _(pool):
                    pool.tensor_tensor(gate[:], gate[:], spread(norm_w, 1, TT), ALU.mult).then_inc(weighed, 1)
                    pool.wait_ge(var_ready, 1)
                    v = head_var[:].rearrange("p t h -> p (t h)")
                    pool.tensor_tensor(v, v, minus_half[:, 0:TT * HEADS_C], ALU.pow).then_inc(rstd_ready, 1)

                @block.tensor
                def _(pe):
                    pe.wait_ge(normed, 1)
                    transposes(pe, o, turned, turned_read)

        def mlstm(mem):
            buf, p = params("mlstm", mem)
            qkT = sbuf("qkT", [P, DK, TOKENS], mem=mem)
            v = sbuf("v", [P, TT, D], mem=mem)
            out_gate = sbuf("out_gate", [P, TT, D], mem=mem)
            lanes = slice(0, HEADS_C)
            gate_t = sbuf("gate_t", [HEADS_C, 5, TOKENS], mem=mem)
            decay = sbuf("decay", [P, TT, HEADS_C], mem=mem)
            key_gate = sbuf("key_gate", [P, HEADS_C, TOKENS], mem=mem)
            pick = sbuf("pick", [HEADS_C, HEADS_C, P], mem=mem)
            before = 3
            with ExitStack() as conv, signals(
                    "params_loaded", "t_ready", "t_read", "n_ready", "n_read", "dve_step", "pad_ready", "convolved", "o_copied",
                    "act_step", "summed", "turned", "pool_step", "pick_ready", "repeated", "repeated_read") as (
                    params_loaded, t_ready, t_read, n_ready, n_read, dve_step, pad_ready, convolved, o_copied,
                    act_step, summed, turned, pool_step, pick_ready, repeated, repeated_read):
                raw = sbuf("raw", [P, DK, before + TOKENS], mem=conv)
                block = conv.enter_context(nc.Block())

                @block.sync
                def _(sp):
                    sp.dma_start(buf[:], d["mlstm"]).then_inc(params_loaded, 16)
                    stream.feed(sp, 7)
                    sp.wait_ge(params_loaded, 16)

                @block.tensor
                def _(pe):
                    at = 0
                    for _ in range(2):
                        at = product_t(pe, hT, ALL_T, at, t_ready, t_read)
                    for n in range(4):
                        product_n(pe, hT, n, n_ready, n_read)
                    product_t(pe, hT, [(0, HEADS_C), (HEADS_C, HEADS_C)], at, t_ready, t_read)
                    pe.wait_ge(summed, 1)
                    for t in range(TT):
                        last = pe.transpose(ps[:, 2, t * HEADS_C:t * HEADS_C + HEADS_C], gate_t[:, 3, t * P:t * P + P], ident[lanes, lanes])
                    last.then_inc(turned, 1)
                    pe.wait_ge(summed, 2)
                    pe.wait_ge(pick_ready, 1)
                    for n in range(HEADS_C // 2):
                        bank = (3, 0, 1, 3)[n]
                        if n == 3:
                            pe.wait_ge(repeated_read, 1)
                        for b in range(2):
                            last = pe.matmul(ps[:, bank, b * TOKENS:b * TOKENS + TOKENS], pick[:, 2 * n + b, :], gate_t[:, 4, :],
                                             start=True, stop=True)
                        last.then_inc(repeated, 1)

                @block.scalar
                def _(act):
                    act.wait_ge(pad_ready, 1)
                    for b in range(DK):
                        act.wait_ge(t_ready, b + 1)
                        act.activation(raw[:, b, before:], ps[:, b % 4, 0:TOKENS], ACT.Copy).then_inc(t_read, 1)
                    for b in range(DK):
                        act.wait_ge(convolved, b + 1)
                        act.activation(qkT[:, b, :], qkT[:, b, :], ACT.Silu, bias=col("conv_b", b))
                    act.wait_ge(o_copied, 2)
                    act.activation(out_gate[:], out_gate[:], ACT.Sigmoid)
                    act.wait_ge(act_step, 1)
                    act.activation(gate_t[:, 0], gate_t[:, 0], ACT.Tanh, scale=1.0 / IGATE_CAP).then_inc(act_step, 1)
                    act.activation(gate_t[:, 2], gate_t[:, 2], ACT.Exp, scale=-1.0).then_inc(act_step, 1)
                    act.wait_ge(act_step, 3)
                    act.activation(gate_t[:, 2], gate_t[:, 2], ACT.Ln, bias=1.0).then_inc(act_step, 1)
                    act.wait_ge(turned, 1)
                    act.activation(decay[:], ps[:, 2, 0:TT * HEADS_C].rearrange("p (t h) -> p t h", t=TT), ACT.Copy)
                    for n in range(HEADS_C // 2):
                        act.wait_ge(repeated, n + 1)
                        act.activation(key_gate[:, 2 * n:2 * n + 2, :], ps[:, (3, 0, 1, 3)[n], :].rearrange("p (b n) -> p b n", b=2),
                                       ACT.Copy).then_inc(repeated_read, 1)

                @block.vector
                def _(dve):
                    step = Chain(dve, dve_step)
                    dve.memset(raw[:, :, 0:before], 0.0).then_inc(pad_ready, 1)
                    dve.wait_ge(pad_ready, 1)
                    for b in range(DK):
                        dve.wait_ge(t_read, b + 1)
                        step(dve.tensor_scalar(qkT[:, b, :], raw[:, b, 0:TOKENS], col("conv_w", 4 * b), None, ALU.mult))
                        for j in range(1, 4):
                            last = dve.scalar_tensor_tensor(qkT[:, b, :], raw[:, b, j:j + TOKENS], col("conv_w", 4 * b + j), qkT[:, b, :],
                                                            ALU.mult, ALU.add)
                            if j < 3:
                                step(last)
                        last.then_inc(convolved, 1)
                    for n in range(4):
                        out = v if n < 2 else out_gate
                        dve.wait_ge(n_ready, n + 1)
                        dve.tensor_copy(out[:, :, n % 2 * WIDE:n % 2 * WIDE + WIDE], bank_n(n)).then_inc(n_read, 1)
                        if n >= 2:
                            dve.wait_ge(n_read, n + 1)
                            dve.memset(spare[:], 0.0).then_inc(o_copied, 1)
                    dve.wait_ge(t_ready, DK + 2)
                    dve.tensor_scalar(gate_t[:, 0], ps[lanes, 0, 0:TOKENS], col("i_bias", rows=HEADS_C), None, ALU.add)
                    step(dve.tensor_scalar(gate_t[:, 1], ps[lanes, 1, 0:TOKENS], col("f_bias", rows=HEADS_C), None, ALU.add))
                    dve.scalar_tensor_tensor(gate_t[:, 2], gate_t[:, 1], -1.0, gate_t[:, 1], ALU.mult, ALU.max).then_inc(act_step, 1)
                    dve.wait_ge(act_step, 4)
                    step(dve.scalar_tensor_tensor(gate_t[:, 1], gate_t[:, 1], 0.0, gate_t[:, 2], ALU.min, ALU.subtract))
                    dve.tensor_tensor_scan(gate_t[:, 3], ones[lanes, :], gate_t[:, 1], 0.0, ALU.mult, ALU.add).then_inc(summed, 1)
                    dve.wait_ge(summed, 1)
                    dve.scalar_tensor_tensor(gate_t[:, 4], gate_t[:, 0], IGATE_CAP, gate_t[:, 3], ALU.mult, ALU.subtract).then_inc(summed, 1)

                @block.gpsimd
                def _(pool):
                    step = Chain(pool, pool_step)
                    step(pool.memset(pick[:], 0.0))
                    pool.affine_select(out=pick[:], in_=pick[:], compare_op=ALU.not_equal, fill=1.0, base=0,
                                       pattern=[[-1, HEADS_C], [0, P]], channel_multiplier=1).then_inc(pick_ready, 1)

            with signals("scored", "biased", "exped", "probs_ready", "probs_turned", "turned_copied", "weighted", "dve_step") as (
                    scored, biased, exped, probs_ready, probs_turned, turned_copied, weighted, dve_step), ExitStack() as att:
                weight = sbuf("weight", [P, 2, TRI], mem=att)
                weight_t = sbuf("weight_t", [P, 2, TRI], mem=att)
                top = sbuf("top", [P, 2, TT], mem=att)
                least = sbuf("least", [P, 2, TT], mem=att)
                total = sbuf("total", [P, 2, TT], mem=att)
                part = (slice(0, P), slice(P, TRI))
                keys = (P, TOKENS)
                n = HEADS_C
                block = att.enter_context(nc.Block())

                @block.tensor
                def _(pe):
                    for i in range(n + 2):
                        if i < n:
                            half = slice(i % 2 * HD, i % 2 * HD + HD)
                            if i >= 2:
                                pe.wait_ge(probs_ready, i - 1)
                            q, k = qkT[half, i // 2, :], qkT[half, 4 + i // 2, :]
                            pe.matmul(ps[:, i % 2, 0:P], q[:, 0:P], k[:, 0:P], start=True, stop=True)
                            pe.matmul(ps[:, i % 2, P:TRI], q[:, P:TOKENS], k, start=True, stop=True).then_inc(scored, 1)
                        j = i - 1
                        if 0 <= j < n:
                            pe.wait_ge(probs_ready, j + 1)
                            if j >= 2:
                                pe.wait_ge(turned_copied, j - 1)
                            for b in range(3):
                                last = pe.transpose(ps[:, 2 + j % 2, b * P:b * P + P], weight[:, j % 2, b * P:b * P + P], ident[:])
                            last.then_inc(probs_turned, 1)
                        j = i - 2
                        if j >= 0:
                            pe.wait_ge(turned_copied, j + 1)
                            t = weight_t[:, j % 2, :]
                            out = [ps[:, 4 + 2 * (j // 4) + a, j % 4 * P:j % 4 * P + P] for a in range(TT)]
                            val = [v[:, s, j * P:j * P + P] for s in range(TT)]
                            pe.matmul(out[0], t[:, 0:P], val[0], start=True, stop=True, skip_group_check=True)
                            pe.matmul(out[1], t[:, P:2 * P], val[0], start=True, stop=False, skip_group_check=True)
                            pe.matmul(out[1], t[:, 2 * P:TRI], val[1], start=False, stop=True,
                                      skip_group_check=True).then_inc(weighted, 1)

                @block.vector
                def _(dve):
                    step = Chain(dve, dve_step)
                    for i in range(n + 1):
                        if i < n:
                            o = weight[:, i % 2, :]
                            if i >= 2:
                                dve.wait_ge(probs_turned, i - 1)
                            for t in range(TT):
                                last = dve.scalar_tensor_tensor(o[:, part[t]], key_gate[:, i, 0:keys[t]], decay[:, t, i:i + 1],
                                                                mask[:, part[t]], ALU.add, ALU.add)
                            step(last)
                            for t in range(TT):
                                last = dve.tensor_reduce(top[:, i % 2, t:t + 1], o[:, part[t]], AX.X, ALU.max)
                            step(last)
                            step(dve.tensor_tensor(top[:, i % 2, :], top[:, i % 2, :], decay[:, :, i], ALU.max))
                            dve.tensor_scalar(top[:, i % 2, :], top[:, i % 2, :], -1.0, None, ALU.mult).then_inc(biased, 1)
                        j = i - 1
                        if j >= 0:
                            o = weight[:, j % 2, :]
                            s = total[:, j % 2, :]
                            dve.wait_ge(exped, j + 1)
                            dve.wait_ge(scored, j + 1)
                            for t in range(TT):
                                last = dve.scalar_tensor_tensor(o[:, part[t]], o[:, part[t]], HD ** -0.5, ps[:, j % 2, part[t]],
                                                                ALU.mult, ALU.mult, accum_out=s[:, t:t + 1])
                            step(last)
                            step(dve.scalar_tensor_tensor(s, s, -1.0, s, ALU.mult, ALU.max))
                            step(dve.tensor_tensor(s, s, least[:, j % 2, :], ALU.max))
                            step(dve.reciprocal(s, s))
                            for t in range(TT):
                                last = dve.tensor_scalar(o[:, part[t]], o[:, part[t]], s[:, t:t + 1], None, ALU.mult)
                            last.then_inc(probs_ready, 1)

                @block.scalar
                def _(act):
                    for i in range(n + 1):
                        if i < n:
                            act.wait_ge(biased, i + 1)
                            act.activation(least[:, i % 2, :], top[:, i % 2, :], ACT.Exp)
                            for t in range(TT):
                                o = weight[:, i % 2, part[t]]
                                last = act.activation(o, o, ACT.Exp, bias=top[:, i % 2, t:t + 1])
                            last.then_inc(exped, 1)
                        j = i - 1
                        if j >= 0:
                            act.wait_ge(probs_turned, j + 1)
                            if j >= 2:
                                act.wait_ge(weighted, j - 1)
                            act.activation(weight_t[:, j % 2, :], ps[:, 2 + j % 2, 0:TRI], ACT.Copy).then_inc(turned_copied, 1)

            oT = qkT
            head_norm(v, out_gate, p["norm_w"], oT)
            return oT

        def hgrn2(mem):
            buf, p = params("hgrn", mem)
            qT = sbuf("qT", [P, HEADS_C, TOKENS], mem=mem)
            kT = sbuf("kT", [P, HEADS_C, TOKENS], mem=mem)
            cum = sbuf("cum", [P, HEADS_C, TOKENS], mem=mem)
            v = sbuf("v", [P, TT, D], mem=mem)
            out_gate = sbuf("out_gate", [P, TT, D], mem=mem)

            with signals("params_loaded", "t_ready", "t_read", "n_ready", "n_read", "g_copied", "act_step", "dve_step") as (
                    params_loaded, t_ready, t_read, n_ready, n_read, g_copied, act_step, dve_step), \
                    buffer("log_f", [P, HEADS_C, TOKENS]) as log_f, buffer("soft", [P, HEADS_C, TOKENS]) as soft, nc.Block() as block:
                @block.sync
                def _(sp):
                    sp.dma_start(buf[:], d["hgrn"]).then_inc(params_loaded, 16)
                    stream.feed(sp, 8)
                    sp.wait_ge(params_loaded, 16)

                @block.tensor
                def _(pe):
                    at = 0
                    for _ in range(4):
                        at = product_t(pe, hT, ALL_T, at, t_ready, t_read)
                    for n in range(4):
                        product_n(pe, hT, n, n_ready, n_read)

                @block.scalar
                def _(act):
                    for at in range(16):
                        out, func = (qT, ACT.Silu) if at < 8 else (log_f, ACT.Copy)
                        act.wait_ge(t_ready, at + 1)
                        act.activation(out[:, at % 8, :], ps[:, at % 4, 0:TOKENS], func).then_inc(t_read, 1)
                    act.wait_ge(t_read, 16)
                    act.activation(kT[:], log_f[:], ACT.Sigmoid, scale=-1.0)
                    act.activation(soft[:], log_f[:], ACT.Abs).then_inc(act_step, 1)
                    act.wait_ge(act_step, 1)
                    act.activation(soft[:], soft[:], ACT.Exp, scale=-1.0).then_inc(act_step, 1)
                    act.wait_ge(act_step, 2)
                    act.activation(soft[:], soft[:], ACT.Ln, bias=1.0).then_inc(act_step, 1)
                    act.wait_ge(g_copied, 1)
                    act.activation(out_gate[:], out_gate[:], ACT.Silu)

                @block.vector
                def _(dve):
                    step = Chain(dve, dve_step)
                    for n in range(4):
                        out = v if n < 2 else out_gate
                        dve.wait_ge(n_ready, n + 1)
                        dve.tensor_copy(out[:, :, n % 2 * WIDE:n % 2 * WIDE + WIDE], bank_n(n)).then_inc(n_read, 1)
                    dve.wait_ge(n_read, 4)
                    dve.memset(spare[:], 0.0).then_inc(g_copied, 1)
                    dve.wait_ge(act_step, 3)
                    step(dve.scalar_tensor_tensor(log_f[:], log_f[:], 0.0, soft[:], ALU.min, ALU.subtract))
                    step(dve.tensor_scalar(log_f[:], log_f[:], LOG_FLOOR, None, ALU.max))
                    for h in range(HEADS_C):
                        dve.tensor_tensor_scan(cum[:, h, :], ones[:], log_f[:, h, :], 0.0, ALU.mult, ALU.add)

            with ExitStack() as att:
                weight = sbuf("weight", [P, TT, HEADS_C, P], mem=att)
                weight_far = sbuf("weight_far", [P, HEADS_C, P], mem=att)
                q_dec = sbuf("q_dec", [P, 2, HEADS_C, TOKENS], mem=att)
                k_dec = sbuf("k_dec", [P, 2, HEADS_C, TOKENS], mem=att)
                diff = sbuf("diff", [P, 2, HEADS_C * P], mem=att)
                levels = [P >> n for n in range(8)]
                pair_bits = sbuf("pair_bits", [P, 2, D], mem=att)
                pairs_of = pair_bits[:, 0, :].rearrange("p (n t) -> p n t", n=8)
                pairs_bit = pair_bits[:, 1, :].bitcast(U32).rearrange("p (n t) -> p n t", n=8)
                with signals("diff_ready", "exped", "scaled", "scored", "placed", "dve_step", "pool_step", "masks_ready", "done") as (
                        diff_ready, exped, scaled, scored, placed, dve_step, pool_step, masks_ready, done), nc.Block() as block:
                    @block.gpsimd
                    def _(pool):
                        step = Chain(pool, pool_step)
                        pool.memset(q_dec[:], 0.0)
                        pool.memset(k_dec[:], 0.0).then_inc(masks_ready, 1)
                        step(pool.memset(pairs_of, 0.0))
                        for n, half in enumerate(levels[1:]):
                            segs = P // (2 * half)
                            m = pairs_of[:, n, :].rearrange("p (g a w) -> p g a w", a=2, w=half)[:, :, 1, :]
                            step(pool.memset(m, 1.0))
                            step(pool.affine_select(out=m, in_=m, compare_op=ALU.is_ge, fill=0.0, base=0,
                                                    pattern=[[-2 * half, segs], [0, half]], channel_multiplier=1))
                            step(pool.affine_select(out=m, in_=m, compare_op=ALU.is_ge, fill=0.0, base=half - 1,
                                                    pattern=[[2 * half, segs], [0, half]], channel_multiplier=-1))
                        step(pool.tensor_copy(pairs_of[:, 7, :], ident[:]))
                        pool.tensor_copy(pairs_bit, pairs_of).then_inc(masks_ready, 1)

                    def split(a, half):
                        return a.rearrange("p h (g a w) -> p (h g) a w", a=2, w=half)

                    @block.vector
                    def _(dve):
                        step = Chain(dve, dve_step)

                        def decays(n):
                            half = levels[n]
                            c = split(cum[:], half)
                            ref = c[:, :, 0, half - 1:half].broadcast_to([P, HEADS_C * P // half, half])
                            if n >= 1:
                                dve.wait_ge(scaled, n)
                            dve.tensor_tensor(diff[:, 0, :].rearrange("p (g w) -> p g w", w=half), c[:, :, 1, :], ref, ALU.subtract)
                            dve.tensor_tensor(diff[:, 1, :].rearrange("p (g w) -> p g w", w=half), ref, c[:, :, 0, :],
                                              ALU.subtract).then_inc(diff_ready, 1)

                        def scale(n):
                            half = levels[n]
                            dve.wait_ge(exped, n + 1)
                            if n >= 2:
                                dve.wait_ge(scored, 2 * (n - 2) + 2)
                            e = diff[:].rearrange("p a (g w) -> p a g w", w=half)
                            dve.tensor_tensor(split(q_dec[:, n % 2], half)[:, :, 1, :], split(qT[:], half)[:, :, 1, :], e[:, 0], ALU.mult)
                            dve.tensor_tensor(split(k_dec[:, n % 2], half)[:, :, 0, :], split(kT[:], half)[:, :, 0, :], e[:, 1],
                                              ALU.mult).then_inc(scaled, 1)

                        def place(n):
                            for t in range(TT):
                                dve.wait_ge(scored, 2 * n + t + 1)
                                if n >= 2:
                                    dve.wait_ge(placed, 2 * (n - 1) + t)
                                for b in range(2):
                                    got = ps[:, 4 * (n % 2) + 2 * t + b, :].rearrange("p (h n) -> p h n", h=4)
                                    if n == 0:
                                        if t == 0:
                                            last = dve.tensor_copy(weight_far[:, 4 * b:4 * b + 4, :], got)
                                        continue
                                    last = dve.copy_predicated(weight[:, t, 4 * b:4 * b + 4, :], spread(pairs_bit[:, n - 1, :], 1, 4), got)
                                last.then_inc(placed, 1) if n or t == 0 else None

                        dve.wait_ge(masks_ready, 2)
                        step(dve.memset(weight[:], 0.0))
                        decays(0)
                        for n in range(8):
                            scale(n)
                            if n + 1 < 8:
                                decays(n + 1)
                            if n >= 1:
                                place(n - 1)
                        place(7)
                        place(8)

                    @block.scalar
                    def _(act):
                        for n in range(8):
                            act.wait_ge(diff_ready, n + 1)
                            act.activation(diff[:], diff[:], ACT.Exp).then_inc(exped, 1)

                    @block.tensor
                    def _(pe):
                        for n in range(9):
                            if n < 8:
                                pe.wait_ge(scaled, n + 1)
                            q, k = (q_dec[:, n % 2], k_dec[:, n % 2]) if n < 8 else (qT, kT)
                            for t in range(TT):
                                if n >= 2:
                                    pe.wait_ge(placed, max(1, 2 * (n - 2)) + (t if n > 2 else 0))
                                for h in range(HEADS_C):
                                    s, u = (0, 1) if n == 0 else (t, t)
                                    if n == 0 and t == 1:
                                        break
                                    last = pe.matmul(ps[:, 4 * (n % 2) + 2 * t + h // 4, h % 4 * P:h % 4 * P + P],
                                                     k[:, h, s * P:s * P + P], q[:, h, u * P:u * P + P], start=True, stop=True)
                                if n == 0 and t == 1:
                                    continue
                                last.then_inc(scored, 1 if n else 2)

                with nc.Block() as block:
                    @block.tensor
                    def _(pe):
                        for h in range(HEADS_C):
                            out = [ps[:, 4 + 2 * (h // 4) + t, h % 4 * P:h % 4 * P + P] for t in range(TT)]
                            val = [v[:, s, h * P:h * P + P] for s in range(TT)]
                            pe.matmul(out[0], weight[:, 0, h, :], val[0], start=True, stop=True, skip_group_check=True)
                            pe.matmul(out[1], weight_far[:, h, :], val[0], start=True, stop=False, skip_group_check=True)
                            pe.matmul(out[1], weight[:, 1, h, :], val[1], start=False, stop=True, skip_group_check=True)

            oT = qT
            head_norm(v, out_gate, p["norm_w"], oT)
            return oT

        def route(expert_gate):
            with signals("n_ready", "n_read", "exped", "logits_ready", "dve_step", "gates_ready", "turned", "turned_read", "pick_ready",
                         "pool_step", "repeated", "repeated_read") as (
                    n_ready, n_read, exped, logits_ready, dve_step, gates_ready, turned, turned_read, pick_ready, pool_step,
                    repeated, repeated_read), ExitStack() as own:
                logit = sbuf("logit", [P, TT, EXPERTS], mem=own)
                best = sbuf("best", [P, TT, EXPERTS], mem=own)
                best_no = sbuf("best_no", [P, TT, EXPERTS], U32, mem=own)
                best_e = sbuf("best_e", [P, TT, EXPERTS], mem=own)
                share = sbuf("share", [P, TT, 2], mem=own)
                share_sum = sbuf("share_sum", [P, TT], mem=own)
                number = sbuf("number", [P, EXPERTS], mem=own)
                gate = sbuf("gate", [P, TT, EXPERTS], mem=own)
                second = sbuf("second", [P, TT, EXPERTS], mem=own)
                gate_t = sbuf("gate_t", [EXPERTS, TOKENS], mem=own)
                pick = sbuf("pick", [EXPERTS, EXPERTS, P], mem=own)
                block = own.enter_context(nc.Block())

                @block.sync
                def _(sp):
                    stream.feed(sp, 1)

                @block.tensor
                def _(pe):
                    product_n(pe, hT, 0, n_ready, n_read)
                    pe.wait_ge(gates_ready, 1)
                    for t in range(TT):
                        last = pe.transpose(ps[0:EXPERTS, 0, t * P:t * P + P], gate[:, t, :], ident[:])
                    last.then_inc(turned, 1)
                    pe.wait_ge(turned_read, 1)
                    pe.wait_ge(pick_ready, 1)
                    for n in range(EXPERTS // 2):
                        for b in range(2):
                            last = pe.matmul(ps[:, 4 + n, b * TOKENS:b * TOKENS + TOKENS], pick[:, 2 * n + b, :], gate_t[:],
                                             start=True, stop=True)
                        last.then_inc(repeated, 1)

                @block.vector
                def _(dve):
                    step = Chain(dve, dve_step)
                    dve.wait_ge(n_ready, 1)
                    step(dve.tensor_copy(logit[:], bank_n(0, EXPERTS)))
                    for t in range(TT):
                        last = dve.max(best[:, t, :], logit[:, t, :])
                    step(last)
                    for t in range(TT):
                        last = dve.max_index(best_no[:, t, :], best[:, t, :], logit[:, t, :])
                    dve.tensor_tensor(share[:], best[:, :, 0:2], best[:, :, 0:1].broadcast_to([P, TT, 2]), ALU.subtract).then_inc(logits_ready, 1)
                    dve.wait_ge(logits_ready, 1)
                    step(dve.tensor_copy(best_e[:], best_no[:]))
                    dve.wait_ge(exped, 1)
                    step(dve.tensor_tensor(share_sum[:], share[:, :, 0], share[:, :, 1], ALU.add))
                    step(dve.reciprocal(share_sum[:], share_sum[:]))
                    step(dve.tensor_tensor(share[:], share[:], spread(share_sum[:], 2, 2), ALU.mult))
                    dve.wait_ge(pick_ready, 1)
                    for t in range(TT):
                        for j, out in ((0, gate), (1, second)):
                            last = dve.tensor_scalar(out[:, t, :], number[:], best_e[:, t, j:j + 1], share[:, t, j:j + 1],
                                                     ALU.is_equal, ALU.mult)
                    step(last)
                    dve.tensor_tensor(gate[:], gate[:], second[:], ALU.add).then_inc(gates_ready, 1)

                @block.scalar
                def _(act):
                    act.wait_ge(logits_ready, 1)
                    act.activation(share[:], share[:], ACT.Exp).then_inc(exped, 1)
                    act.wait_ge(turned, 1)
                    act.activation(gate_t[:], ps[0:EXPERTS, 0, 0:TOKENS], ACT.Copy).then_inc(turned_read, 1)
                    for n in range(EXPERTS // 2):
                        act.wait_ge(repeated, n + 1)
                        act.activation(expert_gate[:, 2 * n:2 * n + 2, :], ps[:, 4 + n, :].rearrange("p (b n) -> p b n", b=2), ACT.Copy)

                @block.gpsimd
                def _(pool):
                    step = Chain(pool, pool_step)
                    pool.iota(number[:], pattern=[[1, EXPERTS]], base=0, channel_multiplier=0, allow_small_or_imprecise_dtypes=True)
                    step(pool.memset(pick[:], 0.0))
                    pool.affine_select(out=pick[:], in_=pick[:], compare_op=ALU.not_equal, fill=1.0, base=0,
                                       pattern=[[-1, EXPERTS], [0, P]], channel_multiplier=1).then_inc(pick_ready, 1)

        def third(mem):
            buf, p = params("ada", mem)
            gain = sbuf("gain", [P, 4, DK], mem=mem)
            with signals("params_loaded") as (params_loaded,), nc.Block() as block:
                @block.sync
                def _(sp):
                    sp.dma_start(buf[:], d["ada"]).then_inc(params_loaded, 16)
                    sp.wait_ge(params_loaded, 16)
            modulation(p, gain)

            def norm(n):
                pre_norm(lambda b: gain[:, n, b:b + 1], lambda b: p["shifts"][:, 2 * n * DK + b:2 * n * DK + b + 1])

            def gate(n):
                return p["gates"][:, n * D:n * D + D]

            norm(0)
            with ExitStack() as mix:
                add_gated(gate(0), mixer=mlstm(mix))
            norm(1)
            feed_forward("swiglu", FFN_TILES, ACT.Silu, gates=2)
            add_gated(gate(1))
            norm(2)
            with ExitStack() as mix:
                add_gated(gate(2), mixer=hgrn2(mix))
            norm(3)
            with ExitStack() as own:
                expert_gate = sbuf("expert_gate", [P, EXPERTS, TOKENS], mem=own)
                route(expert_gate)
                feed_forward("moe", EXPERTS * EXPERT_TILES, ACT.Silu, gates=2, scale_by=expert_gate)
            add_gated(gate(3))

        def last_norm(mem):
            buf, p = params("last", mem)
            with signals("params_loaded", "squared", "var_ready", "rstd_ready") as (params_loaded, squared, var_ready, rstd_ready), \
                    buffer("junk", [P, TT, D]) as junk, nc.Block() as block:
                @block.sync
                def _(sp):
                    sp.dma_start(buf[:], d["last"]).then_inc(params_loaded, 16)

                @block.scalar
                def _(act):
                    for t in range(TT):
                        last = act.activation(junk[:, t, :], x[:, t, :], ACT.Square, accum_out=squares[:, t:t + 1])
                    last.then_inc(squared, 1)

                @block.gpsimd
                def _(pool):
                    power(pool, var_ready, rstd_ready)

                @block.vector
                def _(dve):
                    dve.wait_ge(squared, 1)
                    dve.tensor_scalar(spare[:], squares[:], 1.0 / D, RMS_EPS, ALU.mult, ALU.add).then_inc(var_ready, 1)
                    dve.wait_ge(rstd_ready, 1)
                    dve.wait_ge(params_loaded, 16)
                    for t in range(TT):
                        dve.scalar_tensor_tensor(x[:, t, :], x[:, t, :], rstd[:, t:t + 1], p["norm_w"], ALU.mult, ALU.mult)

        for section in (mixers, peer, nsa, fox, third, last_norm):
            with ExitStack() as mem:
                section(mem)


        with signals("stored") as (stored,), nc.Block() as block:
            @block.sync
            def _(sp):
                sp.dma_start(d["out"], x[:]).then_inc(stored, 16)
                sp.wait_ge(stored, 16)



def _launch_arrays(a):
    chunks = _chunk_layout(a)
    widths = [c.shape[1] for c in chunks]
    packed = np.zeros((len(chunks), P, CHUNK), np.float32)
    for n, c in enumerate(chunks):
        packed[n, :, :c.shape[1]] = c
    arrays = {"stream": packed}
    offsets = {}
    for section, parts in _param_layout(a).items():
        at, offsets[section] = 0, {}
        for name, v in parts.items():
            offsets[section][name] = (at, v.shape[1])
            at += v.shape[1]
        arrays[section] = np.ascontiguousarray(np.concatenate(list(parts.values()), 1))
    x = a["x"][0]
    arrays["x"] = np.ascontiguousarray(x.reshape(TT, P, D).transpose(1, 0, 2))
    arrays["xT"] = np.ascontiguousarray(x.T.reshape(DK, P, TOKENS).transpose(1, 0, 2))
    return arrays, widths, offsets


def kernel(**inputs):
    import concourse.bacc as bacc
    from concourse.bass_utils import run_bass_kernel_spmd

    arrays, widths, offsets = _launch_arrays({n: np.asarray(v) for n, v in inputs.items()})
    nc = bacc.Bacc("TRN2", target_bir_lowering=False, num_devices=1)
    d = {n: nc.dram_tensor("in_" + n, v.shape, F32, kind="ExternalInput").ap() for n, v in arrays.items()}
    d["out"] = nc.dram_tensor("out", (P, TT, D), F32, kind="ExternalOutput").ap()
    build(nc, d, widths, offsets)
    r = run_bass_kernel_spmd(nc, [{"in_" + n: v for n, v in arrays.items()}], core_ids=[0])
    return r.results[0]["out"].transpose(1, 0, 2).reshape(1, TOKENS, D)
```

```python
import math
from contextlib import ExitStack, contextmanager

import concourse.bass as bass
import numpy as np
from concourse import mybir

F32 = mybir.dt.float32
F32R = mybir.dt.float32r
BF16 = mybir.dt.bfloat16
U32 = mybir.dt.uint32
ALU = mybir.AluOpType
ACT = mybir.ActivationFunctionType
AX = mybir.AxisListType

P = 128
TOKENS = 256
TT = TOKENS // P
D = 1024
DK = D // P
CHUNK = 4096
RING = 4
WIDE = 512
NEG = -1e30
ALPHA = 2.0 ** 0.25
LN_EPS = 1e-5
RMS_EPS = 1e-6
TRI = 3 * P
HEADS_A, HEADS_B, HEADS_C = 8, 16, 8
KEYS, TOPK, PEER_HEADS = 128, 16, 8
GROUPS, REP, HD = 4, 4, 64
N_CMP, CMP_LEN, CMP_STRIDE = 15, 32, 16
FFN_TILES, EXPERTS, EXPERT_TILES = 22, 8, 11
MLP_TILES = 32
ADA_ROWS = 2 * 6 * 2
LOG_FLOOR = math.log(1e-30)
IGATE_CAP = 15.0



def _k_major(w):
    k, n = w.shape
    return w.reshape(k // P, P, n).transpose(1, 0, 2).reshape(P, -1)


def _columns(v):
    return v.reshape(-1, P).T


def _rows(v):
    return np.broadcast_to(v.reshape(1, -1), (P, v.size))


def _pad_rows(a):
    out = np.zeros((P,) + a.shape[1:], a.dtype)
    out[:a.shape[0]] = a
    return out


def _bucket_of_distance():
    dist = np.arange(TOKENS)
    far = np.maximum(dist, 16).astype(np.float32)
    large = 16 + (np.log(far / np.float32(16)) / np.float32(math.log(64)) * np.float32(16)).astype(np.int32)
    return np.where(dist < 16, dist, np.minimum(large, 31))


def _rope_tables():
    inv = np.float32(10000.0) ** (-np.arange(0, HD, 2, dtype=np.float32) / np.float32(HD))
    angle = (np.arange(TOKENS, dtype=np.float32)[:, None] * inv[None, :]).astype(np.float32)
    table = lambda f: np.tile(f(angle).astype(np.float32).T, (4, 1))
    return table(np.cos), table(np.sin)


def _chunk_layout(a):
    out = []

    def product(w, step=WIDE):
        for n in range(0, w.shape[1], step):
            out.append(_k_major(w[:, n:n + step]))

    w = a["w_in"][0]
    for lo in (1024, 0, 4096, 2048, 3072, 5120, 6144):
        product(w[:, lo:lo + D])
    product(a["w_proj_a"][0])
    product(a["w_proj_b"][0])
    product(a["w_out"][0])
    product(a["ple_w_gate"][0])
    out.append(_k_major(a["ple_w_proj"][0]))
    product(a["peer_w_q"][0])
    product(a["ada_w_3"][0])
    product(a["ada_w_3"][1])
    u = a["peer_u"][0].reshape(KEYS, KEYS, DK, P).transpose(1, 3, 2, 0).reshape(KEYS, P, D)
    v = a["peer_v"][0].reshape(KEYS, KEYS, D).transpose(1, 0, 2)
    for j in range(0, KEYS, 2):
        out.append(np.concatenate([u[j], v[j], u[j + 1], v[j + 1]], 1))

    def mlp(up, down):
        for f in range(0, MLP_TILES, 2):
            out.append(np.concatenate([x for g in (f, f + 1) for x in
                                       (_k_major(up[:, g * P:g * P + P]), down[g * P:g * P + P])], 1))

    def glu(gate, up, down):
        for f in range(0, gate.shape[1], P):
            out.append(np.concatenate([_k_major(gate[:, f:f + P]), _k_major(up[:, f:f + P]), down[f:f + P]], 1))

    w = a["nsa_w_in_2"][0]
    order = [g * REP + r for pair in range(2) for r in range(REP) for g in (2 * pair, 2 * pair + 1)]
    q = w[:, :D].reshape(D, 16, HD)[:, order].reshape(D, D)
    kc, vc, ks, vs, kw, vw = (w[:, D + 256 * n:D + 256 * n + 256] for n in range(6))
    product(q)
    product(np.concatenate([kc, ks], 1))
    product(np.concatenate([kw, vc], 1))
    product(np.concatenate([vs, vw], 1))
    product(w[:, D + 6 * 256:])
    out.append(_k_major(a["nsa_cmp_w1_2"][0, 0]))
    out.append(_k_major(a["nsa_cmp_w1_2"][0, 1]))
    product(a["nsa_w_out_2"][0])
    mlp(a["mlp_w_up_2"][0], a["mlp_w_down_2"][0])
    product(a["fox_w_in_2"][0])
    product(a["fox_w_out_2"][0])
    mlp(a["mlp_w_up_2"][1], a["mlp_w_down_2"][1])
    product(a["m_w_in_3"][0])
    product(a["m_w_out_3"][0])
    glu(a["ffn_w_gate_3"][0], a["ffn_w_up_3"][0], a["ffn_w_down_3"][0])
    product(a["h_w_in_3"][0])
    product(a["h_w_out_3"][0])
    product(a["moe_router_3"][0])
    for f in range(EXPERT_TILES):
        for e in range(EXPERTS):
            tile = slice(f * P, f * P + P)
            glu(a["moe_w_gate_3"][0, e][:, tile], a["moe_w_up_3"][0, e][:, tile], a["moe_w_down_3"][0, e][tile])
    return out


def _param_layout(a):
    rel = a["rel_bias"].T[:, _bucket_of_distance()]
    t, s = np.arange(TOKENS)[:, None], np.arange(TOKENS)[None, :]
    toeplitz = rel[:, np.maximum(t - s, 0)]
    bias = np.concatenate([toeplitz[:, :P, :P], toeplitz[:, P:, :]], 2).transpose(1, 0, 2).reshape(P, -1)
    b_in = a["b_in"][0]
    w_s = a["gmlp_w_s"][0].transpose(2, 0, 1).reshape(P, -1)
    cos, sin = _rope_tables()
    pos = a["nsa_cmp_pos_2"][0].reshape(2, 16, P)
    w2 = a["nsa_cmp_w2_2"][0].reshape(2, 2, P, HD)
    w2k = np.concatenate([w2[0], w2[0]], 2).transpose(1, 0, 2).reshape(P, -1)
    w2v = w2[1].transpose(1, 0, 2).reshape(P, -1)
    ada = a["ada_b_3"].reshape(2, 6, D)
    return {
        "cols": {
            "b_u": _columns(b_in[0:1024]), "b_q": _columns(b_in[2048:3072]), "b_k": _columns(b_in[3072:4096]),
            "b_ga": _columns(b_in[5120:6144]), "b_gb": _columns(b_in[6144:7168]),
            "norm_g": np.concatenate([_columns(a["norm_g_2"][i, j]) for i in range(2) for j in (0, 2)], 1),
            "norm_w": np.concatenate([_columns(a[n][i]) for i in range(2) for n in ("norm1_w_3", "norm2_w_3")], 1),
            "conv_w": a["m_conv_w_3"][0].reshape(4, 8, P).transpose(2, 1, 0).reshape(P, -1),
            "conv_b": _columns(a["m_conv_b_3"][0]),
            "pos_k": pos[0].T, "pos_v": pos[1].T,
            "b_f": _pad_rows(a["fox_b_f_2"][0][:, None]),
            "i_bias": _pad_rows(a["m_i_bias_3"][0][:, None]), "f_bias": _pad_rows(a["m_f_bias_3"][0][:, None]),
            "cond": _columns(a["c_3"][0]),
        },
        "mix": {
            "b_va": _rows(b_in[1024:2048]), "b_vb": _rows(b_in[4096:5120]), "ln_g": _rows(a["gmlp_ln_g"][0]),
            "ln_b": _rows(a["gmlp_ln_b"][0]), "b_s": _rows(a["gmlp_b_s"][0]), "w_s": w_s,
        },
        "rel": {"rel": bias},
        "ln1": {"g": _rows(a["ln1_g"][0]), "b": _rows(a["ln1_b"][0])},
        "peer": {
            "b_gate": _rows(a["ple_b_gate"][0]),
            "pT": _k_major(a["p"][0, 0].T), "keys": a["peer_sub_keys"][0].transpose(2, 0, 1).reshape(P, -1),
        },
        "ln2": {"g": _rows(a["ln2_g"][0]), "b": _rows(a["ln2_b"][0])},
        "nsa": {
            "cos": cos, "sin": sin, "w2k": w2k, "w2v": w2v,
            "post1": _rows(a["norm_g_2"][0, 1]), "post2": _rows(a["norm_g_2"][0, 3]),
        },
        "fox": {"post1": _rows(a["norm_g_2"][1, 1]), "post2": _rows(a["norm_g_2"][1, 3])},
        "ada": {
            "gates": np.concatenate([_rows(ada[i, j]) for i in range(2) for j in (2, 5)], 1),
            "shifts": np.concatenate([_columns(ada[i, j]) for i in range(2) for j in (0, 1, 3, 4)], 1),
        },
        "mlstm": {"norm_w": _rows(a["m_norm_w_3"][0])},
        "hgrn": {"norm_w": _rows(a["h_norm_w_3"][0])},
        "last": {"norm_w": _rows(a["final_norm_w_3"])},
    }



def spread(ap, axis, n):
    shape = list(ap.shape)
    return ap.unsqueeze(axis).broadcast_to(shape[:axis] + [n] + shape[axis:])


class Chain:

    def __init__(self, eng, sem):
        self.eng, self.sem, self.n = eng, sem, 0

    def __call__(self, ins):
        self.n += 1
        ins.then_inc(self.sem, 1)
        self.eng.wait_ge(self.sem, self.n)


class Stream:

    def __init__(self, dram, widths, ring, loaded, used):
        self.dram, self.widths, self.ring, self.loaded, self.used = dram, widths, ring, loaded, used
        self.asked = 0
        self.taken = 0
        self.pending = False

    def release(self, ins):
        if self.pending:
            ins.then_inc(self.used, 1)
            self.pending = False

    def slot(self, c):
        return self.ring[:, c % RING, :]

    def feed(self, sp, n):
        end = min(self.taken + n + RING - 1, len(self.widths))
        while self.asked < end:
            c = self.asked
            same = 0
            while c + same < end and self.widths[c + same] == self.widths[c]:
                same += 1
            turns = same // RING
            w = self.widths[c]
            if c >= RING and turns >= 2:
                with sp.Fori(0, turns) as i:
                    for s in range(RING):
                        sp.wait_ge(self.used, i * RING + (c + s - RING + 1))
                        src = self.dram[bass.ds(i * RING + (c + s), 1), :, 0:w].rearrange("a p n -> (a p) n")
                        sp.dma_start(self.slot(c + s)[:, 0:w], src).then_inc(self.loaded[(c + s) % RING], 16)
                self.asked += turns * RING
            else:
                if c >= RING:
                    sp.wait_ge(self.used, c - RING + 1)
                sp.dma_start(self.slot(c)[:, 0:w], self.dram[c, :, 0:w]).then_inc(self.loaded[c % RING], 16)
                self.asked += 1

    def wait(self, eng, c, turn=None):
        value = 16 * (c // RING + 1)
        eng.wait_ge(self.loaded[c % RING], value if turn is None else turn * 16 + value)

    def take(self, pe):
        c = self.taken
        self.taken += 1
        self.wait(pe, c)
        return c


class Parts:

    SLOTS = 4

    def __init__(self, stream, kinds, hi, lo, high_ready, split, block_used):
        self.stream, self.hi, self.lo = stream, hi, lo
        self.high_ready, self.split, self.block_used = high_ready, split, block_used
        self.blocks = [(stream.taken + n, kind, q) for n, kind in enumerate(kinds) if kind != "." for q in range(4)]
        self.n_high = self.n_low = self.n_used = 0

    def raw(self, b):
        c, kind, q = self.blocks[b]
        w = self.stream.slot(c)
        if kind == "t":
            return w.rearrange("p (k n) -> p k n", k=DK)[:, :, q * P:q * P + P]
        return w[:, q * D:q * D + D].rearrange("p (k n) -> p k n", k=2)

    def place(self, buf, b):
        return buf[:, b % self.SLOTS, :].rearrange("p (k n) -> p k n", k=DK if self.blocks[b][1] == "t" else 2)

    def high(self, act, end):
        for b in range(self.n_high, min(end, len(self.blocks))):
            if self.blocks[b][2] == 0:
                self.stream.wait(act, self.blocks[b][0])
            if b >= self.SLOTS:
                act.wait_ge(self.block_used, b - self.SLOTS + 1)
            act.activation(self.place(self.hi, b), self.raw(b), ACT.Copy).then_inc(self.high_ready, 1)
            self.n_high = b + 1

    def low(self, dve, end):
        for b in range(self.n_low, min(end, len(self.blocks))):
            dve.wait_ge(self.high_ready, b + 1)
            dve.tensor_tensor(self.place(self.lo, b), self.raw(b), self.place(self.hi, b), ALU.subtract).then_inc(self.split, 1)
            self.n_low = b + 1

    def take(self, pe):
        b = self.n_used
        self.n_used += 1
        c, _, q = self.blocks[b]
        if q == 0:
            assert c == self.stream.taken
            self.stream.taken += 1
        pe.wait_ge(self.split, b + 1)
        return self.place(self.hi, b), self.place(self.lo, b)

    def began(self, n, ins):
        b = self.n_used - 1
        q = self.blocks[b][2]
        if n == 0 and b > 0:
            ins.then_inc(self.block_used, 1)
        elif n == 1 and q == 0:
            self.stream.release(ins)
        elif n == 1 and q == 3:
            ins.then_inc(self.stream.used, 1)


def build(nc, d, widths, offsets):
    ctx = ExitStack()
    with ctx:
        names = {}

        def buffer(name, shape, dt=F32):
            names[name] = names.get(name, 0) + 1
            return nc.sbuf_tensor(name if names[name] == 1 else f"{name}_{names[name]}", shape, dt)

        def sbuf(name, shape, dt=F32, mem=ctx):
            return mem.enter_context(buffer(name, shape, dt))

        stage = [0]
        former = []

        @contextmanager
        def signals(*names):
            stage[0] += 1
            sems = [nc.alloc_semaphore(f"{n}_{stage[0]}") for n in names]
            if former:
                nc.clear_and_free_semaphores(former)
            former[:] = sems
            yield sems

        ring = sbuf("ring", [P, RING, CHUNK])
        x = sbuf("x", [P, TT, D])
        hT = sbuf("hT", [P, DK, TOKENS])
        n_cols = max(o + n for o, n in offsets["cols"].values())
        cols = sbuf("cols", [P, n_cols])
        ident = sbuf("ident", [P, P])
        ones = sbuf("ones", [P, TOKENS])
        mask = sbuf("mask", [P, TRI])
        eps_ln = sbuf("eps_ln", [P, 1])
        minus_half = sbuf("minus_half", [P, 16])
        mod = sbuf("mod", [ADA_ROWS, WIDE])
        ps = ctx.enter_context(nc.psum_tensor("ps", [P, 8, WIDE], F32))

        loaded = [ctx.enter_context(nc.semaphore(f"chunk_loaded_{i}")) for i in range(RING)]
        used = ctx.enter_context(nc.semaphore("chunk_used"))
        stream = Stream(d["stream"], widths, ring, loaded, used)

        def col(name, n=0, rows=P):
            o = offsets["cols"][name][0] + n
            return cols[0:rows, o:o + 1]

        def params(section, mem):
            n = max(o + w for o, w in offsets[section].values())
            buf = sbuf("params_" + section, [P, n], mem=mem)
            return buf, {k: buf[:, o:o + w] for k, (o, w) in offsets[section].items()}


        def product_t(pe, rhs, blocks, at, ready, freed, banks=4):
            c = stream.take(pe)
            w = stream.slot(c)
            n = stream.widths[c] // DK
            for b, (o, m) in enumerate(blocks):
                if at + b >= banks:
                    pe.wait_ge(freed, at + b - banks + 1)
                for k in range(DK):
                    last = pe.matmul(ps[0:m, (at + b) % banks, 0:TOKENS], w[:, k * n + o:k * n + o + m], rhs[:, k, :],
                                     start=(k == 0), stop=(k == DK - 1))
                    if b == 0 and k == 0:
                        stream.release(last)
                last.then_inc(ready, 1)
            stream.pending = True
            return at + len(blocks)

        def product_n(pe, lhsT, at, ready, freed, tiles=TT, k_tiles=DK):
            c = stream.take(pe)
            w = stream.slot(c)
            n = stream.widths[c] // k_tiles
            if at >= 2:
                pe.wait_ge(freed, at - 1)
            for t in range(tiles):
                for k in range(k_tiles):
                    last = pe.matmul(ps[:, 4 + 2 * (at % 2) + t, 0:n], lhsT[:, k, t * P:t * P + P], w[:, k * n:k * n + n],
                                     start=(k == 0), stop=(k == k_tiles - 1))
                    if t == 0 and k == 0:
                        stream.release(last)
            last.then_inc(ready, 1)
            stream.pending = True
            return at + 1

        PARTS = ("high_ready", "split", "block_used")

        def weight_parts(kinds, sems, mem):
            hi, lo = (sbuf(n, [P, Parts.SLOTS, D], F32R, mem=mem) for n in ("weight_hi", "weight_lo"))
            return Parts(stream, kinds, hi, lo, *sems)

        def token_parts(mem):
            return [sbuf(n, [P, DK, TOKENS], F32R, mem=mem) for n in ("x_hi", "x_lo")]

        def split_block(dve, src, parts, b, part_hi, part_ready, count):
            dve.tensor_copy(parts[0][:, b, :], src[:, b, :]).then_inc(part_hi, 1)
            dve.wait_ge(part_hi, count + 1)
            dve.tensor_tensor(parts[1][:, b, :], src[:, b, :], parts[0][:, b, :], ALU.subtract).then_inc(part_ready, 1)

        def parts_t(pe, weights, x_parts, at, ready, freed, x_ready=None):
            for b in range(4):
                if at + b >= 4:
                    pe.wait_ge(freed, at + b - 3)
                hi, lo = weights.take(pe)
                out = ps[:, (at + b) % 4, 0:TOKENS]
                for k in range(DK):
                    if x_ready is not None and b == 0:
                        pe.wait_ge(x_ready, k + 1)
                    first = pe.matmul(out, hi[:, k, :], x_parts[0][:, k, :], start=(k == 0), stop=False)
                    second = pe.matmul(out, hi[:, k, :], x_parts[1][:, k, :], start=False, stop=False)
                    last = pe.matmul(out, lo[:, k, :], x_parts[0][:, k, :], start=False, stop=(k == DK - 1))
                    if k == 0:
                        weights.began(0, first)
                        weights.began(1, second)
                last.then_inc(ready, 1)
            stream.pending = False
            return at + 4

        def parts_n(pe, weights, x_parts, at, ready, freed, x_ready=None):
            if at >= 2:
                pe.wait_ge(freed, at - 1)
            for b in range(4):
                hi, lo = weights.take(pe)
                for k in (2 * b, 2 * b + 1):
                    if x_ready is not None and at == 0:
                        pe.wait_ge(x_ready, k + 1)
                    for t in range(TT):
                        out = ps[:, 4 + 2 * (at % 2) + t, :]
                        x_hi, x_lo = (part[:, k, t * P:t * P + P] for part in x_parts)
                        first = pe.matmul(out, x_hi, hi[:, k % 2, :], start=(k == 0), stop=False, skip_group_check=True)
                        second = pe.matmul(out, x_hi, lo[:, k % 2, :], start=False, stop=False, skip_group_check=True)
                        last = pe.matmul(out, x_lo, hi[:, k % 2, :], start=False, stop=(k == DK - 1), skip_group_check=True)
                        if k == 2 * b and t == 0:
                            weights.began(0, first)
                            weights.began(1, second)
            last.then_inc(ready, 1)
            stream.pending = False
            return at + 1

        def bank_n(at, n=WIDE):
            return ps[:, 4 + 2 * (at % 2):6 + 2 * (at % 2), 0:n]

        ALL_T = [(n * P, P) for n in range(4)]

        def transposes(pe, src, ready, freed, blocks=DK, banks=4):
            for b in range(blocks):
                if b >= banks:
                    pe.wait_ge(freed, b - banks + 1)
                for t in range(TT):
                    last = pe.transpose(ps[:, b % banks, t * P:t * P + P], src[:, t, b * P:b * P + P], ident[:])
                last.then_inc(ready, 1)

        stats = sbuf("stats", [P, TT, 2, 6])
        moments = sbuf("moments", [P, TT, 2])
        squares = sbuf("squares", [P, TT])
        spare = sbuf("spare", [P, TT])
        rstd = sbuf("rstd", [P, TT])

        def y_banks(t):
            return ps[:, 4 + t:8:2, :]

        def halves(ap):
            return ap.rearrange("p (c n) -> p c n", c=2)

        def power(pool, var_ready, rstd_ready):
            pool.wait_ge(var_ready, 1)
            pool.tensor_tensor(rstd[:], spare[:], minus_half[:, 0:TT], ALU.pow).then_inc(rstd_ready, 1)

        def layer_norm(dve, step, y, g, b, out, var_ready, rstd_ready):
            for t in range(TT):
                for c in range(2):
                    last = dve.bn_stats(stats[:, t, c, :], y[:, t, c * WIDE:c * WIDE + WIDE])
            step(last)
            for t in range(TT):
                last = dve.bn_aggr(moments[:, t, :], stats[:, t, :, :].rearrange("p a b -> p (a b)"))
            step(last)
            dve.tensor_scalar(spare[:], moments[:, :, 1], LN_EPS, None, ALU.add).then_inc(var_ready, 1)
            dve.wait_ge(rstd_ready, 1)
            for t in range(TT):
                last = dve.tensor_scalar(y[:, t, :], y[:, t, :], moments[:, t, 0:1], rstd[:, t:t + 1],
                                         ALU.subtract, ALU.mult)
            step(last)
            step(dve.tensor_tensor(y[:, :, :], y[:, :, :], spread(g, 1, TT), ALU.mult))
            return dve.tensor_tensor(out[:, :, :], y[:, :, :], spread(b, 1, TT), ALU.add)

        def pre_norm(gain, x_parts, bias=None):
            with signals("squared", "var_ready", "rstd_ready", "scaled", "turned", "turned_read", "part_hi",
                         "part_ready") as (
                    squared, var_ready, rstd_ready, scaled, turned, turned_read, part_hi, part_ready), \
                    buffer("xhat", [P, TT, D], F32) as xhat, \
                    nc.Block() as block:
                @block.scalar
                def _(act):
                    for t in range(TT):
                        last = act.activation(xhat[:, t, :], x[:, t, :], ACT.Square, accum_out=squares[:, t:t + 1])
                    last.then_inc(squared, 1)
                    for b in range(DK):
                        act.wait_ge(turned, b + 1)
                        act.activation(hT[:, b, :], ps[:, b % 4, 0:TOKENS], ACT.Identity, scale=gain(b),
                                       bias=0.0 if bias is None else bias(b)).then_inc(turned_read, 1)

                @block.vector
                def _(dve):
                    dve.wait_ge(squared, 1)
                    dve.tensor_scalar(spare[:], squares[:], 1.0 / D, RMS_EPS, ALU.mult, ALU.add).then_inc(var_ready, 1)
                    dve.wait_ge(rstd_ready, 1)
                    for t in range(TT):
                        last = dve.tensor_scalar(xhat[:, t, :], x[:, t, :], rstd[:, t:t + 1], None, ALU.mult)
                    last.then_inc(scaled, 1)
                    for b in range(DK):
                        dve.wait_ge(turned_read, b + 1)
                        split_block(dve, hT, x_parts, b, part_hi, part_ready, b)

                @block.gpsimd
                def _(pool):
                    power(pool, var_ready, rstd_ready)

                @block.tensor
                def _(pe):
                    pe.wait_ge(scaled, 1)
                    transposes(pe, xhat, turned, turned_read)



        with signals("x_loaded", "pool_step") as (x_loaded, pool_step), nc.Block() as block:
            @block.sync
            def _(sp):
                sp.dma_start(hT[:], d["xT"]).then_inc(x_loaded, 16)
                sp.dma_start(cols[:], d["cols"]).then_inc(x_loaded, 16)
                stream.feed(sp, 0)
                sp.wait_ge(x_loaded, 32)

            @block.gpsimd
            def _(pool):
                step = Chain(pool, pool_step)
                pool.memset(ones[:], 1.0)
                pool.memset(minus_half[:], -0.5)
                pool.memset(mask[:], 0.0)
                step(pool.memset(ident[:], 0.0))
                pool.affine_select(out=ident[:], in_=ident[:], compare_op=ALU.not_equal, fill=1.0, base=0,
                                   pattern=[[-1, P]], channel_multiplier=1)
                for o in (0, 2 * P):
                    pool.affine_select(out=mask[:, o:o + P], in_=mask[:, o:o + P], compare_op=ALU.is_ge, fill=NEG,
                                       base=0, pattern=[[-1, P]], channel_multiplier=1)


        def mixers(mem):
            x_parts = token_parts(mem)
            uT, qT, kT = (sbuf(n, [P, DK, TOKENS], mem=mem) for n in ("uT", "qT", "kT"))
            v_a = sbuf("v_a", [P, TT, D], mem=mem)
            v_b = sbuf("v_b", [P, TT, D], mem=mem)
            gating = mem.enter_context(ExitStack())
            buf, p = params("mix", gating)

            with signals("params_loaded", "x_loaded", "t_ready", "t_read", "n_ready", "n_read", "va_gelu", "var_ready",
                         "rstd_ready", "dve_step", "part_hi", "part_ready", *PARTS) as (
                    params_loaded, x_loaded, t_ready, t_read, n_ready, n_read, va_gelu, var_ready, rstd_ready, dve_step, part_hi,
                    part_ready, *sems), ExitStack() as own:
                weights = weight_parts("nnttnntttt", sems, own)
                block = own.enter_context(nc.Block())

                @block.sync
                def _(sp):
                    sp.dma_start(buf[:], d["mix"]).then_inc(params_loaded, 16)
                    stream.feed(sp, 10)
                    sp.dma_start(x[:], d["x"]).then_inc(x_loaded, 16)
                    sp.wait_ge(x_loaded, 16)

                @block.tensor
                def _(pe):
                    at_t = at_n = 0
                    for part in "nnttnntttt":
                        if part == "n":
                            at_n = parts_n(pe, weights, x_parts, at_n, n_ready, n_read, part_ready)
                        else:
                            at_t = parts_t(pe, weights, x_parts, at_t, t_ready, t_read)

                @block.scalar
                def _(act):
                    weights.high(act, 11)
                    act.wait_ge(n_read, 2)
                    act.activation(v_a[:], v_a[:], ACT.Gelu).then_inc(va_gelu, 1)
                    at = 0
                    for out, bias, func, block_of in ((uT, "b_u", ACT.Gelu, 8), (qT, "b_q", ACT.Identity, 24),
                                                      (kT, "b_k", ACT.Identity, 32)):
                        for b in range(DK):
                            weights.high(act, block_of + b + 4)
                            act.wait_ge(t_ready, at + 1)
                            act.activation(out[:, b, :], ps[:, at % 4, 0:TOKENS], func,
                                           bias=col(bias, b)).then_inc(t_read, 1)
                            at += 1

                @block.vector
                def _(dve):
                    step = Chain(dve, dve_step)
                    for b in range(DK):
                        split_block(dve, hT, x_parts, b, part_hi, part_ready, b)
                        if b % 2:
                            weights.low(dve, b // 2 + 1)
                    dve.wait_ge(params_loaded, 16)
                    for at, (out, bias, c, ahead) in enumerate(((v_a, "b_va", 0, 7), (v_a, "b_va", 1, 11),
                                                                (v_b, "b_vb", 0, 23), (v_b, "b_vb", 1, 27))):
                        weights.low(dve, ahead)
                        dve.wait_ge(n_ready, at + 1)
                        o = c * WIDE
                        dve.tensor_tensor(out[:, :, o:o + WIDE], bank_n(at), spread(p[bias][:, o:o + WIDE], 1, TT),
                                          ALU.add).then_inc(n_read, 1)
                        if at == 1:
                            weights.low(dve, 12)
                            dve.wait_ge(va_gelu, 1)
                            layer_norm(dve, step, v_a, p["ln_g"], p["ln_b"], v_a, var_ready, rstd_ready)
                    weights.low(dve, 40)

                @block.gpsimd
                def _(pool):
                    power(pool, var_ready, rstd_ready)
                    pool.wait_ge(params_loaded, 16)
                    w = p["w_s"].rearrange("p (g t) -> p g t", g=8)
                    pool.affine_select(out=w, in_=w, compare_op=ALU.is_ge, fill=0.0, base=0, pattern=[[0, 8], [1, P]],
                                       channel_multiplier=-1)

            w_s = p["w_s"].rearrange("p (g t) -> p g t", g=8)
            b_s = p["b_s"].rearrange("p (g t) -> p g t", g=8)

            with signals("mixed", "mixed_read", "gated") as (mixed, mixed_read, gated), \
                    buffer("gate", [P, 2, TOKENS], F32) as gate, nc.Block() as block:
                @block.tensor
                def _(pe):
                    for g in range(8):
                        if g >= 4:
                            pe.wait_ge(mixed_read, g - 3)
                        for t in range(TT):
                            last = pe.matmul(ps[:, g % 4, t * P:t * P + P], v_a[:, t, g * P:g * P + P], w_s[:, g, :],
                                             start=True, stop=True)
                        last.then_inc(mixed, 1)

                @block.vector
                def _(dve):
                    for g in range(8):
                        dve.wait_ge(mixed, g + 1)
                        if g >= 2:
                            dve.wait_ge(gated, g - 1)
                        dve.tensor_tensor(gate[:, g % 2, :].rearrange("p (t n) -> p t n", t=TT),
                                          ps[:, g % 4, 0:TOKENS].rearrange("p (t n) -> p t n", t=TT),
                                          spread(b_s[:, g, :], 1, TT), ALU.add).then_inc(mixed_read, 1)

                @block.gpsimd
                def _(pool):
                    for g in range(8):
                        pool.wait_ge(mixed_read, g + 1)
                        pool.tensor_tensor(uT[:, g, :], uT[:, g, :], gate[:, g % 2, :], ALU.mult).then_inc(gated, 1)

            gating.close()

            with ExitStack() as biases:
                buf_rel, p = params("rel", biases)
                with signals("params_loaded") as (params_loaded,), nc.Block() as block:
                    @block.sync
                    def _(sp):
                        sp.dma_start(buf_rel[:], d["rel"]).then_inc(params_loaded, 16)
                        sp.wait_ge(params_loaded, 16)

                rel = p["rel"].rearrange("p (h n) -> p h n", h=HEADS_A)
                scale = float(P) ** -0.5

                def scores(pe, h):
                    pe.matmul(ps[:, h % 2, 0:P], qT[:, h, 0:P], kT[:, h, 0:P], start=True, stop=True)
                    return pe.matmul(ps[:, h % 2, P:TRI], qT[:, h, P:TOKENS], kT[:, h, :], start=True, stop=True)

                def logits(dve, step, h, out):
                    step(dve.scalar_tensor_tensor(out, ps[:, h % 2, 0:TRI], scale, rel[:, h, :], ALU.mult, ALU.add))
                    return dve.tensor_tensor(out, out, mask[:], ALU.add)

                attention(HEADS_A, scores, logits, lambda h, s: v_b[:, s, h * P:h * P + P],
                          lambda h, t: ps[:, 4 + 2 * (h // 4) + t, (h % 4) * P:(h % 4) * P + P])
            projections = mem.enter_context(ExitStack())
            u_parts, o_parts = token_parts(projections), token_parts(projections)
            turn_heads(v_a, o_parts)

            mT = kT
            gaT, gbT = (v[:].rearrange("p t n -> p (t n)").rearrange("p (k n) -> p k n", k=DK) for v in (v_a, v_b))
            part_b = qT
            with signals("g_ready", "g_read", "t_ready", "t_read", "summed", "part_hi", "part_ready", "u_ready", *PARTS) as (
                    g_ready, g_read, t_ready, t_read, summed, part_hi, part_ready, u_ready, *sems), ExitStack() as own:
                weights = weight_parts("tttttttt", sems, own)
                block = own.enter_context(nc.Block())

                @block.sync
                def _(sp):
                    stream.feed(sp, 8)

                @block.tensor
                def _(pe):
                    at = 0
                    for _ in range(4):
                        at = parts_t(pe, weights, x_parts, at, g_ready, g_read)
                    pe.wait_ge(g_read, 2 * DK)
                    at = 0
                    for rhs in (u_parts, u_parts, o_parts, o_parts):
                        at = parts_t(pe, weights, rhs, at, t_ready, t_read, u_ready if at == 0 else None)

                @block.scalar
                def _(act):
                    for at in range(2 * DK):
                        out, bias = (gaT, "b_ga") if at < DK else (gbT, "b_gb")
                        weights.high(act, at + 4)
                        act.wait_ge(g_ready, at + 1)
                        act.activation(out[:, at % DK, :], ps[:, at % 4, 0:TOKENS], ACT.Sigmoid,
                                       bias=col(bias, at % DK)).then_inc(g_read, 1)
                    weights.high(act, 32)

                @block.vector
                def _(dve):
                    for b in range(DK):
                        weights.low(dve, b + 4)
                        split_block(dve, uT, u_parts, b, part_hi, u_ready, b)
                    for at in range(2 * DK):
                        b = at % DK
                        weights.low(dve, 2 * DK + at + 4)
                        dve.wait_ge(t_ready, at + 1)
                        if at < DK:
                            dve.wait_ge(g_read, b + 1)
                            dve.tensor_tensor(mT[:, b, :], ps[:, at % 4, 0:TOKENS], gaT[:, b, :], ALU.mult).then_inc(t_read, 1)
                        else:
                            dve.tensor_tensor(part_b[:, b, :], ps[:, at % 4, 0:TOKENS], gbT[:, b, :], ALU.mult).then_inc(t_read, 1)
                            if b > 0:
                                dve.wait_ge(summed, b)
                                split_block(dve, mT, x_parts, b - 1, part_hi, part_ready, DK + b - 1)
                    dve.wait_ge(summed, DK)
                    split_block(dve, mT, x_parts, DK - 1, part_hi, part_ready, 2 * DK - 1)

                @block.gpsimd
                def _(pool):
                    for b in range(DK):
                        pool.wait_ge(t_read, DK + b + 1)
                        pool.tensor_tensor(mT[:, b, :], mT[:, b, :], part_b[:, b, :], ALU.add).then_inc(summed, 1)

            projections.close()
            buf_ln, p = params("ln1", mem)

            with signals("params_loaded", "n_ready", "n_read", "var_ready", "rstd_ready", "dve_step", "normed", "turned",
                         "turned_read", *PARTS) as (
                    params_loaded, n_ready, n_read, var_ready, rstd_ready, dve_step, normed, turned, turned_read, *sems), \
                    ExitStack() as own:
                weights = weight_parts("nn", sems, own)
                block = own.enter_context(nc.Block())

                @block.sync
                def _(sp):
                    sp.dma_start(buf_ln[:], d["ln1"]).then_inc(params_loaded, 16)
                    stream.feed(sp, 2)

                @block.tensor
                def _(pe):
                    for at in range(2):
                        parts_n(pe, weights, x_parts, at, n_ready, n_read)
                    pe.wait_ge(normed, 1)
                    transposes(pe, x, turned, turned_read)

                @block.vector
                def _(dve):
                    step = Chain(dve, dve_step)
                    weights.low(dve, 8)
                    for at in range(2):
                        dve.wait_ge(n_ready, at + 1)
                        o = x[:, :, at * WIDE:at * WIDE + WIDE]
                        step(dve.scalar_tensor_tensor(o, o, ALPHA, bank_n(at), ALU.mult, ALU.add))
                    dve.wait_ge(params_loaded, 16)
                    layer_norm(dve, step, x, p["g"], p["b"], x, var_ready, rstd_ready).then_inc(normed, 1)

                @block.gpsimd
                def _(pool):
                    power(pool, var_ready, rstd_ready)

                @block.scalar
                def _(act):
                    weights.high(act, 8)
                    copy_turned(act, hT, turned, turned_read)

        def copy_turned(act, out, turned, turned_read):
            for b in range(DK):
                act.wait_ge(turned, b + 1)
                act.activation(out[:, b, :], ps[:, b % 4, 0:TOKENS], ACT.Copy).then_inc(turned_read, 1)

        def high_turned(act, parts, turned, high_ready):
            for b in range(DK):
                act.wait_ge(turned, b + 1)
                act.activation(parts[0][:, b, :], ps[:, b % 4, 0:TOKENS], ACT.Copy).then_inc(high_ready, 1)

        def low_turned(dve, parts, high_ready, turned_read):
            for b in range(DK):
                dve.wait_ge(high_ready, b + 1)
                dve.tensor_tensor(parts[1][:, b, :], ps[:, b % 4, 0:TOKENS], parts[0][:, b, :], ALU.subtract).then_inc(turned_read, 1)

        def turn_heads(o, parts):
            with signals("copied", "turned", "high_ready", "turned_read") as (copied, turned, high_ready, turned_read), \
                    nc.Block() as block:
                @block.vector
                def _(dve):
                    for t in range(TT):
                        dve.tensor_copy(halves(o[:, t, :]), y_banks(t)).then_inc(copied, 1)
                    low_turned(dve, parts, high_ready, turned_read)

                @block.tensor
                def _(pe):
                    pe.wait_ge(copied, TT)
                    transposes(pe, o, turned, turned_read)

                @block.scalar
                def _(act):
                    high_turned(act, parts, turned, high_ready)

        def attention(n, scores, logits, values, out, gate=None, starts=True):
            with signals("scored", "biased", "exped", "probs_ready", "probs_turned", "turned_copied", "weighted", "dve_step") as (
                    scored, biased, exped, probs_ready, probs_turned, turned_copied, weighted, dve_step), ExitStack() as mem:
                prob = sbuf("prob", [P, 2, TRI], mem=mem)
                prob_t = sbuf("prob_t", [P, 2, TRI], mem=mem)
                top = sbuf("top", [P, 2, TT], mem=mem)
                total = sbuf("total", [P, 2, TT], mem=mem)
                part = (slice(0, P), slice(P, TRI))
                block = mem.enter_context(nc.Block())

                @block.tensor
                def _(pe):
                    for i in range(-1, n + 2):
                        if i + 1 < n:
                            if i >= 1:
                                pe.wait_ge(biased, i)
                            scores(pe, i + 1).then_inc(scored, 1)
                        j = i - 1
                        if 0 <= j < n:
                            pe.wait_ge(probs_ready, j + 1)
                            if j >= 2:
                                pe.wait_ge(turned_copied, j - 1)
                            for b in range(3):
                                last = pe.transpose(ps[:, 2 + j % 2, b * P:b * P + P], prob[:, j % 2, b * P:b * P + P], ident[:])
                            last.then_inc(probs_turned, 1)
                        j = i - 2
                        if j >= 0:
                            pe.wait_ge(turned_copied, j + 1)
                            t = prob_t[:, j % 2, :]
                            pe.matmul(out(j, 0), t[:, 0:P], values(j, 0), start=starts, stop=True, skip_group_check=True)
                            pe.matmul(out(j, 1), t[:, P:2 * P], values(j, 0), start=starts, stop=False, skip_group_check=True)
                            pe.matmul(out(j, 1), t[:, 2 * P:TRI], values(j, 1), start=False, stop=True,
                                      skip_group_check=True).then_inc(weighted, 1)

                @block.vector
                def _(dve):
                    step = Chain(dve, dve_step)
                    for i in range(n + 1):
                        if i < n:
                            dve.wait_ge(scored, i + 1)
                            if i >= 2:
                                dve.wait_ge(probs_turned, i - 1)
                            step(logits(dve, step, i, prob[:, i % 2, :]))
                            for t in range(TT):
                                last = dve.tensor_reduce(top[:, i % 2, t:t + 1], prob[:, i % 2, part[t]], AX.X, ALU.max,
                                                         negate=True)
                            last.then_inc(biased, 1)
                        j = i - 1
                        if j >= 0:
                            dve.wait_ge(exped, j + 1)
                            step(dve.reciprocal(total[:, j % 2, :], total[:, j % 2, :]))
                            if gate is not None:
                                step(dve.tensor_tensor(total[:, j % 2, :], total[:, j % 2, :], gate(j), ALU.mult))
                            for t in range(TT):
                                o = prob[:, j % 2, part[t]]
                                last = dve.tensor_scalar(o, o, total[:, j % 2, t:t + 1], None, ALU.mult)
                            last.then_inc(probs_ready, 1)

                @block.scalar
                def _(act):
                    for i in range(n + 2):
                        if i < n:
                            act.wait_ge(biased, i + 1)
                            for t in range(TT):
                                o = prob[:, i % 2, part[t]]
                                last = act.activation(o, o, ACT.Exp, bias=top[:, i % 2, t:t + 1],
                                                      accum_out=total[:, i % 2, t:t + 1])
                            last.then_inc(exped, 1)
                        j = i - 1
                        if 0 <= j < n:
                            act.wait_ge(probs_turned, j + 1)
                            if j >= 2:
                                act.wait_ge(weighted, j - 1)
                            act.activation(prob_t[:, j % 2, :], ps[:, 2 + j % 2, 0:TRI], ACT.Copy).then_inc(turned_copied, 1)


        def feed_forward(kind, tiles, act_func, x_parts, gates=1, starts=True, stops=True, scale_by=None, work=None):
            per_chunk = 2 if gates == 1 else 1
            n_up = gates * D
            size = n_up + D
            turn = RING * per_chunk
            first = stream.taken
            n_chunks = tiles // per_chunk
            head = 2
            with signals("up_ready", "acted", "scaled_ready", "full_ready", "high_ready", "hidden_ready", "down_done",
                         "up_hi_ready", "up_split", "down_hi_ready", "down_split") as (
                    up_ready, acted, scaled_ready, full_ready, high_ready, hidden_ready, down_done,
                    up_hi_ready, up_split, down_hi_ready, down_split), \
                    buffer("hidden_hi", [P, 2, TOKENS], F32R) as hidden_hi, \
                    buffer("hidden_lo", [P, 2, TOKENS], F32R) as hidden_lo, \
                    buffer("up_hi", [P, 2, n_up], F32R) as up_hi, buffer("up_lo", [P, 2, n_up], F32R) as up_lo, \
                    buffer("down_hi", [P, 2, D], F32R) as down_hi, buffer("down_lo", [P, 2, D], F32R) as down_lo, \
                    ExitStack() as mem:
                x_hi, x_lo = x_parts
                if work is None:
                    work = sbuf("work", [P, 2, 2, TOKENS], mem=mem)
                act_out, full = work[:, 0], work[:, 1]
                block = mem.enter_context(nc.Block())

                def later(value, i):
                    return value if i is None else i * turn + value

                def raw(j):
                    o = j % per_chunk * size
                    return stream.slot(first + j // per_chunk)[:, o:o + size]

                def run(eng, step, n, times=1):
                    span = turn * times
                    turns = max((n - head) // span, 0)
                    for j in range(min(head, n)):
                        step(j)
                    if turns:
                        with eng.Fori(0, turns) as i:
                            for j in range(head, head + span):
                                step(j, i * times if times > 1 else i)
                    for j in range(head + turns * span, n):
                        step(j)

                @block.sync
                def _(sp):
                    stream.feed(sp, n_chunks)

                @block.tensor
                def _(pe):
                    def up(j, i=None):
                        hi, lo = up_hi[:, j % 2, :], up_lo[:, j % 2, :]
                        pe.wait_ge(up_split, later(j + 1, i))
                        if i is not None or j >= 2:
                            pe.wait_ge(hidden_ready, later(j - 1, i))
                        for g in range(gates):
                            out = ps[:, j % 2, g * TOKENS:g * TOKENS + TOKENS]
                            for k in range(DK):
                                o = g * D + k * P
                                last = pe.matmul(out, hi[:, o:o + P], x_hi[:, k, :], start=(k == 0), stop=False)
                                if g == 0 and k == 0 and i is None and j == 0:
                                    stream.release(last)
                                pe.matmul(out, hi[:, o:o + P], x_lo[:, k, :], start=False, stop=False)
                                last = pe.matmul(out, lo[:, o:o + P], x_hi[:, k, :], start=False, stop=(k == DK - 1))
                        last.then_inc(up_ready, 1)

                    def down(j, i=None):
                        hi, lo = down_hi[:, j % 2, :], down_lo[:, j % 2, :]
                        pe.wait_ge(down_split, later(j + 1, i))
                        pe.wait_ge(hidden_ready, later(j + 1, i))
                        for t in range(TT):
                            tokens = slice(t * P, t * P + P)
                            for c in range(2):
                                o = c * WIDE
                                out = ps[:, 4 + 2 * c + t, :]
                                last = pe.matmul(out, hidden_hi[:, j % 2, tokens], hi[:, o:o + WIDE],
                                                 start=(starts and i is None and j == 0), stop=False, skip_group_check=True)
                                if t == 0 and c == 0 and j % per_chunk == per_chunk - 1:
                                    last.then_inc(used, 1)
                                pe.matmul(out, hidden_hi[:, j % 2, tokens], lo[:, o:o + WIDE], start=False, stop=False,
                                          skip_group_check=True)
                            for c in range(2):
                                o = c * WIDE
                                last = pe.matmul(ps[:, 4 + 2 * c + t, :], hidden_lo[:, j % 2, tokens], hi[:, o:o + WIDE], start=False,
                                                 stop=(stops and i is None and j == tiles - 1), skip_group_check=True)
                        last.then_inc(down_done, 1)

                    def step(j, i=None):
                        up(j + 1, i)
                        down(j, i)

                    up(0)
                    run(pe, step, tiles - 1)
                    down(tiles - 1)
                    stream.taken += n_chunks
                    stream.pending = False

                @block.scalar
                def _(act):
                    def split_up(j, i=None):
                        if j % per_chunk == 0:
                            stream.wait(act, first + j // per_chunk, i)
                        act.activation(up_hi[:, j % 2, :], raw(j)[:, 0:n_up], ACT.Copy).then_inc(up_hi_ready, 1)

                    def split_down(j, i=None):
                        if i is not None or j >= 2:
                            act.wait_ge(down_done, later(j - 1, i))
                        act.activation(down_hi[:, j % 2, :], raw(j)[:, n_up:size], ACT.Copy).then_inc(down_hi_ready, 1)

                    def step(j, i=None):
                        act.wait_ge(up_ready, later(j + 1, i))
                        if i is not None or j >= 2:
                            act.wait_ge(hidden_ready, later(j - 1, i))
                        act.activation(act_out[:, j % 2, :], ps[:, j % 2, 0:TOKENS], act_func).then_inc(acted, 1)
                        if i is not None or j + 2 < tiles:
                            split_up(j + 2, i)
                        if i is not None or j + 1 < tiles:
                            split_down(j + 1, i)

                    split_up(0)
                    split_up(1)
                    split_down(0)
                    run(act, step, tiles - 2)
                    for j in range(tiles - 2, tiles):
                        step(j)

                @block.vector
                def _(dve):
                    def split_up(j, i=None):
                        dve.wait_ge(up_hi_ready, later(j + 1, i))
                        dve.tensor_tensor(up_lo[:, j % 2, :], raw(j)[:, 0:n_up], up_hi[:, j % 2, :], ALU.subtract).then_inc(up_split, 1)

                    def split_down(j, i=None):
                        dve.wait_ge(down_hi_ready, later(j + 1, i))
                        dve.tensor_tensor(down_lo[:, j % 2, :], raw(j)[:, n_up:size], down_hi[:, j % 2, :],
                                          ALU.subtract).then_inc(down_split, 1)

                    def step(j, i=None):
                        b = j % 2
                        dve.wait_ge(acted, later(j + 1, i))
                        if i is not None or j >= 2:
                            dve.wait_ge(down_done, later(j - 1, i))
                        if kind == "relu2":
                            ins = dve.tensor_tensor(full[:, b, :], act_out[:, b, :], act_out[:, b, :], ALU.mult)
                        elif kind == "peer":
                            gate = scale_by[:, j, :] if i is None else \
                                scale_by[:, bass.ds(i * turn + j, 1), :].rearrange("p a n -> p (a n)")
                            ins = dve.tensor_tensor(full[:, b, :], act_out[:, b, :], gate, ALU.mult)
                        elif kind == "swiglu":
                            ins = dve.tensor_tensor(full[:, b, :], act_out[:, b, :], ps[:, b, TOKENS:2 * TOKENS], ALU.mult)
                        else:
                            dve.tensor_tensor(act_out[:, b, :], act_out[:, b, :], scale_by[:, j % EXPERTS, :],
                                              ALU.mult).then_inc(scaled_ready, 1)
                            dve.wait_ge(scaled_ready, later(j + 1, i))
                            ins = dve.tensor_tensor(full[:, b, :], act_out[:, b, :], ps[:, b, TOKENS:2 * TOKENS], ALU.mult)
                        ins.then_inc(full_ready, 1)
                        dve.wait_ge(full_ready, later(j + 1, i))
                        dve.tensor_copy(hidden_hi[:, b, :], full[:, b, :]).then_inc(high_ready, 1)
                        dve.wait_ge(high_ready, later(j + 1, i))
                        dve.tensor_tensor(hidden_lo[:, b, :], full[:, b, :], hidden_hi[:, b, :], ALU.subtract).then_inc(hidden_ready, 1)
                        if i is not None or j + 2 < tiles:
                            split_up(j + 2, i)
                        if i is not None or j + 1 < tiles:
                            split_down(j + 1, i)

                    split_up(0)
                    split_up(1)
                    split_down(0)
                    run(dve, step, tiles - 2, times=EXPERTS // turn if kind == "moe" else 1)
                    for j in range(tiles - 2, tiles):
                        step(j)


        def peer(mem):
            expert = sbuf("expert", [P, 3, TOKENS], mem=mem)
            key_no = sbuf("key_no", [P, KEYS], mem=mem)
            x_parts = token_parts(mem)
            groups = PEER_HEADS * 2
            lists = PEER_HEADS * TOPK
            with ExitStack() as route:
                buf, p = params("peer", route)
                rest = sbuf("rest", [P, TT, D], mem=route)
                qT = sbuf("qT", [P, groups, TOKENS], mem=route)
                score = sbuf("score", [P, TT, groups, KEYS], mem=route)
                pT = p["pT"].rearrange("p (k n) -> p k n", k=2)

                with signals("params_loaded", "n_ready", "n_read", "t_ready", "t_read", "gate_biased", "gate_ready", "dve_step",
                             "part_hi", "part_ready", *PARTS) as (
                        params_loaded, n_ready, n_read, t_ready, t_read, gate_biased, gate_ready, dve_step, part_hi, part_ready,
                        *sems), ExitStack() as own:
                    weights = weight_parts("nn.tttt", sems, own)
                    block = own.enter_context(nc.Block())

                    @block.sync
                    def _(sp):
                        sp.dma_start(buf[:], d["peer"]).then_inc(params_loaded, 16)
                        stream.feed(sp, 7)

                    @block.tensor
                    def _(pe):
                        at = 0
                        for _ in range(2):
                            at = parts_n(pe, weights, x_parts, at, n_ready, n_read, part_ready)
                        pe.wait_ge(params_loaded, 16)
                        c = stream.take(pe)
                        w = stream.slot(c)
                        for h in range(2):
                            pe.wait_ge(n_read, h + 1)
                            for t in range(TT):
                                for k in range(2):
                                    last = pe.matmul(ps[:, 4 + 2 * h + t, :], pT[:, k, t * P:t * P + P],
                                                     w[:, k * D + h * WIDE:k * D + h * WIDE + WIDE], start=(k == 0), stop=(k == 1))
                                    if h + t + k == 0:
                                        stream.release(last)
                            last.then_inc(n_ready, 1)
                        stream.pending = True
                        at_t = 0
                        for _ in range(4):
                            at_t = parts_t(pe, weights, x_parts, at_t, t_ready, t_read)

                    @block.scalar
                    def _(act):
                        weights.high(act, 11)
                        act.wait_ge(gate_biased, 1)
                        act.activation(rest[:], rest[:], ACT.Sigmoid).then_inc(gate_ready, 1)
                        for b in range(groups):
                            weights.high(act, 8 + b + 4)
                            act.wait_ge(t_ready, b + 1)
                            act.activation(qT[:, b, :], ps[:, b % 4, 0:TOKENS], ACT.Copy).then_inc(t_read, 1)

                    @block.vector
                    def _(dve):
                        step = Chain(dve, dve_step)
                        for b in range(DK):
                            split_block(dve, hT, x_parts, b, part_hi, part_ready, b)
                            if b % 2:
                                weights.low(dve, b // 2 + 1)
                        dve.wait_ge(params_loaded, 16)
                        for h in range(2):
                            o = slice(h * WIDE, h * WIDE + WIDE)
                            weights.low(dve, 7 + 4 * h)
                            dve.wait_ge(n_ready, h + 1)
                            last = dve.tensor_tensor(rest[:, :, o], bank_n(h), spread(p["b_gate"][:, o], 1, TT), ALU.add)
                            last.then_inc(n_read, 1)
                        dve.wait_ge(n_read, 2)
                        dve.memset(spare[:], 0.0).then_inc(gate_biased, 1)
                        weights.low(dve, 12)
                        dve.wait_ge(gate_ready, 1)
                        for h in range(2):
                            o = slice(h * WIDE, h * WIDE + WIDE)
                            dve.wait_ge(n_ready, 3 + h)
                            step(dve.tensor_tensor(rest[:, :, o], rest[:, :, o], bank_n(h), ALU.mult))
                        step(dve.scalar_tensor_tensor(x[:, :, :], x[:, :, :], ALPHA, rest[:, :, :], ALU.mult, ALU.add))
                        weights.low(dve, 24)

                keys = p["keys"].rearrange("p (h n) -> p h n", h=2)
                with signals("scored", "score_read") as (scored, score_read), nc.Block() as block:
                    @block.tensor
                    def _(pe):
                        for n in range(TT * groups // 4):
                            t, g = n // 4, n % 4 * 4
                            if n >= 4:
                                pe.wait_ge(score_read, n - 3)
                            for b in range(4):
                                last = pe.matmul(ps[:, n % 4, b * KEYS:b * KEYS + KEYS], qT[:, g + b, t * P:t * P + P],
                                                 keys[:, (g + b) % 2, :], start=True, stop=True)
                            last.then_inc(scored, 1)

                    @block.scalar
                    def _(act):
                        for n in range(TT * groups // 4):
                            act.wait_ge(scored, n + 1)
                            act.activation(score[:, n // 4, n % 4 * 4:n % 4 * 4 + 4, :],
                                           ps[:, n % 4, :].rearrange("p (b n) -> p b n", b=4), ACT.Copy).then_inc(score_read, 1)

                    @block.gpsimd
                    def _(pool):
                        pool.iota(key_no[:], pattern=[[1, KEYS]], base=0, channel_multiplier=0,
                                  allow_small_or_imprecise_dtypes=True)

                found = sbuf("found", [P, TT, 3, lists], mem=route)
                left = sbuf("left", [P, groups, KEYS], mem=route)
                best = sbuf("best", [P, groups, TOPK], mem=route)
                best_no = sbuf("best_no", [P, groups, TOPK], U32, mem=route)
                best_key = sbuf("best_key", [P, groups, TOPK], mem=route)
                sums = sbuf("sums", [P, PEER_HEADS, TOPK, TOPK], mem=route)
                top = sbuf("top", [P, PEER_HEADS, TOPK], mem=route)
                top_no = sbuf("top_no", [P, PEER_HEADS, TOPK], U32, mem=route)
                top_part = sbuf("top_part", [P, 2, PEER_HEADS, TOPK], U32, mem=route)
                top_pos = sbuf("top_pos", [P, 2, PEER_HEADS, TOPK], mem=route)
                gate_sum = sbuf("gate_sum", [P, PEER_HEADS], mem=route)

                cond_at = sbuf("cond_at", [P, DK, 2 * ADA_ROWS - 1], mem=route)

                with signals("dve_step", "top_ready", "exped", "found_ready", "turned", "zeroed", "cond_ready", "mod_ready") as (
                        dve_step, top_ready, exped, found_ready, turned, zeroed, cond_ready, mod_ready), nc.Block() as block:
                    @block.sync
                    def _(sp):
                        stream.feed(sp, ADA_ROWS)

                    @block.gpsimd
                    def _(pool):
                        pool.memset(cond_at[:], 0.0).then_inc(zeroed, 1)

                    @block.vector
                    def _(dve):
                        step = Chain(dve, dve_step)

                        def best_16(values, n, out, out_no, rest_of):
                            for g in range(n):
                                last = dve.max(out[:, g, 0:8], values(g))
                            step(last)
                            for g in range(n):
                                dve.max_index(out_no[:, g, 0:8], out[:, g, 0:8], values(g))
                                last = dve.match_replace(rest_of(g), out[:, g, 0:8], values(g), -3.0e38)
                            step(last)
                            for g in range(n):
                                last = dve.max(out[:, g, 8:16], rest_of(g))
                            step(last)
                            for g in range(n):
                                last = dve.max_index(out_no[:, g, 8:16], out[:, g, 8:16], rest_of(g))
                            step(last)

                        for t in range(TT):
                            best_16(lambda g: score[:, t, g, :], groups, best, best_no, lambda g: left[:, g, :])
                            step(dve.tensor_copy(best_key[:], best_no[:]))
                            halves_s = best[:].rearrange("p (h a) k -> p h a k", a=2)
                            halves_k = best_key[:].rearrange("p (h a) k -> p h a k", a=2)
                            step(dve.tensor_tensor(sums[:], spread(halves_s[:, :, 0, :], 3, TOPK),
                                                   spread(halves_s[:, :, 1, :], 2, TOPK), ALU.add))
                            flat = sums[:].rearrange("p h a b -> p h (a b)")
                            rest_sums = left[:].rearrange("p (h a) n -> p h (a n)", a=2)
                            best_16(lambda h: flat[:, h, :], PEER_HEADS, top, top_no, lambda h: rest_sums[:, h, :])
                            g = found[:, t, 2, :].rearrange("p (h k) -> p h k", k=TOPK)
                            dve.tensor_tensor(g, top[:], top[:, :, 0:1].broadcast_to([P, PEER_HEADS, TOPK]),
                                              ALU.subtract).then_inc(top_ready, 1)
                            dve.tensor_scalar(top_part[:, 0], top_no[:], 4, None, ALU.logical_shift_right)
                            step(dve.tensor_scalar(top_part[:, 1], top_no[:], 15, None, ALU.bitwise_and))
                            step(dve.tensor_copy(top_pos[:], top_part[:]))
                            for a in range(2):
                                step(dve.tensor_tensor(sums[:], spread(top_pos[:, a], 3, TOPK),
                                                       spread(spread(key_no[:, 0:TOPK], 1, TOPK), 1, PEER_HEADS), ALU.is_equal))
                                step(dve.tensor_tensor(sums[:], sums[:], spread(halves_k[:, :, a, :], 2, TOPK), ALU.mult))
                                step(dve.tensor_reduce(found[:, t, a, :].rearrange("p (h k) -> p h k", k=TOPK), sums[:], AX.X, ALU.add))
                            dve.wait_ge(exped, t + 1)
                            step(dve.tensor_reduce(gate_sum[:], g, AX.X, ALU.add))
                            step(dve.reciprocal(gate_sum[:], gate_sum[:]))
                            dve.tensor_tensor(g, g, spread(gate_sum[:], 2, TOPK), ALU.mult).then_inc(found_ready, 1)

                    @block.scalar
                    def _(act):
                        act.wait_ge(zeroed, 1)
                        act.activation(cond_at[:, :, ADA_ROWS - 1], cols[:, offsets["cols"]["cond"][0]:][:, 0:DK],
                                       ACT.Silu).then_inc(cond_ready, 1)
                        for t in range(TT):
                            act.wait_ge(top_ready, t + 1)
                            act.activation(found[:, t, 2, :], found[:, t, 2, :], ACT.Exp).then_inc(exped, 1)
                        act.wait_ge(mod_ready, 1)
                        act.activation(mod[:], ps[0:ADA_ROWS, 4, :], ACT.Copy)
                        act.wait_ge(turned, 1)
                        for a in range(3):
                            act.activation(expert[:, a, :], ps[:, a, 0:TOKENS], ACT.Copy)

                    @block.tensor
                    def _(pe):
                        pe.wait_ge(cond_ready, 1)
                        for n in range(ADA_ROWS):
                            w = stream.slot(stream.take(pe))
                            for k in range(DK):
                                last = pe.matmul(ps[0:ADA_ROWS, 4, :], cond_at[:, k, ADA_ROWS - 1 - n:2 * ADA_ROWS - 1 - n],
                                                 w[:, k * WIDE:k * WIDE + WIDE], start=(n + k == 0),
                                                 stop=(n == ADA_ROWS - 1 and k == DK - 1))
                                if k == 0:
                                    stream.release(last)
                            stream.pending = True
                        last.then_inc(mod_ready, 1)
                        for t in range(TT):
                            pe.wait_ge(found_ready, t + 1)
                            for a in range(3):
                                last = pe.transpose(ps[:, a, t * P:t * P + P], found[:, t, a, :], ident[:])
                        last.then_inc(turned, 1)

            half = KEYS // 2
            with ExitStack() as dense:
                gates = sbuf("gates", [P, half, TOKENS], mem=dense)
                work = hT[:, 0:4, :].rearrange("p (a b) n -> p a b n", a=2)
                for part in range(2):
                    spread_gates(expert, key_no, gates, part * half)
                    feed_forward("peer", half, ACT.Gelu, x_parts, scale_by=gates, starts=(part == 0), stops=(part == 1),
                                 work=work)

            buf_2, p = params("ln2", mem)
            with signals("params_loaded", "var_ready", "rstd_ready", "dve_step") as (
                    params_loaded, var_ready, rstd_ready, dve_step), nc.Block() as block:
                @block.sync
                def _(sp):
                    sp.dma_start(buf_2[:], d["ln2"]).then_inc(params_loaded, 16)

                @block.vector
                def _(dve):
                    step = Chain(dve, dve_step)
                    for t in range(TT):
                        last = dve.tensor_tensor(halves(x[:, t, :]), halves(x[:, t, :]), y_banks(t), ALU.add)
                    step(last)
                    dve.wait_ge(params_loaded, 16)
                    layer_norm(dve, step, x, p["g"], p["b"], x, var_ready, rstd_ready)

                @block.gpsimd
                def _(pool):
                    power(pool, var_ready, rstd_ready)

        def spread_gates(expert, key_no, gates, first):
            n = gates.shape[1]
            few = WIDE // n
            steps = TOKENS // few
            with signals("dve_step", "parts_ready", "columns_ready", "rows_ready", "second_ready", "third_ready", "placed",
                         "placed_read") as (
                    dve_step, parts_ready, columns_ready, rows_ready, second_ready, third_ready, placed, placed_read), \
                    buffer("gate_part", [P, 3, TOKENS], BF16) as gate_part, buffer("gate_rest", [P, 3, TOKENS]) as gate_rest, \
                    buffer("row_hot", [P, 4, few, KEYS], BF16) as row_hot, \
                    buffer("col_hot", [P, 4, few, n], BF16) as col_hot, \
                    buffer("col_gate", [P, 4, 3, few, n], BF16) as col_gate, nc.Block() as block:

                def tokens(s):
                    return slice(s * few, s * few + few)

                def count(s, i):
                    return s if i is None else i * 4 + s

                @block.vector
                def _(dve):
                    step = Chain(dve, dve_step)
                    left = expert[:, 2, :]
                    for a in range(3):
                        step(dve.tensor_copy(gate_part[:, a, :], left))
                        if a < 2:
                            step(dve.tensor_tensor(gate_rest[:, a, :], left, gate_part[:, a, :], ALU.subtract))
                            left = gate_rest[:, a, :]
                    dve.tensor_copy(gate_rest[:, 2, :], gate_part[:, 2, :]).then_inc(parts_ready, 1)
                    for s in range(steps):
                        b = s % 4
                        if s >= 4:
                            dve.wait_ge(placed, s - 3)
                        dve.tensor_tensor(col_hot[:, b], spread(key_no[:, first:first + n], 1, few), spread(expert[:, 1, tokens(s)], 2, n),
                                          ALU.is_equal).then_inc(columns_ready, 1)
                        dve.tensor_tensor(row_hot[:, b], spread(key_no[:, :], 1, few), spread(expert[:, 0, tokens(s)], 2, KEYS),
                                          ALU.is_equal)
                        dve.wait_ge(columns_ready, s + 1)
                        dve.tensor_tensor(col_gate[:, b, 0], col_hot[:, b], spread(gate_part[:, 0, tokens(s)], 2, n),
                                          ALU.mult).then_inc(rows_ready, 1)

                @block.gpsimd
                def _(pool):
                    pool.wait_ge(parts_ready, 1)
                    for s in range(steps):
                        pool.wait_ge(columns_ready, s + 1)
                        pool.tensor_tensor(col_gate[:, s % 4, 1], col_hot[:, s % 4], spread(gate_part[:, 1, tokens(s)], 2, n),
                                           ALU.mult).then_inc(second_ready, 1)

                @block.scalar
                def _(act):
                    def weigh(s):
                        act.wait_ge(columns_ready, s + 1)
                        for m in range(few):
                            token = s * few + m
                            last = act.activation(col_gate[:, s % 4, 2, m], col_hot[:, s % 4, m], ACT.Copy,
                                                  scale=gate_rest[:, 2, token:token + 1])
                        last.then_inc(third_ready, 1)

                    def read(s):
                        act.wait_ge(placed, s + 1)
                        act.activation(gates[:, :, tokens(s)].rearrange("p j m -> p m j"),
                                       ps[:, s % 4, 0:few * n].rearrange("p (m j) -> p m j", m=few), ACT.Copy).then_inc(placed_read, 1)

                    act.wait_ge(parts_ready, 1)
                    for s in range(steps + 2):
                        if s < steps:
                            weigh(s)
                        if s >= 2:
                            read(s - 2)

                @block.tensor
                def _(pe):
                    def place(s, i=None):
                        for ready in (rows_ready, second_ready, third_ready):
                            pe.wait_ge(ready, count(s + 1, i))
                        if i is not None:
                            pe.wait_ge(placed_read, count(s - 3, i))
                        for m in range(few):
                            for a in range(3):
                                last = pe.matmul(ps[:, s, m * n:m * n + n], row_hot[:, s, m, :], col_gate[:, s, a, m, :],
                                                 start=(a == 0), stop=(a == 2))
                        last.then_inc(placed, 1)

                    for s in range(4):
                        place(s)
                    with pe.Fori(1, steps // 4) as i:
                        for s in range(4):
                            place(s, i)


        def post_norm(g, params_loaded=None, mixer=None):
            with signals("n_ready", "n_read", "squared", "var_ready", "rstd_ready", "dve_step", *PARTS) as (
                    n_ready, n_read, squared, var_ready, rstd_ready, dve_step, *sems), ExitStack() as own:
                scaled_y = sbuf("scaled_y", [P, D], mem=own)
                junk = sbuf("junk", [P, TT, D], mem=own)
                if mixer is not None:
                    weights = weight_parts("nn", sems, own)
                block = own.enter_context(nc.Block())
                if mixer is not None:
                    @block.sync
                    def _(sp):
                        stream.feed(sp, 2)

                    @block.tensor
                    def _(pe):
                        for at in range(2):
                            parts_n(pe, weights, mixer, at, n_ready, n_read)

                @block.scalar
                def _(act):
                    if mixer is not None:
                        weights.high(act, 8)
                        act.wait_ge(n_ready, 2)
                    for t in range(TT):
                        last = act.activation(halves(junk[:, t, :]), y_banks(t), ACT.Square, accum_out=squares[:, t:t + 1])
                    last.then_inc(squared, 1)

                @block.vector
                def _(dve):
                    step = Chain(dve, dve_step)
                    if mixer is not None:
                        weights.low(dve, 8)
                    dve.wait_ge(squared, 1)
                    dve.tensor_scalar(spare[:], squares[:], 1.0 / D, RMS_EPS, ALU.mult, ALU.add).then_inc(var_ready, 1)
                    dve.wait_ge(rstd_ready, 1)
                    for t in range(TT):
                        step(dve.scalar_tensor_tensor(halves(scaled_y[:]), y_banks(t), rstd[:, t:t + 1], halves(g), ALU.mult, ALU.mult))
                        step(dve.tensor_tensor(x[:, t, :], x[:, t, :], scaled_y[:], ALU.add))

                @block.gpsimd
                def _(pool):
                    power(pool, var_ready, rstd_ready)

        def nsa(mem):
            buf, p = params("nsa", mem)
            x_parts = token_parts(mem)
            pre_norm(lambda b: col("norm_g", b), x_parts)

            with ExitStack() as mix:
                n_rope = 14
                qk = sbuf("qk", [P, n_rope, TOKENS], mem=mix)
                v_cmp_t = sbuf("v_cmp_t", [P, 2, TOKENS], mem=mix)
                v_tok = sbuf("v_tok", [P, TT, 2, GROUPS, HD], mem=mix)
                branch = sbuf("branch", [P, TT, 16, 3], mem=mix)

                rot = sbuf("rot", [P, P], mem=mix)
                shift = sbuf("shift", [P, TOKENS], mem=mix)
                cmp_mask = sbuf("cmp_mask", [P, TT, N_CMP], mem=mix)
                cmp_seen = sbuf("cmp_seen", [P, TT], mem=mix)
                own_head = sbuf("own_head", [P, 8], mem=mix)

                with signals("params_loaded", "t_ready", "t_read", "n_ready", "n_read", "gates_copied", "pool_step",
                             *PARTS) as (
                        params_loaded, t_ready, t_read, n_ready, n_read, gates_copied, pool_step, *sems), ExitStack() as own:
                    weights = weight_parts("ttttn.", sems, own)
                    block = own.enter_context(nc.Block())

                    @block.sync
                    def _(sp):
                        sp.dma_start(buf[:], d["nsa"]).then_inc(params_loaded, 16)
                        stream.feed(sp, 6)
                        sp.wait_ge(params_loaded, 16)

                    @block.tensor
                    def _(pe):
                        at = 0
                        for _ in range(4):
                            at = parts_t(pe, weights, x_parts, at, t_ready, t_read)
                        parts_n(pe, weights, x_parts, 0, n_ready, n_read)
                        product_n(pe, hT, 1, n_ready, n_read)

                    @block.scalar
                    def _(act):
                        for at in range(16):
                            weights.high(act, at + 4)
                            out = qk[:, at, :] if at < n_rope else v_cmp_t[:, at - n_rope, :]
                            act.wait_ge(t_ready, at + 1)
                            act.activation(out, ps[:, at % 4, 0:TOKENS], ACT.Copy).then_inc(t_read, 1)
                        weights.high(act, 20)
                        act.wait_ge(gates_copied, 1)
                        act.activation(branch[:], branch[:], ACT.Sigmoid)

                    @block.vector
                    def _(dve):
                        weights.low(dve, 20)
                        dve.wait_ge(n_ready, 1)
                        dve.tensor_copy(v_tok[:].rearrange("p t a g n -> p t (a g n)"), bank_n(0)).then_inc(n_read, 1)
                        dve.wait_ge(n_ready, 2)
                        dve.tensor_copy(branch[:].rearrange("p t h a -> p t (h a)"), bank_n(1, 48)).then_inc(gates_copied, 1)

                    @block.gpsimd
                    def _(pool):
                        step = Chain(pool, pool_step)
                        pool.memset(rot[:], 0.0)
                        pool.memset(shift[:], 0.0)
                        pool.memset(cmp_mask[:], 0.0)
                        pool.memset(cmp_seen[:], 1.0)
                        step(pool.memset(own_head[:], 1.0))
                        r = rot[:].rearrange("p (h a n) -> p h a n", h=2, a=2)
                        for a, sign in ((0, -1.0), (1, 1.0)):
                            pool.affine_select(out=r[:, :, a, :], in_=r[:, :, a, :], compare_op=ALU.not_equal, fill=sign,
                                               base=-32 * (1 - a), pattern=[[-HD, 2], [-1, 32]], channel_multiplier=1)
                        pool.affine_select(out=shift[:], in_=shift[:], compare_op=ALU.not_equal, fill=1.0, base=HD,
                                           pattern=[[-1, TOKENS]], channel_multiplier=1)
                        pool.affine_select(out=cmp_mask[:], in_=cmp_mask[:], compare_op=ALU.is_ge, fill=NEG, base=1 - CMP_LEN,
                                           pattern=[[P, TT], [-CMP_STRIDE, N_CMP]], channel_multiplier=1)
                        pool.affine_select(out=cmp_seen[:], in_=cmp_seen[:], compare_op=ALU.is_ge, fill=0.0, base=1 - CMP_LEN,
                                           pattern=[[P, TT]], channel_multiplier=1)
                        step(pool.affine_select(out=own_head[:], in_=own_head[:], compare_op=ALU.is_ge, fill=0.0, base=0,
                                                pattern=[[-N_CMP, 8]], channel_multiplier=1))
                        pool.affine_select(out=own_head[:], in_=own_head[:], compare_op=ALU.is_ge, fill=0.0, base=N_CMP - 1,
                                           pattern=[[N_CMP, 8]], channel_multiplier=-1)

                with signals("rotated", "with_sin", "with_cos", "rotated_read") as (rotated, with_sin, with_cos, rotated_read), \
                        buffer("part_sin", [P, 2, 2, TOKENS]) as part_sin, nc.Block() as block:
                    pairs = n_rope // 2

                    @block.tensor
                    def _(pe):
                        for n in range(pairs):
                            if n >= 4:
                                pe.wait_ge(with_sin, n - 3)
                            for b in range(2):
                                last = pe.matmul(ps[:, n % 4, b * TOKENS:b * TOKENS + TOKENS], rot[:], qk[:, 2 * n + b, :],
                                                 start=True, stop=True)
                            last.then_inc(rotated, 1)

                    @block.vector
                    def _(dve):
                        for n in range(pairs):
                            dve.wait_ge(rotated, n + 1)
                            if n >= 2:
                                dve.wait_ge(with_cos, 2 * (n - 1))
                            dve.tensor_tensor(part_sin[:, n % 2], ps[:, n % 4, :].rearrange("p (b n) -> p b n", b=2),
                                              spread(p["sin"], 1, 2), ALU.mult).then_inc(with_sin, 1)

                    @block.gpsimd
                    def _(pool):
                        for n in range(pairs):
                            o = qk[:, 2 * n:2 * n + 2, :]
                            pool.wait_ge(with_sin, n + 1)
                            pool.tensor_tensor(o, o, spread(p["cos"], 1, 2), ALU.mult).then_inc(with_cos, 1)
                            pool.wait_ge(with_cos, 2 * n + 1)
                            pool.tensor_tensor(o, o, part_sin[:, n % 2], ALU.add).then_inc(with_cos, 1)

                cmp = mix.enter_context(ExitStack())
                kv_pairs = sbuf("kv_pairs", [P, 2, GROUPS, P], mem=cmp)
                window = sbuf("window", [P, 2, 16, GROUPS, N_CMP], mem=cmp)
                hid_nat = sbuf("hid_nat", [GROUPS * N_CMP, 2, 2, P], mem=cmp)
                hid = sbuf("hid", [P, 2, 2, GROUPS, N_CMP], mem=cmp)
                hid_heads = sbuf("hid_heads", [P, 2, 16, N_CMP], mem=cmp)
                k_cmp = sbuf("k_cmp", [P, GROUPS, N_CMP], mem=cmp)
                v_cmp = sbuf("v_cmp", [P, 2, 8, HD], mem=cmp)
                rows = 8 * N_CMP
                w2k = p["w2k"].rearrange("p (a n) -> p a n", a=2)
                w2v = p["w2v"].rearrange("p (a n) -> p a n", a=2)

                with signals("paired", "pairs_copied", "windowed", "hid_ready", "hid_done", "hid_turned", "hid_copied", "hid_spread", "k_ready",
                             "v_ready") as (
                        paired, pairs_copied, windowed, hid_ready, hid_done, hid_turned, hid_copied, hid_spread, k_ready,
                        v_ready), nc.Block() as block:
                    @block.sync
                    def _(sp):
                        stream.feed(sp, 2)

                    @block.tensor
                    def _(pe):
                        for a in range(2):
                            for g in range(GROUPS):
                                half = g % 2
                                lanes = slice(half * HD, half * HD + HD)
                                src = qk[lanes, 8 + g // 2, :] if a == 0 else v_cmp_t[lanes, g // 2, :]
                                for parity in range(2):
                                    s = HD * (half + 1 - parity)
                                    last = pe.matmul(ps[:, a + 6 * half, g // 2 * P:g // 2 * P + P], shift[lanes, s:s + P],
                                                     src.rearrange("p (j a) -> p a j", a=2)[:, parity, :],
                                                     start=(parity == 0), stop=(parity == 1))
                            last.then_inc(paired, 1)
                        for a in range(2):
                            c = stream.take(pe)
                            w = stream.slot(c)
                            pe.wait_ge(windowed, a + 1)
                            for k in range(16):
                                last = pe.matmul(ps[0:GROUPS * N_CMP, 2 + a, 0:TOKENS], window[:, a, k].rearrange("p g c -> p (g c)"),
                                                 w[:, k * 256:k * 256 + 256], start=(k == 0), stop=(k == 15))
                                if k == 0:
                                    stream.release(last)
                            last.then_inc(hid_ready, 1)
                            stream.pending = True
                        for a in range(2):
                            pe.wait_ge(hid_done, a + 1)
                            for n in range(2):
                                last = pe.transpose(ps[:, 4 + a, n * GROUPS * N_CMP:(n + 1) * GROUPS * N_CMP], hid_nat[:, a, n, :],
                                                    ident[0:GROUPS * N_CMP, 0:GROUPS * N_CMP])
                            last.then_inc(hid_turned, 1)
                        pe.wait_ge(hid_copied, 1)
                        for n in range(2):
                            last = pe.matmul(ps[:, 6, 0:GROUPS * N_CMP], w2k[:, n, :], hid[:, 0, n].rearrange("p g c -> p (g c)"),
                                             start=(n == 0), stop=(n == 1))
                        last.then_inc(k_ready, 1)
                        pe.wait_ge(hid_spread, 1)
                        for b in range(2):
                            for n in range(2):
                                last = pe.matmul(ps[0:rows, 7, b * HD:b * HD + HD],
                                                 hid_heads[:, n, 8 * b:8 * b + 8, :].rearrange("p h c -> p (h c)"), w2v[:, n, :],
                                                 start=(n == 0), stop=(n == 1))
                        last.then_inc(v_ready, 1)

                    @block.scalar
                    def _(act):
                        for a in range(2):
                            act.wait_ge(paired, a + 1)
                            for half in range(2):
                                last = act.activation(kv_pairs[:, a].rearrange("p (g b) j -> p b g j", b=2)[:, half],
                                                      ps[:, a + 6 * half, 0:2 * P].rearrange("p (g j) -> p g j", g=2), ACT.Copy)
                            last.then_inc(pairs_copied, 1)
                        for a in range(2):
                            act.wait_ge(hid_ready, a + 1)
                            act.activation(hid_nat[:, a], ps[0:GROUPS * N_CMP, 2 + a, 0:TOKENS].rearrange("p (n m) -> p n m", n=2),
                                           ACT.Silu).then_inc(hid_done, 1)
                        for a in range(2):
                            act.wait_ge(hid_turned, a + 1)
                            act.activation(hid[:, a], ps[:, 4 + a, 0:2 * GROUPS * N_CMP].rearrange("p (n g c) -> p n g c", n=2, g=GROUPS),
                                           ACT.Copy).then_inc(hid_copied, 1)
                        act.wait_ge(k_ready, 1)
                        act.activation(k_cmp[:], ps[:, 6, 0:GROUPS * N_CMP].rearrange("p (g c) -> p g c", g=GROUPS), ACT.Copy)

                    @block.vector
                    def _(dve):
                        for a, name in enumerate(("pos_k", "pos_v")):
                            o, n = offsets["cols"][name]
                            pos = cols[:, o:o + n]
                            pairs = kv_pairs[:, a].rearrange("p g (c r) -> p r g c", r=8)
                            dve.wait_ge(pairs_copied, a + 1)
                            for h in range(2):
                                last = dve.tensor_tensor(window[:, a, 8 * h:8 * h + 8], pairs[:, :, :, h:h + N_CMP],
                                                         spread(spread(pos[:, 8 * h:8 * h + 8], 2, GROUPS), 3, N_CMP), ALU.add)
                            last.then_inc(windowed, 1)
                        dve.wait_ge(hid_copied, 2)
                        for n in range(2):
                            last = dve.tensor_copy(hid_heads[:, n].rearrange("p (g r) c -> p g r c", g=GROUPS),
                                                   spread(hid[:, 1, n], 2, REP))
                        last.then_inc(hid_spread, 1)
                        dve.wait_ge(v_ready, 1)
                        for b in range(2):
                            dve.tensor_tensor(v_cmp[0:rows, b], spread(ps[0:rows, 7, b * HD:b * HD + HD], 1, 8),
                                              spread(own_head[0:rows, :], 2, HD), ALU.mult)

                def q_of(h, t0, t1):
                    g, r = h // REP, h % REP
                    half = g % 2 * HD
                    return qk[half:half + HD, (g // 2) * REP + r, t0:t1]

                with signals("scored", "biased", "exped", "probs_ready", "turned", "turned_copied", "dve_step") as (
                        scored, biased, exped, probs_ready, turned, turned_copied, dve_step), \
                        buffer("prob_cmp", [P, TT, 16, N_CMP]) as prob, buffer("prob_cmp_t", [P, TT, 2, P]) as prob_t, \
                        buffer("cmp_top", [P, TT, 16]) as cmp_top, nc.Block() as block:
                    @block.tensor
                    def _(pe):
                        for t in range(TT):
                            for h in range(16):
                                g = h // REP
                                half = g % 2
                                at = (g // 2 * REP + h % REP) * N_CMP
                                last = pe.matmul(ps[:, t + 2 * half, at:at + N_CMP], q_of(h, t * P, t * P + P),
                                                 k_cmp[half * HD:half * HD + HD, g, :], start=True, stop=True)
                            last.then_inc(scored, 1)
                        for t in range(TT):
                            pe.wait_ge(probs_ready, t + 1)
                            for b in range(2):
                                last = pe.transpose(ps[0:rows, 2 + t, b * P:b * P + P],
                                                    prob[:, t, 8 * b:8 * b + 8, :].rearrange("p h c -> p (h c)"), ident[:])
                            last.then_inc(turned, 1)
                        for t in range(TT):
                            pe.wait_ge(turned_copied, t + 1)
                            for b in range(2):
                                pe.matmul(ps[:, 4 + 2 * b + t, :], prob_t[0:rows, t, b, :],
                                          v_cmp[0:rows, b].rearrange("p h n -> p (h n)"), start=True, stop=False,
                                          skip_group_check=True)

                    @block.vector
                    def _(dve):
                        step = Chain(dve, dve_step)
                        for t in range(TT):
                            o = prob[:, t]
                            dve.wait_ge(scored, t + 1)
                            for g in range(GROUPS):
                                at = g // 2 * REP * N_CMP
                                last = dve.scalar_tensor_tensor(
                                    o[:, g * REP:g * REP + REP, :],
                                    ps[:, t + 2 * (g % 2), at:at + REP * N_CMP].rearrange("p (h c) -> p h c", h=REP), HD ** -0.5,
                                    spread(cmp_mask[:, t, :], 1, REP), ALU.mult, ALU.add)
                            step(last)
                            step(dve.tensor_reduce(cmp_top[:, t, :], o, AX.X, ALU.max))
                            dve.tensor_tensor(o, o, spread(cmp_top[:, t, :], 2, N_CMP), ALU.subtract).then_inc(biased, 1)
                        for t in range(TT):
                            o = prob[:, t]
                            dve.wait_ge(exped, t + 1)
                            step(dve.tensor_reduce(cmp_top[:, t, :], o, AX.X, ALU.add))
                            step(dve.reciprocal(cmp_top[:, t, :], cmp_top[:, t, :]))
                            step(dve.scalar_tensor_tensor(cmp_top[:, t, :], cmp_top[:, t, :], cmp_seen[:, t:t + 1], branch[:, t, :, 0],
                                                          ALU.mult, ALU.mult))
                            dve.tensor_tensor(o, o, spread(cmp_top[:, t, :], 2, N_CMP), ALU.mult).then_inc(probs_ready, 1)

                    @block.scalar
                    def _(act):
                        for t in range(TT):
                            act.wait_ge(biased, t + 1)
                            act.activation(prob[:, t], prob[:, t], ACT.Exp).then_inc(exped, 1)
                        for t in range(TT):
                            act.wait_ge(turned, t + 1)
                            act.activation(prob_t[0:rows, t], ps[0:rows, 2 + t, 0:2 * P].rearrange("p (b n) -> p b n", b=2),
                                           ACT.Copy).then_inc(turned_copied, 1)

                cmp.close()

                def scores(pe, i):
                    h, a = i // 2, i % 2
                    half = h // REP % 2 * HD
                    k = qk[half:half + HD, 10 + 2 * a + h // REP // 2, :]
                    pe.matmul(ps[:, i % 2, 0:P], q_of(h, 0, P), k[:, 0:P], start=True, stop=True)
                    return pe.matmul(ps[:, i % 2, P:TRI], q_of(h, P, TOKENS), k, start=True, stop=True)

                def logits(dve, step, i, out):
                    return dve.scalar_tensor_tensor(out, ps[:, i % 2, 0:TRI], HD ** -0.5, mask[:], ALU.mult, ALU.add)

                attention(32, scores, logits, lambda i, s: v_tok[:, s, i % 2, i // 2 // REP, :],
                          lambda i, t: ps[:, 4 + 2 * (i // 16) + t, i // 2 % 8 * HD:i // 2 % 8 * HD + HD],
                          gate=lambda i: branch[:, :, i // 2, 1 + i % 2], starts=False)
                o = sbuf("o", [P, TT, D], mem=mix)
                turn_heads(o, x_parts)
                post_norm(p["post1"], mixer=x_parts)

            pre_norm(lambda b: col("norm_g", DK + b), x_parts)
            feed_forward("relu2", MLP_TILES, ACT.Relu, x_parts)
            post_norm(p["post2"])

        def fox(mem):
            buf, p = params("fox", mem)
            x_parts = token_parts(mem)
            pre_norm(lambda b: col("norm_g", 2 * DK + b), x_parts)
            with ExitStack() as mix:
                qT = sbuf("qT", [P, DK, TOKENS], mem=mix)
                kT = sbuf("kT", [P, DK, TOKENS], mem=mix)
                v = sbuf("v", [P, TT, D], mem=mix)
                forget = sbuf("forget", [HEADS_B, 3, TOKENS], mem=mix)
                decay = sbuf("decay", [P, TT, HEADS_B], mem=mix)
                pick = sbuf("pick", [HEADS_B, HEADS_B, P], mem=mix)

                with signals("params_loaded", "t_ready", "t_read", "n_ready", "n_read", "act_step", "dve_step", "summed",
                             "turned", "pool_step", *PARTS) as (
                        params_loaded, t_ready, t_read, n_ready, n_read, act_step, dve_step, summed, turned, pool_step, *sems), \
                        ExitStack() as own:
                    weights = weight_parts("ttttnn.", sems, own)
                    block = own.enter_context(nc.Block())

                    @block.sync
                    def _(sp):
                        sp.dma_start(buf[:], d["fox"]).then_inc(params_loaded, 16)
                        stream.feed(sp, 7)
                        sp.wait_ge(params_loaded, 16)

                    @block.tensor
                    def _(pe):
                        at = 0
                        for _ in range(4):
                            at = parts_t(pe, weights, x_parts, at, t_ready, t_read)
                        for n in range(2):
                            parts_n(pe, weights, x_parts, n, n_ready, n_read)
                        product_t(pe, hT, [(0, HEADS_B)], at, t_ready, t_read)
                        pe.wait_ge(summed, 1)
                        for t in range(TT):
                            last = pe.transpose(ps[:, 1, t * HEADS_B:t * HEADS_B + HEADS_B], forget[:, 2, t * P:t * P + P],
                                                ident[0:HEADS_B, 0:HEADS_B])
                        last.then_inc(turned, 1)

                    @block.scalar
                    def _(act):
                        for at in range(16):
                            weights.high(act, at + 4)
                            out = qT[:, at, :] if at < DK else kT[:, at - DK, :]
                            act.wait_ge(t_ready, at + 1)
                            act.activation(out, ps[:, at % 4, 0:TOKENS], ACT.Copy,
                                           scale=HD ** -0.5 if at < DK else 1.0).then_inc(t_read, 1)
                        weights.high(act, 24)
                        act.wait_ge(act_step, 1)
                        act.activation(forget[:, 1], forget[:, 1], ACT.Exp, scale=-1.0).then_inc(act_step, 1)
                        act.wait_ge(act_step, 2)
                        act.activation(forget[:, 1], forget[:, 1], ACT.Ln, bias=1.0).then_inc(act_step, 1)
                        act.wait_ge(turned, 1)
                        act.activation(decay[:], ps[:, 1, 0:TT * HEADS_B].rearrange("p (t h) -> p t h", t=TT), ACT.Copy)

                    @block.vector
                    def _(dve):
                        step = Chain(dve, dve_step)
                        for n in range(2):
                            weights.low(dve, 23 + n)
                            dve.wait_ge(n_ready, n + 1)
                            dve.tensor_copy(v[:, :, n * WIDE:n * WIDE + WIDE], bank_n(n)).then_inc(n_read, 1)
                        dve.wait_ge(t_ready, 17)
                        step(dve.tensor_scalar(forget[:, 0], ps[0:HEADS_B, 0, 0:TOKENS], col("b_f", rows=HEADS_B), None, ALU.add))
                        dve.scalar_tensor_tensor(forget[:, 1], forget[:, 0], -1.0, forget[:, 0], ALU.mult, ALU.max).then_inc(act_step, 1)
                        dve.wait_ge(act_step, 3)
                        step(dve.scalar_tensor_tensor(forget[:, 0], forget[:, 0], 0.0, forget[:, 1], ALU.min, ALU.subtract))
                        dve.tensor_tensor_scan(forget[:, 2], ones[0:HEADS_B, :], forget[:, 0], 0.0, ALU.mult, ALU.add).then_inc(summed, 1)

                    @block.gpsimd
                    def _(pool):
                        step = Chain(pool, pool_step)
                        step(pool.memset(pick[:], 0.0))
                        pool.affine_select(out=pick[:], in_=pick[:], compare_op=ALU.not_equal, fill=-1.0, base=0,
                                           pattern=[[-1, HEADS_B], [0, P]], channel_multiplier=1)

                key_decay = sbuf("key_decay", [P, HEADS_B, TOKENS], mem=mix)
                with signals("repeated", "repeated_read") as (repeated, repeated_read), nc.Block() as block:
                    @block.tensor
                    def _(pe):
                        for n in range(HEADS_B // 2):
                            if n >= 4:
                                pe.wait_ge(repeated_read, n - 3)
                            for b in range(2):
                                last = pe.matmul(ps[:, n % 4, b * TOKENS:b * TOKENS + TOKENS], pick[:, 2 * n + b, :], forget[:, 2, :],
                                                 start=True, stop=True)
                            last.then_inc(repeated, 1)

                    @block.scalar
                    def _(act):
                        for n in range(HEADS_B // 2):
                            act.wait_ge(repeated, n + 1)
                            act.activation(key_decay[:, 2 * n:2 * n + 2, :], ps[:, n % 4, :].rearrange("p (b n) -> p b n", b=2),
                                           ACT.Copy).then_inc(repeated_read, 1)

                def scores(pe, h):
                    half = slice(h % 2 * HD, h % 2 * HD + HD)
                    pe.matmul(ps[:, h % 2, 0:P], qT[half, h // 2, 0:P], kT[half, h // 2, 0:P], start=True, stop=True)
                    return pe.matmul(ps[:, h % 2, P:TRI], qT[half, h // 2, P:TOKENS], kT[half, h // 2, :], start=True, stop=True)

                def logits(dve, step, h, out):
                    for t, o, n in ((0, 0, P), (1, P, TOKENS)):
                        last = dve.scalar_tensor_tensor(out[:, o:o + n], ps[:, h % 2, o:o + n], decay[:, t, h:h + 1],
                                                        key_decay[:, h, 0:n], ALU.add, ALU.add)
                    step(last)
                    return dve.tensor_tensor(out, out, mask[:], ALU.add)

                attention(HEADS_B, scores, logits, lambda h, s: v[:, s, h * HD:h * HD + HD],
                          lambda h, t: ps[:, 4 + 2 * (h // 8) + t, h % 8 * HD:h % 8 * HD + HD])
                turn_heads(v, x_parts)
                post_norm(p["post1"], mixer=x_parts)

            pre_norm(lambda b: col("norm_g", 3 * DK + b), x_parts)
            feed_forward("relu2", MLP_TILES, ACT.Relu, x_parts)
            post_norm(p["post2"])


        def add_gated(gate, mixer=None):
            with signals("n_ready", "n_read", "dve_step", *PARTS) as (n_ready, n_read, dve_step, *sems), ExitStack() as own:
                gated_y = sbuf("gated_y", [P, TT, D], mem=own)
                if mixer is not None:
                    weights = weight_parts("nn", sems, own)
                block = own.enter_context(nc.Block())
                if mixer is not None:
                    @block.sync
                    def _(sp):
                        stream.feed(sp, 2)

                    @block.tensor
                    def _(pe):
                        for at in range(2):
                            parts_n(pe, weights, mixer, at, n_ready, n_read)

                if mixer is not None:
                    @block.scalar
                    def _(act):
                        weights.high(act, 8)

                @block.vector
                def _(dve):
                    step = Chain(dve, dve_step)
                    if mixer is not None:
                        weights.low(dve, 8)
                        dve.wait_ge(n_ready, 2)
                    for t in range(TT):
                        last = dve.tensor_tensor(halves(gated_y[:, t, :]), y_banks(t), halves(gate), ALU.mult)
                    step(last)
                    dve.tensor_tensor(x[:], x[:], gated_y[:], ALU.add)

        def modulation(buf, p, gain):
            with signals("params_loaded", "turned", "repeated", "added", "dve_step") as (
                    params_loaded, turned, repeated, added, dve_step), nc.Block() as block:
                gate_rows = [layer * 12 + piece * 2 + half for layer in range(2) for piece in (2, 5) for half in range(2)]

                @block.sync
                def _(sp):
                    sp.dma_start(buf[:], d["ada"]).then_inc(params_loaded, 16)

                @block.tensor
                def _(pe):
                    for q in range(4):
                        last = pe.transpose(ps[:, q, 0:ADA_ROWS], mod[:, q * P:q * P + P], ident[0:ADA_ROWS, 0:ADA_ROWS])
                    last.then_inc(turned, 1)
                    for n, row in enumerate(gate_rows):
                        if n >= 4:
                            pe.wait_ge(added, n - 3)
                        pe.matmul(ps[:, 4 + n % 4, :], ident[0:ADA_ROWS, row:row + 1].broadcast_to([ADA_ROWS, P]), mod[:],
                                  start=True, stop=True).then_inc(repeated, 1)

                @block.vector
                def _(dve):
                    step = Chain(dve, dve_step)
                    dve.wait_ge(params_loaded, 16)
                    dve.wait_ge(turned, 1)
                    shifts = p["shifts"].rearrange("p (n m q) -> p n m q", n=4, q=4)
                    for q in range(4):
                        last = dve.tensor_tensor(shifts[:, :, :, q], shifts[:, :, :, q],
                                                 ps[:, q, 0:ADA_ROWS].rearrange("p (n m) -> p n m", n=4)[:, :, 0:4], ALU.add)
                    step(last)
                    o, n = offsets["cols"]["norm_w"]
                    pairs = p["shifts"].rearrange("p (n a k) -> p n a k", a=2, k=DK)
                    dve.scalar_tensor_tensor(gain[:], pairs[:, :, 1, :], 1.0, cols[:, o:o + n].rearrange("p (n k) -> p n k", k=DK),
                                             ALU.add, ALU.mult)
                    for n in range(len(gate_rows)):
                        g = p["gates"][:, n * WIDE:n * WIDE + WIDE]
                        dve.wait_ge(repeated, n + 1)
                        dve.tensor_tensor(g, g, ps[:, 4 + n % 4, :], ALU.add).then_inc(added, 1)

        def head_norm(o, gate, norm_w, parts):
            with signals("copied", "squared", "var_ready", "rstd_ready", "weighed", "normed", "turned", "turned_read", "dve_step",
                         "high_ready") as (
                    copied, squared, var_ready, rstd_ready, weighed, normed, turned, turned_read, dve_step,
                    high_ready), \
                    buffer("square", [P, TT, D]) as square, buffer("head_var", [P, TT, HEADS_C]) as head_var, nc.Block() as block:
                @block.scalar
                def _(act):
                    for t in range(TT):
                        act.activation(halves(square[:, t, :]), y_banks(t), ACT.Square).then_inc(squared, 1)
                    high_turned(act, parts, turned, high_ready)

                @block.vector
                def _(dve):
                    step = Chain(dve, dve_step)
                    heads = lambda a: a.rearrange("p t (h n) -> p t h n", h=HEADS_C)
                    for t in range(TT):
                        dve.wait_ge(squared, t + 1)
                        last = dve.tensor_reduce(head_var[:, t, :], square[:, t, :].rearrange("p (h n) -> p h n", h=HEADS_C), AX.X, ALU.add)
                    step(last)
                    dve.tensor_scalar(head_var[:], head_var[:], 1.0 / P, RMS_EPS, ALU.mult, ALU.add).then_inc(var_ready, 1)
                    dve.wait_ge(weighed, 1)
                    for t in range(TT):
                        last = dve.tensor_tensor(halves(o[:, t, :]), y_banks(t), halves(gate[:, t, :]), ALU.mult)
                    step(last)
                    dve.wait_ge(rstd_ready, 1)
                    dve.tensor_tensor(heads(o[:]), heads(o[:]), spread(head_var[:], 3, P), ALU.mult).then_inc(normed, 1)
                    low_turned(dve, parts, high_ready, turned_read)

                @block.gpsimd
                def _(pool):
                    pool.tensor_tensor(gate[:], gate[:], spread(norm_w, 1, TT), ALU.mult).then_inc(weighed, 1)
                    pool.wait_ge(var_ready, 1)
                    v = head_var[:].rearrange("p t h -> p (t h)")
                    pool.tensor_tensor(v, v, minus_half[:, 0:TT * HEADS_C], ALU.pow).then_inc(rstd_ready, 1)

                @block.tensor
                def _(pe):
                    pe.wait_ge(normed, 1)
                    transposes(pe, o, turned, turned_read)

        def mlstm(mem, x_parts):
            buf, p = params("mlstm", mem)
            qkT = sbuf("qkT", [P, DK, TOKENS], mem=mem)
            v = sbuf("v", [P, TT, D], mem=mem)
            out_gate = sbuf("out_gate", [P, TT, D], mem=mem)
            lanes = slice(0, HEADS_C)
            gate_t = sbuf("gate_t", [HEADS_C, 5, TOKENS], mem=mem)
            decay = sbuf("decay", [P, TT, HEADS_C], mem=mem)
            key_gate = sbuf("key_gate", [P, HEADS_C, TOKENS], mem=mem)
            pick = sbuf("pick", [HEADS_C, HEADS_C, P], mem=mem)
            before = 3
            with ExitStack() as conv, signals(
                    "params_loaded", "t_ready", "t_read", "n_ready", "n_read", "dve_step", "pad_ready", "convolved", "o_copied",
                    "act_step", "summed", "turned", "pool_step", "pick_ready", "repeated", "repeated_read", *PARTS) as (
                    params_loaded, t_ready, t_read, n_ready, n_read, dve_step, pad_ready, convolved, o_copied,
                    act_step, summed, turned, pool_step, pick_ready, repeated, repeated_read, *sems):
                weights = weight_parts("ttnnnn.", sems, conv)
                raw = sbuf("raw", [P, DK, before + TOKENS], mem=conv)
                block = conv.enter_context(nc.Block())

                @block.sync
                def _(sp):
                    sp.dma_start(buf[:], d["mlstm"]).then_inc(params_loaded, 16)
                    stream.feed(sp, 7)
                    sp.wait_ge(params_loaded, 16)

                @block.tensor
                def _(pe):
                    at = 0
                    for _ in range(2):
                        at = parts_t(pe, weights, x_parts, at, t_ready, t_read)
                    for n in range(4):
                        parts_n(pe, weights, x_parts, n, n_ready, n_read)
                    product_t(pe, hT, [(0, HEADS_C), (HEADS_C, HEADS_C)], at, t_ready, t_read)
                    pe.wait_ge(summed, 1)
                    for t in range(TT):
                        last = pe.transpose(ps[:, 2, t * HEADS_C:t * HEADS_C + HEADS_C], gate_t[:, 3, t * P:t * P + P], ident[lanes, lanes])
                    last.then_inc(turned, 1)
                    pe.wait_ge(summed, 2)
                    pe.wait_ge(pick_ready, 1)
                    for n in range(HEADS_C // 2):
                        bank = (3, 0, 1, 3)[n]
                        if n == 3:
                            pe.wait_ge(repeated_read, 1)
                        for b in range(2):
                            last = pe.matmul(ps[:, bank, b * TOKENS:b * TOKENS + TOKENS], pick[:, 2 * n + b, :], gate_t[:, 4, :],
                                             start=True, stop=True)
                        last.then_inc(repeated, 1)

                @block.scalar
                def _(act):
                    act.wait_ge(pad_ready, 1)
                    for b in range(DK):
                        weights.high(act, b + 4)
                        act.wait_ge(t_ready, b + 1)
                        act.activation(raw[:, b, before:], ps[:, b % 4, 0:TOKENS], ACT.Copy).then_inc(t_read, 1)
                    for b in range(DK):
                        weights.high(act, DK + 4 + b // 2)
                        act.wait_ge(convolved, b + 1)
                        act.activation(qkT[:, b, :], qkT[:, b, :], ACT.Silu, bias=col("conv_b", b))
                    weights.high(act, 24)
                    act.wait_ge(o_copied, 2)
                    act.activation(out_gate[:], out_gate[:], ACT.Sigmoid)
                    act.wait_ge(act_step, 1)
                    act.activation(gate_t[:, 0], gate_t[:, 0], ACT.Tanh, scale=1.0 / IGATE_CAP).then_inc(act_step, 1)
                    act.activation(gate_t[:, 2], gate_t[:, 2], ACT.Exp, scale=-1.0).then_inc(act_step, 1)
                    act.wait_ge(act_step, 3)
                    act.activation(gate_t[:, 2], gate_t[:, 2], ACT.Ln, bias=1.0).then_inc(act_step, 1)
                    act.wait_ge(turned, 1)
                    act.activation(decay[:], ps[:, 2, 0:TT * HEADS_C].rearrange("p (t h) -> p t h", t=TT), ACT.Copy)
                    for n in range(HEADS_C // 2):
                        act.wait_ge(repeated, n + 1)
                        act.activation(key_gate[:, 2 * n:2 * n + 2, :], ps[:, (3, 0, 1, 3)[n], :].rearrange("p (b n) -> p b n", b=2),
                                       ACT.Copy).then_inc(repeated_read, 1)

                @block.vector
                def _(dve):
                    step = Chain(dve, dve_step)
                    dve.memset(raw[:, :, 0:before], 0.0).then_inc(pad_ready, 1)
                    dve.wait_ge(pad_ready, 1)
                    for b in range(DK):
                        weights.low(dve, b + 5)
                        dve.wait_ge(t_read, b + 1)
                        step(dve.tensor_scalar(qkT[:, b, :], raw[:, b, 0:TOKENS], col("conv_w", 4 * b), None, ALU.mult))
                        for j in range(1, 4):
                            last = dve.scalar_tensor_tensor(qkT[:, b, :], raw[:, b, j:j + TOKENS], col("conv_w", 4 * b + j), qkT[:, b, :],
                                                            ALU.mult, ALU.add)
                            if j < 3:
                                step(last)
                        last.then_inc(convolved, 1)
                    for n in range(4):
                        out = v if n < 2 else out_gate
                        weights.low(dve, DK + 4 * n + 7)
                        dve.wait_ge(n_ready, n + 1)
                        dve.tensor_copy(out[:, :, n % 2 * WIDE:n % 2 * WIDE + WIDE], bank_n(n)).then_inc(n_read, 1)
                        if n >= 2:
                            dve.wait_ge(n_read, n + 1)
                            dve.memset(spare[:], 0.0).then_inc(o_copied, 1)
                    dve.wait_ge(t_ready, DK + 2)
                    dve.tensor_scalar(gate_t[:, 0], ps[lanes, 0, 0:TOKENS], col("i_bias", rows=HEADS_C), None, ALU.add)
                    step(dve.tensor_scalar(gate_t[:, 1], ps[lanes, 1, 0:TOKENS], col("f_bias", rows=HEADS_C), None, ALU.add))
                    dve.scalar_tensor_tensor(gate_t[:, 2], gate_t[:, 1], -1.0, gate_t[:, 1], ALU.mult, ALU.max).then_inc(act_step, 1)
                    dve.wait_ge(act_step, 4)
                    step(dve.scalar_tensor_tensor(gate_t[:, 1], gate_t[:, 1], 0.0, gate_t[:, 2], ALU.min, ALU.subtract))
                    dve.tensor_tensor_scan(gate_t[:, 3], ones[lanes, :], gate_t[:, 1], 0.0, ALU.mult, ALU.add).then_inc(summed, 1)
                    dve.wait_ge(summed, 1)
                    dve.scalar_tensor_tensor(gate_t[:, 4], gate_t[:, 0], IGATE_CAP, gate_t[:, 3], ALU.mult, ALU.subtract).then_inc(summed, 1)

                @block.gpsimd
                def _(pool):
                    step = Chain(pool, pool_step)
                    step(pool.memset(pick[:], 0.0))
                    pool.affine_select(out=pick[:], in_=pick[:], compare_op=ALU.not_equal, fill=1.0, base=0,
                                       pattern=[[-1, HEADS_C], [0, P]], channel_multiplier=1).then_inc(pick_ready, 1)

            with signals("scored", "biased", "exped", "probs_ready", "probs_turned", "turned_copied", "weighted", "dve_step") as (
                    scored, biased, exped, probs_ready, probs_turned, turned_copied, weighted, dve_step), ExitStack() as att:
                weight = sbuf("weight", [P, 2, TRI], mem=att)
                weight_t = sbuf("weight_t", [P, 2, TRI], mem=att)
                top = sbuf("top", [P, 2, TT], mem=att)
                least = sbuf("least", [P, 2, TT], mem=att)
                total = sbuf("total", [P, 2, TT], mem=att)
                part = (slice(0, P), slice(P, TRI))
                keys = (P, TOKENS)
                n = HEADS_C
                block = att.enter_context(nc.Block())

                @block.tensor
                def _(pe):
                    for i in range(n + 2):
                        if i < n:
                            half = slice(i % 2 * HD, i % 2 * HD + HD)
                            if i >= 2:
                                pe.wait_ge(probs_ready, i - 1)
                            q, k = qkT[half, i // 2, :], qkT[half, 4 + i // 2, :]
                            pe.matmul(ps[:, i % 2, 0:P], q[:, 0:P], k[:, 0:P], start=True, stop=True)
                            pe.matmul(ps[:, i % 2, P:TRI], q[:, P:TOKENS], k, start=True, stop=True).then_inc(scored, 1)
                        j = i - 1
                        if 0 <= j < n:
                            pe.wait_ge(probs_ready, j + 1)
                            if j >= 2:
                                pe.wait_ge(turned_copied, j - 1)
                            for b in range(3):
                                last = pe.transpose(ps[:, 2 + j % 2, b * P:b * P + P], weight[:, j % 2, b * P:b * P + P], ident[:])
                            last.then_inc(probs_turned, 1)
                        j = i - 2
                        if j >= 0:
                            pe.wait_ge(turned_copied, j + 1)
                            t = weight_t[:, j % 2, :]
                            out = [ps[:, 4 + 2 * (j // 4) + a, j % 4 * P:j % 4 * P + P] for a in range(TT)]
                            val = [v[:, s, j * P:j * P + P] for s in range(TT)]
                            pe.matmul(out[0], t[:, 0:P], val[0], start=True, stop=True, skip_group_check=True)
                            pe.matmul(out[1], t[:, P:2 * P], val[0], start=True, stop=False, skip_group_check=True)
                            pe.matmul(out[1], t[:, 2 * P:TRI], val[1], start=False, stop=True,
                                      skip_group_check=True).then_inc(weighted, 1)

                @block.vector
                def _(dve):
                    step = Chain(dve, dve_step)
                    for i in range(n + 1):
                        if i < n:
                            o = weight[:, i % 2, :]
                            if i >= 2:
                                dve.wait_ge(probs_turned, i - 1)
                            for t in range(TT):
                                last = dve.scalar_tensor_tensor(o[:, part[t]], key_gate[:, i, 0:keys[t]], decay[:, t, i:i + 1],
                                                                mask[:, part[t]], ALU.add, ALU.add)
                            step(last)
                            for t in range(TT):
                                last = dve.tensor_reduce(top[:, i % 2, t:t + 1], o[:, part[t]], AX.X, ALU.max)
                            step(last)
                            step(dve.tensor_tensor(top[:, i % 2, :], top[:, i % 2, :], decay[:, :, i], ALU.max))
                            dve.tensor_scalar(top[:, i % 2, :], top[:, i % 2, :], -1.0, None, ALU.mult).then_inc(biased, 1)
                        j = i - 1
                        if j >= 0:
                            o = weight[:, j % 2, :]
                            s = total[:, j % 2, :]
                            dve.wait_ge(exped, j + 1)
                            dve.wait_ge(scored, j + 1)
                            for t in range(TT):
                                last = dve.scalar_tensor_tensor(o[:, part[t]], o[:, part[t]], HD ** -0.5, ps[:, j % 2, part[t]],
                                                                ALU.mult, ALU.mult, accum_out=s[:, t:t + 1])
                            step(last)
                            step(dve.scalar_tensor_tensor(s, s, -1.0, s, ALU.mult, ALU.max))
                            step(dve.tensor_tensor(s, s, least[:, j % 2, :], ALU.max))
                            step(dve.reciprocal(s, s))
                            for t in range(TT):
                                last = dve.tensor_scalar(o[:, part[t]], o[:, part[t]], s[:, t:t + 1], None, ALU.mult)
                            last.then_inc(probs_ready, 1)

                @block.scalar
                def _(act):
                    for i in range(n + 1):
                        if i < n:
                            act.wait_ge(biased, i + 1)
                            act.activation(least[:, i % 2, :], top[:, i % 2, :], ACT.Exp)
                            for t in range(TT):
                                o = weight[:, i % 2, part[t]]
                                last = act.activation(o, o, ACT.Exp, bias=top[:, i % 2, t:t + 1])
                            last.then_inc(exped, 1)
                        j = i - 1
                        if j >= 0:
                            act.wait_ge(probs_turned, j + 1)
                            if j >= 2:
                                act.wait_ge(weighted, j - 1)
                            act.activation(weight_t[:, j % 2, :], ps[:, 2 + j % 2, 0:TRI], ACT.Copy).then_inc(turned_copied, 1)

            head_norm(v, out_gate, p["norm_w"], x_parts)

        def hgrn2(mem, normalise):
            buf, p = params("hgrn", mem)
            qT = sbuf("qT", [P, HEADS_C, TOKENS], mem=mem)
            kT = sbuf("kT", [P, HEADS_C, TOKENS], mem=mem)
            cum = sbuf("cum", [P, HEADS_C, TOKENS], mem=mem)
            v = sbuf("v", [P, TT, D], mem=mem)
            out_gate = sbuf("out_gate", [P, TT, D], mem=mem)

            own = ExitStack()
            x_parts = token_parts(own)
            normalise(x_parts)
            with own, signals("params_loaded", "t_ready", "t_read", "n_ready", "n_read", "g_copied", "act_step", "dve_step", *PARTS) as (
                    params_loaded, t_ready, t_read, n_ready, n_read, g_copied, act_step, dve_step, *sems):
                weights = weight_parts("ttttnnnn", sems, own)
                log_f = cum
                soft = hT
                block = own.enter_context(nc.Block())

                @block.sync
                def _(sp):
                    sp.dma_start(buf[:], d["hgrn"]).then_inc(params_loaded, 16)
                    stream.feed(sp, 8)
                    sp.wait_ge(params_loaded, 16)

                @block.tensor
                def _(pe):
                    at = 0
                    for _ in range(4):
                        at = parts_t(pe, weights, x_parts, at, t_ready, t_read)
                    for n in range(4):
                        parts_n(pe, weights, x_parts, n, n_ready, n_read)

                @block.scalar
                def _(act):
                    for at in range(16):
                        out, func = (qT, ACT.Silu) if at < 8 else (log_f, ACT.Copy)
                        weights.high(act, at + 4)
                        act.wait_ge(t_ready, at + 1)
                        act.activation(out[:, at % 8, :], ps[:, at % 4, 0:TOKENS], func).then_inc(t_read, 1)
                    act.wait_ge(t_read, 16)
                    weights.high(act, 20)
                    act.activation(kT[:], log_f[:], ACT.Sigmoid, scale=-1.0)
                    weights.high(act, 22)
                    act.activation(soft[:], log_f[:], ACT.Abs).then_inc(act_step, 1)
                    weights.high(act, 24)
                    act.wait_ge(act_step, 1)
                    act.activation(soft[:], soft[:], ACT.Exp, scale=-1.0).then_inc(act_step, 1)
                    weights.high(act, 32)
                    act.wait_ge(act_step, 2)
                    act.activation(soft[:], soft[:], ACT.Ln, bias=1.0).then_inc(act_step, 1)
                    act.wait_ge(g_copied, 1)
                    act.activation(out_gate[:], out_gate[:], ACT.Silu)

                @block.vector
                def _(dve):
                    step = Chain(dve, dve_step)
                    for n in range(4):
                        out = v if n < 2 else out_gate
                        weights.low(dve, 16 + 4 * n + 7)
                        dve.wait_ge(n_ready, n + 1)
                        dve.tensor_copy(out[:, :, n % 2 * WIDE:n % 2 * WIDE + WIDE], bank_n(n)).then_inc(n_read, 1)
                    dve.wait_ge(n_read, 4)
                    dve.memset(spare[:], 0.0).then_inc(g_copied, 1)
                    dve.wait_ge(act_step, 3)
                    step(dve.scalar_tensor_tensor(log_f[:], log_f[:], 0.0, soft[:], ALU.min, ALU.subtract))
                    step(dve.tensor_scalar(log_f[:], log_f[:], LOG_FLOOR, None, ALU.max))
                    for h in range(HEADS_C):
                        dve.tensor_tensor_scan(cum[:, h, :], ones[:], log_f[:, h, :], 0.0, ALU.mult, ALU.add)

            with ExitStack() as att:
                weight = sbuf("weight", [P, TT, HEADS_C, P], mem=att)
                weight_far = sbuf("weight_far", [P, HEADS_C, P], mem=att)
                q_dec = sbuf("q_dec", [P, 2, HEADS_C, TOKENS], mem=att)
                k_dec = sbuf("k_dec", [P, 2, HEADS_C, TOKENS], mem=att)
                diff = hT[:].rearrange("p k n -> p (k n)").rearrange("p (a n) -> p a n", a=2)
                levels = [P >> n for n in range(8)]
                pair_bits = sbuf("pair_bits", [P, 2, D], mem=att)
                pairs_of = pair_bits[:, 0, :].rearrange("p (n t) -> p n t", n=8)
                pairs_bit = pair_bits[:, 1, :].bitcast(U32).rearrange("p (n t) -> p n t", n=8)
                with signals("diff_ready", "exped", "scaled", "scored", "placed", "dve_step", "pool_step", "masks_ready", "done") as (
                        diff_ready, exped, scaled, scored, placed, dve_step, pool_step, masks_ready, done), nc.Block() as block:
                    @block.gpsimd
                    def _(pool):
                        step = Chain(pool, pool_step)
                        pool.memset(q_dec[:], 0.0)
                        pool.memset(k_dec[:], 0.0).then_inc(masks_ready, 1)
                        step(pool.memset(pairs_of, 0.0))
                        for n, half in enumerate(levels[1:]):
                            segs = P // (2 * half)
                            m = pairs_of[:, n, :].rearrange("p (g a w) -> p g a w", a=2, w=half)[:, :, 1, :]
                            step(pool.memset(m, 1.0))
                            step(pool.affine_select(out=m, in_=m, compare_op=ALU.is_ge, fill=0.0, base=0,
                                                    pattern=[[-2 * half, segs], [0, half]], channel_multiplier=1))
                            step(pool.affine_select(out=m, in_=m, compare_op=ALU.is_ge, fill=0.0, base=half - 1,
                                                    pattern=[[2 * half, segs], [0, half]], channel_multiplier=-1))
                        step(pool.tensor_copy(pairs_of[:, 7, :], ident[:]))
                        pool.tensor_copy(pairs_bit, pairs_of).then_inc(masks_ready, 1)

                    def split(a, half):
                        return a.rearrange("p h (g a w) -> p (h g) a w", a=2, w=half)

                    @block.vector
                    def _(dve):
                        step = Chain(dve, dve_step)

                        def decays(n):
                            half = levels[n]
                            c = split(cum[:], half)
                            ref = c[:, :, 0, half - 1:half].broadcast_to([P, HEADS_C * P // half, half])
                            if n >= 1:
                                dve.wait_ge(scaled, n)
                            dve.tensor_tensor(diff[:, 0, :].rearrange("p (g w) -> p g w", w=half), c[:, :, 1, :], ref, ALU.subtract)
                            dve.tensor_tensor(diff[:, 1, :].rearrange("p (g w) -> p g w", w=half), ref, c[:, :, 0, :],
                                              ALU.subtract).then_inc(diff_ready, 1)

                        def scale(n):
                            half = levels[n]
                            dve.wait_ge(exped, n + 1)
                            if n >= 2:
                                dve.wait_ge(scored, 2 * (n - 2) + 2)
                            e = diff[:].rearrange("p a (g w) -> p a g w", w=half)
                            dve.tensor_tensor(split(q_dec[:, n % 2], half)[:, :, 1, :], split(qT[:], half)[:, :, 1, :], e[:, 0], ALU.mult)
                            dve.tensor_tensor(split(k_dec[:, n % 2], half)[:, :, 0, :], split(kT[:], half)[:, :, 0, :], e[:, 1],
                                              ALU.mult).then_inc(scaled, 1)

                        def place(n):
                            for t in range(TT):
                                dve.wait_ge(scored, 2 * n + t + 1)
                                if n >= 2:
                                    dve.wait_ge(placed, 2 * (n - 1) + t)
                                for b in range(2):
                                    got = ps[:, 4 * (n % 2) + 2 * t + b, :].rearrange("p (h n) -> p h n", h=4)
                                    if n == 0:
                                        if t == 0:
                                            last = dve.tensor_copy(weight_far[:, 4 * b:4 * b + 4, :], got)
                                        continue
                                    last = dve.copy_predicated(weight[:, t, 4 * b:4 * b + 4, :], spread(pairs_bit[:, n - 1, :], 1, 4), got)
                                last.then_inc(placed, 1) if n or t == 0 else None

                        decays(0)
                        step(dve.memset(weight[:], 0.0))
                        dve.wait_ge(masks_ready, 1)
                        for n in range(8):
                            scale(n)
                            if n + 1 < 8:
                                decays(n + 1)
                            if n == 2:
                                dve.wait_ge(masks_ready, 2)
                            if n >= 1:
                                place(n - 1)
                        place(7)
                        place(8)

                    @block.scalar
                    def _(act):
                        for n in range(8):
                            act.wait_ge(diff_ready, n + 1)
                            act.activation(diff[:], diff[:], ACT.Exp).then_inc(exped, 1)

                    @block.tensor
                    def _(pe):
                        for n in range(9):
                            if n < 8:
                                pe.wait_ge(scaled, n + 1)
                            q, k = (q_dec[:, n % 2], k_dec[:, n % 2]) if n < 8 else (qT, kT)
                            for t in range(TT):
                                if n >= 2:
                                    pe.wait_ge(placed, max(1, 2 * (n - 2)) + (t if n > 2 else 0))
                                for h in range(HEADS_C):
                                    s, u = (0, 1) if n == 0 else (t, t)
                                    if n == 0 and t == 1:
                                        break
                                    last = pe.matmul(ps[:, 4 * (n % 2) + 2 * t + h // 4, h % 4 * P:h % 4 * P + P],
                                                     k[:, h, s * P:s * P + P], q[:, h, u * P:u * P + P], start=True, stop=True)
                                if n == 0 and t == 1:
                                    continue
                                last.then_inc(scored, 1 if n else 2)

                with nc.Block() as block:
                    @block.tensor
                    def _(pe):
                        for h in range(HEADS_C):
                            out = [ps[:, 4 + 2 * (h // 4) + t, h % 4 * P:h % 4 * P + P] for t in range(TT)]
                            val = [v[:, s, h * P:h * P + P] for s in range(TT)]
                            pe.matmul(out[0], weight[:, 0, h, :], val[0], start=True, stop=True, skip_group_check=True)
                            pe.matmul(out[1], weight_far[:, h, :], val[0], start=True, stop=False, skip_group_check=True)
                            pe.matmul(out[1], weight[:, 1, h, :], val[1], start=False, stop=True, skip_group_check=True)

            o_parts = token_parts(mem)
            head_norm(v, out_gate, p["norm_w"], o_parts)
            return o_parts

        def route(expert_gate):
            with signals("n_ready", "n_read", "exped", "logits_ready", "dve_step", "gates_ready", "turned", "turned_read", "pick_ready",
                         "pool_step", "repeated", "repeated_read") as (
                    n_ready, n_read, exped, logits_ready, dve_step, gates_ready, turned, turned_read, pick_ready, pool_step,
                    repeated, repeated_read), ExitStack() as own:
                logit = sbuf("logit", [P, TT, EXPERTS], mem=own)
                best = sbuf("best", [P, TT, EXPERTS], mem=own)
                best_no = sbuf("best_no", [P, TT, EXPERTS], U32, mem=own)
                best_e = sbuf("best_e", [P, TT, EXPERTS], mem=own)
                share = sbuf("share", [P, TT, 2], mem=own)
                share_sum = sbuf("share_sum", [P, TT], mem=own)
                number = sbuf("number", [P, EXPERTS], mem=own)
                gate = sbuf("gate", [P, TT, EXPERTS], mem=own)
                second = sbuf("second", [P, TT, EXPERTS], mem=own)
                gate_t = sbuf("gate_t", [EXPERTS, TOKENS], mem=own)
                pick = sbuf("pick", [EXPERTS, EXPERTS, P], mem=own)
                block = own.enter_context(nc.Block())

                @block.sync
                def _(sp):
                    stream.feed(sp, 1)

                @block.tensor
                def _(pe):
                    product_n(pe, hT, 0, n_ready, n_read)
                    pe.wait_ge(gates_ready, 1)
                    for t in range(TT):
                        last = pe.transpose(ps[0:EXPERTS, 0, t * P:t * P + P], gate[:, t, :], ident[:])
                    last.then_inc(turned, 1)
                    pe.wait_ge(turned_read, 1)
                    pe.wait_ge(pick_ready, 1)
                    for n in range(EXPERTS // 2):
                        for b in range(2):
                            last = pe.matmul(ps[:, 4 + n, b * TOKENS:b * TOKENS + TOKENS], pick[:, 2 * n + b, :], gate_t[:],
                                             start=True, stop=True)
                        last.then_inc(repeated, 1)

                @block.vector
                def _(dve):
                    step = Chain(dve, dve_step)
                    dve.wait_ge(n_ready, 1)
                    step(dve.tensor_copy(logit[:], bank_n(0, EXPERTS)))
                    for t in range(TT):
                        last = dve.max(best[:, t, :], logit[:, t, :])
                    step(last)
                    for t in range(TT):
                        last = dve.max_index(best_no[:, t, :], best[:, t, :], logit[:, t, :])
                    dve.tensor_tensor(share[:], best[:, :, 0:2], best[:, :, 0:1].broadcast_to([P, TT, 2]), ALU.subtract).then_inc(logits_ready, 1)
                    dve.wait_ge(logits_ready, 1)
                    step(dve.tensor_copy(best_e[:], best_no[:]))
                    dve.wait_ge(exped, 1)
                    step(dve.tensor_tensor(share_sum[:], share[:, :, 0], share[:, :, 1], ALU.add))
                    step(dve.reciprocal(share_sum[:], share_sum[:]))
                    step(dve.tensor_tensor(share[:], share[:], spread(share_sum[:], 2, 2), ALU.mult))
                    dve.wait_ge(pick_ready, 1)
                    for t in range(TT):
                        for j, out in ((0, gate), (1, second)):
                            last = dve.tensor_scalar(out[:, t, :], number[:], best_e[:, t, j:j + 1], share[:, t, j:j + 1],
                                                     ALU.is_equal, ALU.mult)
                    step(last)
                    dve.tensor_tensor(gate[:], gate[:], second[:], ALU.add).then_inc(gates_ready, 1)

                @block.scalar
                def _(act):
                    act.wait_ge(logits_ready, 1)
                    act.activation(share[:], share[:], ACT.Exp).then_inc(exped, 1)
                    act.wait_ge(turned, 1)
                    act.activation(gate_t[:], ps[0:EXPERTS, 0, 0:TOKENS], ACT.Copy).then_inc(turned_read, 1)
                    for n in range(EXPERTS // 2):
                        act.wait_ge(repeated, n + 1)
                        act.activation(expert_gate[:, 2 * n:2 * n + 2, :], ps[:, 4 + n, :].rearrange("p (b n) -> p b n", b=2), ACT.Copy)

                @block.gpsimd
                def _(pool):
                    step = Chain(pool, pool_step)
                    pool.iota(number[:], pattern=[[1, EXPERTS]], base=0, channel_multiplier=0, allow_small_or_imprecise_dtypes=True)
                    step(pool.memset(pick[:], 0.0))
                    pool.affine_select(out=pick[:], in_=pick[:], compare_op=ALU.not_equal, fill=1.0, base=0,
                                       pattern=[[-1, EXPERTS], [0, P]], channel_multiplier=1).then_inc(pick_ready, 1)

        def third(mem):
            buf, p = params("ada", mem)
            gain = sbuf("gain", [P, 4, DK], mem=mem)
            modulation(buf, p, gain)

            def norm(n, x_parts):
                pre_norm(lambda b: gain[:, n, b:b + 1], x_parts, lambda b: p["shifts"][:, 2 * n * DK + b:2 * n * DK + b + 1])

            def gate(n):
                return p["gates"][:, n * D:n * D + D]

            with ExitStack() as own:
                x_parts = token_parts(own)
                norm(0, x_parts)
                with ExitStack() as mix:
                    mlstm(mix, x_parts)
                    add_gated(gate(0), mixer=x_parts)
                norm(1, x_parts)
                feed_forward("swiglu", FFN_TILES, ACT.Silu, x_parts, gates=2)
                add_gated(gate(1))
            with ExitStack() as own:
                add_gated(gate(2), mixer=hgrn2(own, lambda x_parts: norm(2, x_parts)))
            with ExitStack() as own:
                x_parts = token_parts(own)
                norm(3, x_parts)
                expert_gate = sbuf("expert_gate", [P, EXPERTS, TOKENS], mem=own)
                route(expert_gate)
                feed_forward("moe", EXPERTS * EXPERT_TILES, ACT.Silu, x_parts, gates=2, scale_by=expert_gate)
            add_gated(gate(3))

        def last_norm(mem):
            buf, p = params("last", mem)
            with signals("params_loaded", "squared", "var_ready", "rstd_ready") as (params_loaded, squared, var_ready, rstd_ready), \
                    buffer("junk", [P, TT, D]) as junk, nc.Block() as block:
                @block.sync
                def _(sp):
                    sp.dma_start(buf[:], d["last"]).then_inc(params_loaded, 16)

                @block.scalar
                def _(act):
                    for t in range(TT):
                        last = act.activation(junk[:, t, :], x[:, t, :], ACT.Square, accum_out=squares[:, t:t + 1])
                    last.then_inc(squared, 1)

                @block.gpsimd
                def _(pool):
                    power(pool, var_ready, rstd_ready)

                @block.vector
                def _(dve):
                    dve.wait_ge(squared, 1)
                    dve.tensor_scalar(spare[:], squares[:], 1.0 / D, RMS_EPS, ALU.mult, ALU.add).then_inc(var_ready, 1)
                    dve.wait_ge(rstd_ready, 1)
                    dve.wait_ge(params_loaded, 16)
                    for t in range(TT):
                        dve.scalar_tensor_tensor(x[:, t, :], x[:, t, :], rstd[:, t:t + 1], p["norm_w"], ALU.mult, ALU.mult)

        for section in (mixers, peer, nsa, fox, third, last_norm):
            with ExitStack() as mem:
                section(mem)


        with signals("stored") as (stored,), nc.Block() as block:
            @block.sync
            def _(sp):
                sp.dma_start(d["out"], x[:]).then_inc(stored, 16)
                sp.wait_ge(stored, 16)



def _launch_arrays(a):
    chunks = _chunk_layout(a)
    widths = [c.shape[1] for c in chunks]
    packed = np.zeros((len(chunks), P, CHUNK), np.float32)
    for n, c in enumerate(chunks):
        packed[n, :, :c.shape[1]] = c
    arrays = {"stream": packed}
    offsets = {}
    for section, parts in _param_layout(a).items():
        at, offsets[section] = 0, {}
        for name, v in parts.items():
            offsets[section][name] = (at, v.shape[1])
            at += v.shape[1]
        arrays[section] = np.ascontiguousarray(np.concatenate(list(parts.values()), 1))
    x = a["x"][0]
    arrays["x"] = np.ascontiguousarray(x.reshape(TT, P, D).transpose(1, 0, 2))
    arrays["xT"] = np.ascontiguousarray(x.T.reshape(DK, P, TOKENS).transpose(1, 0, 2))
    return arrays, widths, offsets


def kernel(**inputs):
    import concourse.bacc as bacc
    from concourse.bass_utils import run_bass_kernel_spmd

    arrays, widths, offsets = _launch_arrays({n: np.asarray(v) for n, v in inputs.items()})
    nc = bacc.Bacc("TRN2", target_bir_lowering=False, num_devices=1)
    d = {n: nc.dram_tensor("in_" + n, v.shape, F32, kind="ExternalInput").ap() for n, v in arrays.items()}
    d["out"] = nc.dram_tensor("out", (P, TT, D), F32, kind="ExternalOutput").ap()
    build(nc, d, widths, offsets)
    r = run_bass_kernel_spmd(nc, [{"in_" + n: v for n, v in arrays.items()}], core_ids=[0])
    return r.results[0]["out"].transpose(1, 0, 2).reshape(1, TOKENS, D)
```
